# Optimizing a Trainium2 kernel written in Bass

```python
import jax, jax.numpy as jnp
from jax import lax
import numpy as np
import jax
import jax.numpy as jnp

D_MODEL = 1024
BATCH = 1
SEQ = 256
DEPTH = 1

CHUNK = 64
EPS = 1e-6
D_MIX = D_MODEL
D_A = D_MIX // 2
A_HEADS = 4
A_HEAD_DIM = D_A // A_HEADS
GMLP_BLOCK = 128
D_B = D_MIX - D_A
B_HEADS = 4
B_KEY_DIM = D_B // B_HEADS
B_VAL_DIM = D_B // B_HEADS
D_BK = B_HEADS * B_KEY_DIM
D_BV = B_HEADS * B_VAL_DIM
D_IN = 2 * D_A + 2 * D_BK + 2 * D_BV
N_GROUPS = 4
EXPERTS_PER_GROUP = 8
N_EXPERTS = N_GROUPS * EXPERTS_PER_GROUP
TOP_K_IN_GROUP = 2
D_EXPERT = D_MODEL // 2
MOE_BLOCK = 256


def rms_norm(x, gain):
    xf = x.astype(jnp.float32)
    y = xf * lax.rsqrt(jnp.mean(xf * xf, axis=-1, keepdims=True) + EPS)
    return (y * gain.astype(jnp.float32)).astype(x.dtype)

def gmlp_mixer(u, v, v_gain, w_s, b_s):
    bn, s, _ = u.shape
    nb = s // GMLP_BLOCK
    vh = rms_norm(v.reshape(bn, s, A_HEADS, A_HEAD_DIM), v_gain.reshape(A_HEADS, A_HEAD_DIM))
    vh = vh.reshape(bn, nb, GMLP_BLOCK, A_HEADS, A_HEAD_DIM)
    chunk_id = jnp.arange(GMLP_BLOCK) // CHUNK
    mask = chunk_id[None, :] <= chunk_id[:, None]
    w = jnp.where(mask[None], w_s, jnp.zeros_like(w_s))
    mixed = jnp.einsum('gij,bnjgc->bnigc', w, vh) + jnp.transpose(b_s)[:, :, None]
    return u * mixed.reshape(bn, s, D_A).astype(u.dtype)

def hgrn2_mixer(q_raw, f_raw, i_raw, g_raw, lb, out_gain):
    bn, s, _ = q_raw.shape
    n = s // CHUNK
    f32 = jnp.float32
    q = jax.nn.silu(q_raw.astype(f32))
    f = lb + (1.0 - lb) * jax.nn.sigmoid(f_raw.astype(f32))
    k = 1.0 - f
    lf = jnp.log(f)

    def split(t, d):
        return t.reshape(bn, n, CHUNK, B_HEADS, d).transpose(0, 3, 1, 2, 4)

    q, k, lf = split(q, B_KEY_DIM), split(k, B_KEY_DIM), split(lf, B_KEY_DIM)
    v = split(i_raw.astype(f32), B_VAL_DIM)
    b = lax.cumsum(lf, axis=3)
    ref = b[:, :, :, CHUNK // 2 - 1:CHUNK // 2, :]
    qe = q * jnp.exp(b - ref)
    ke = k * jnp.exp(ref - b)
    causal = jnp.tril(jnp.ones((CHUNK, CHUNK), dtype=bool))
    scores = jnp.einsum('bhncd,bhnsd->bhncs', qe, ke)
    scores = jnp.where(causal, scores, 0.0)
    o_intra = jnp.einsum('bhncs,bhnse->bhnce', scores, v)
    b_last = b[:, :, :, -1:, :]
    u_state = jnp.einsum('bhnsd,bhnse->bhnde', k * jnp.exp(b_last - b), v)
    decay = jnp.exp(b_last[:, :, :, 0, :])

    def step(state, xs):
        dec, upd = xs
        return dec[..., None] * state + upd, state

    s0 = jnp.zeros((bn, B_HEADS, B_KEY_DIM, B_VAL_DIM), f32)
    _, s_prev = lax.scan(step, s0, (jnp.moveaxis(decay, 2, 0), jnp.moveaxis(u_state, 2, 0)))
    s_prev = jnp.moveaxis(s_prev, 0, 2)
    o_inter = jnp.einsum('bhncd,bhnde->bhnce', q * jnp.exp(b), s_prev)
    o = (o_intra + o_inter).transpose(0, 2, 3, 1, 4).reshape(bn, s, B_HEADS, B_VAL_DIM)
    o = rms_norm(o, out_gain.reshape(B_HEADS, B_VAL_DIM))
    o = o * jax.nn.silu(g_raw.reshape(bn, s, B_HEADS, B_VAL_DIM).astype(f32))
    return o.reshape(bn, s, D_BV).astype(q_raw.dtype)

def hier_moe(xn, w_gr, b_gr, w_er, b_er, w_gate, w_up, w_down):
    bn, s, d = xn.shape
    t = bn * s
    xt = xn.reshape(t, d)
    f32 = jnp.float32
    g_logits = (xt @ w_gr).astype(f32) + b_gr.astype(f32)
    g_probs = jax.nn.softmax(g_logits, axis=-1)
    g_idx = jnp.argmax(g_logits, axis=-1)
    g_prob = jnp.take_along_axis(g_probs, g_idx[:, None], axis=1)[:, 0]
    e_logits = ((xt @ w_er).astype(f32) + b_er.astype(f32)).reshape(t, N_GROUPS, EXPERTS_PER_GROUP)
    e_logits = jnp.take_along_axis(e_logits, g_idx[:, None, None], axis=1)[:, 0]
    top_v, top_i = lax.top_k(e_logits, TOP_K_IN_GROUP)
    wts = g_prob[:, None] * jax.nn.softmax(top_v, axis=-1)
    eid = (g_idx[:, None] * EXPERTS_PER_GROUP + top_i).reshape(-1).astype(jnp.int32)
    tok = jnp.repeat(jnp.arange(t, dtype=jnp.int32), TOP_K_IN_GROUP)
    wt = wts.reshape(-1)
    n_assign = t * TOP_K_IN_GROUP

    order = jnp.argsort(eid)
    se, stok, swt = eid[order], tok[order], wt[order]
    counts = jnp.bincount(eid, length=N_EXPERTS).astype(jnp.int32)
    padded = ((counts + MOE_BLOCK - 1) // MOE_BLOCK) * MOE_BLOCK
    pend = jnp.cumsum(padded)
    pstart = pend - padded
    start = jnp.cumsum(counts) - counts
    dest = pstart[se] + (jnp.arange(n_assign, dtype=jnp.int32) - start[se])
    n_blk = -(-n_assign // MOE_BLOCK) + N_EXPERTS
    rows = n_blk * MOE_BLOCK
    buf_tok = jnp.full((rows,), t, jnp.int32).at[dest].set(stok)
    buf_wt = jnp.zeros((rows,), f32).at[dest].set(swt)
    blk_expert = jnp.clip(jnp.searchsorted(pend, jnp.arange(n_blk) * MOE_BLOCK, side='right'),
                          0, N_EXPERTS - 1)
    xpad = jnp.concatenate([xt, jnp.zeros((1, d), xt.dtype)], axis=0)

    def expert_block(args):
        tok_b, e = args
        xb = xpad[tok_b]
        h = jax.nn.silu(xb @ w_gate[e]) * (xb @ w_up[e])
        return h @ w_down[e]

    out = lax.map(expert_block, (buf_tok.reshape(n_blk, MOE_BLOCK), blk_expert))
    out = out.reshape(rows, d) * buf_wt[:, None].astype(out.dtype)
    y = jnp.zeros((t + 1, d), out.dtype).at[buf_tok].add(out)[:t]
    return y.reshape(bn, s, d).astype(xn.dtype)

def first_inputs(seed: int = 0) -> dict:
    key = jax.random.key(seed)
    ks = jax.random.split(key, 20)
    nrm = jax.random.normal
    f32 = jnp.float32
    d = D_MODEL
    return {
        "x": nrm(ks[0], (BATCH, SEQ, d), f32),
        "norm1_gain": 1.0 + 0.05 * nrm(ks[1], (DEPTH, d), f32),
        "w_in": nrm(ks[2], (DEPTH, d, D_IN), f32) * d ** -0.5,
        "gmlp_v_gain": 1.0 + 0.05 * nrm(ks[3], (DEPTH, D_A), f32),
        "gmlp_w_s": nrm(ks[4], (DEPTH, A_HEADS, GMLP_BLOCK, GMLP_BLOCK), f32) * 0.5 * GMLP_BLOCK ** -0.5,
        "gmlp_b_s": 1.0 + 0.1 * nrm(ks[5], (DEPTH, A_HEADS, GMLP_BLOCK), f32),
        "hgrn_lower_bounds": 0.1 * nrm(ks[6], (DEPTH + 1, D_BK), f32),
        "hgrn_out_gain": 1.0 + 0.05 * nrm(ks[7], (DEPTH, D_BV), f32),
        "w_out": nrm(ks[8], (DEPTH, D_MIX, d), f32) * D_MIX ** -0.5,
        "norm2_gain": 1.0 + 0.05 * nrm(ks[9], (DEPTH, d), f32),
        "w_group_router": nrm(ks[10], (DEPTH, d, N_GROUPS), f32) * d ** -0.5,
        "b_group_router": 0.01 * nrm(ks[11], (DEPTH, N_GROUPS), f32),
        "w_expert_router": nrm(ks[12], (DEPTH, d, N_EXPERTS), f32) * d ** -0.5,
        "b_expert_router": 0.01 * nrm(ks[13], (DEPTH, N_EXPERTS), f32),
        "w_gate": nrm(ks[14], (DEPTH, N_EXPERTS, d, D_EXPERT), f32) * d ** -0.5,
        "w_up": nrm(ks[15], (DEPTH, N_EXPERTS, d, D_EXPERT), f32) * d ** -0.5,
        "w_down": nrm(ks[16], (DEPTH, N_EXPERTS, D_EXPERT, d), f32) * D_EXPERT ** -0.5,
        "final_gain": 1.0 + 0.05 * nrm(ks[17], (d,), f32),
    }

def first_block(x, norm1_gain, w_in, gmlp_v_gain, gmlp_w_s, gmlp_b_s, hgrn_lower_bounds,
              hgrn_out_gain, w_out, norm2_gain, w_group_router, b_group_router,
              w_expert_router, b_expert_router, w_gate, w_up, w_down, final_gain):
    lb_all = jnp.cumsum(jax.nn.softmax(hgrn_lower_bounds.astype(jnp.float32), axis=0), axis=0)
    split_at = [D_A, 2 * D_A, 2 * D_A + D_BK, 2 * D_A + 2 * D_BK, 2 * D_A + 2 * D_BK + D_BV]
    h = x
    for l in range(DEPTH):
        n1 = rms_norm(h, norm1_gain[l])
        proj = n1 @ w_in[l]
        u, v, q, f, i, g = jnp.split(proj, split_at, axis=-1)
        a_out = gmlp_mixer(jax.nn.gelu(u, approximate=False), jax.nn.gelu(v, approximate=False),
                           gmlp_v_gain[l], gmlp_w_s[l], gmlp_b_s[l])
        b_out = hgrn2_mixer(q, f, i, g, lb_all[l], hgrn_out_gain[l])
        h = h + jnp.concatenate([a_out, b_out], axis=-1) @ w_out[l]
        n2 = rms_norm(h, norm2_gain[l])
        h = h + hier_moe(n2, w_group_router[l], b_group_router[l], w_expert_router[l],
                         b_expert_router[l], w_gate[l], w_up[l], w_down[l])
    return rms_norm(h, final_gain)


GRID_W = 64
HEAD_DIM = 64
NA_HEADS = 8
NA_WIN_H = 8
NA_WIN_W = 16
GQA_HEADS = 8
GQA_KV_HEADS = 2
Q_BLOCK = 128
ROPE_THETA = 10000.0
PEER_HEADS = 8
PEER_NKEYS = 128
PEER_EXPERTS = PEER_NKEYS * PEER_NKEYS
PEER_QDIM = 256
PEER_HALF = PEER_QDIM // 2
PEER_TOPK = 16
PEER_CHUNK = 128

NA_WIDTH = NA_HEADS * HEAD_DIM
GQA_Q_WIDTH = GQA_HEADS * HEAD_DIM
GQA_KV_WIDTH = GQA_KV_HEADS * HEAD_DIM
IN_SPLITS = (NA_WIDTH, NA_WIDTH, NA_WIDTH, GQA_Q_WIDTH, GQA_KV_WIDTH, GQA_KV_WIDTH, D_MODEL, D_MODEL)
IN_WIDTH = sum(IN_SPLITS)
IN_SPLIT_POINTS = tuple(int(p) for p in np.cumsum(IN_SPLITS)[:-1])


def rmsnorm(x, g):
    xf = x.astype(jnp.float32)
    y = xf * lax.rsqrt(jnp.mean(xf * xf, axis=-1, keepdims=True) + EPS)
    return (y * g.astype(jnp.float32)).astype(x.dtype)

def neighbourhood_attention(q, k, v, rpb):
    b, s, h, dh = q.shape
    rows = s // GRID_W
    kh = min(NA_WIN_H, rows)
    q = q.reshape(b, rows, GRID_W, h, dh)
    k = k.reshape(b, rows, GRID_W, h, dh)
    v = v.reshape(b, rows, GRID_W, h, dh)
    r = jnp.arange(rows)
    row_start = jnp.clip(r - kh // 2, 0, rows - kh)
    key_rows = row_start[:, None] + jnp.arange(kh)[None, :]
    k_g = k[:, key_rows]
    v_g = v[:, key_rows]
    c = jnp.arange(GRID_W)
    col_start = jnp.clip(c - NA_WIN_W // 2, 0, GRID_W - NA_WIN_W)
    in_win = (c[None, :] >= col_start[:, None]) & (c[None, :] < col_start[:, None] + NA_WIN_W)
    dr = key_rows - r[:, None] + (NA_WIN_H - 1)
    dc = jnp.clip(c[None, :] - c[:, None], -(NA_WIN_W - 1), NA_WIN_W - 1) + (NA_WIN_W - 1)
    bias = rpb[:, dr[:, None, :, None], dc[None, :, None, :]].astype(jnp.float32)
    scores = jnp.einsum("brqhd,brkwhd->bhrqkw", q, k_g).astype(jnp.float32) * (dh ** -0.5) + bias[None]
    scores = jnp.where(in_win[:, None, :], scores, -jnp.inf)
    probs = jax.nn.softmax(scores.reshape(b, h, rows, GRID_W, kh * GRID_W), axis=-1)
    probs = probs.reshape(b, h, rows, GRID_W, kh, GRID_W).astype(v.dtype)
    out = jnp.einsum("bhrqkw,brkwhd->brqhd", probs, v_g)
    return out.reshape(b, s, h * dh)

def _rotate(x, ang):
    half = x.shape[-1] // 2
    x1, x2 = x[..., :half], x[..., half:]
    cos = jnp.cos(ang)[None, :, None, :]
    sin = jnp.sin(ang)[None, :, None, :]
    return jnp.concatenate([x1 * cos - x2 * sin, x2 * cos + x1 * sin], axis=-1)

def axial_rope(x):
    b, s, h, dh = x.shape
    sec = dh // 2
    nf = sec // 2
    t = jnp.arange(s)
    inv = ROPE_THETA ** (-jnp.arange(nf, dtype=jnp.float32) / nf)
    ang_r = (t // GRID_W).astype(jnp.float32)[:, None] * inv[None, :]
    ang_c = (t % GRID_W).astype(jnp.float32)[:, None] * inv[None, :]
    xf = x.astype(jnp.float32)
    out = jnp.concatenate([_rotate(xf[..., :sec], ang_r), _rotate(xf[..., sec:], ang_c)], axis=-1)
    return out.astype(x.dtype)

def gqa_attention(q, k, v):
    b, s, h, dh = q.shape
    hkv = k.shape[2]
    grp = h // hkv
    nblk = s // Q_BLOCK
    qb = q.reshape(b, nblk, Q_BLOCK, hkv, grp, dh).transpose(1, 0, 2, 3, 4, 5)
    scale = dh ** -0.5

    def block(qblk):
        sc = jnp.einsum("bqngd,bknd->bngqk", qblk, k).astype(jnp.float32) * scale
        p = jax.nn.softmax(sc, axis=-1).astype(v.dtype)
        return jnp.einsum("bngqk,bknd->bqngd", p, v)

    out = lax.map(block, qb)
    return out.transpose(1, 0, 2, 3, 4, 5).reshape(b, s, h * dh)

def peer(xn, w_q, sub_keys, u, v):
    b, s, d = xn.shape
    t = b * s
    xt = xn.reshape(t, d)
    q = (xt @ w_q).reshape(t, PEER_HEADS, 2, PEER_HALF)
    sc = jnp.einsum("thpc,hpnc->thpn", q, sub_keys).astype(jnp.float32)
    top_s, top_i = lax.top_k(sc, PEER_TOPK)
    cand_s = (top_s[:, :, 0, :, None] + top_s[:, :, 1, None, :]).reshape(t, PEER_HEADS, PEER_TOPK * PEER_TOPK)
    cand_i = (top_i[:, :, 0, :, None] * PEER_NKEYS + top_i[:, :, 1, None, :]).reshape(t, PEER_HEADS, PEER_TOPK * PEER_TOPK)
    best_s, best_pos = lax.top_k(cand_s, PEER_TOPK)
    idx = jnp.take_along_axis(cand_i, best_pos, axis=-1)
    gate = jax.nn.softmax(best_s, axis=-1)
    nchunk = t // PEER_CHUNK
    x_c = xt.reshape(nchunk, PEER_CHUNK, d)
    i_c = idx.reshape(nchunk, PEER_CHUNK, PEER_HEADS * PEER_TOPK)
    g_c = gate.reshape(nchunk, PEER_CHUNK, PEER_HEADS * PEER_TOPK)

    def chunk(args):
        xc, ic, gc = args
        uc = u[ic]
        act = jnp.einsum("cd,ced->ce", xc, uc).astype(jnp.float32)
        hid = (jax.nn.gelu(act, approximate=False) * gc).astype(xc.dtype)
        return jnp.einsum("ce,ced->cd", hid, v[ic])

    out = lax.map(chunk, (x_c, i_c, g_c))
    return out.reshape(b, s, d)

def second_inputs(seed: int = 0) -> dict:
    key = jax.random.key(seed)
    ks = jax.random.split(key, 16)
    f32 = jnp.float32
    nrm = lambda k, shape, scale: jax.random.normal(k, shape, f32) * scale
    return {
        "x": nrm(ks[0], (BATCH, SEQ, D_MODEL), 1.0),
        "norm1_g": 1.0 + nrm(ks[1], (DEPTH, D_MODEL), 0.1),
        "w_in": nrm(ks[2], (DEPTH, D_MODEL, IN_WIDTH), D_MODEL ** -0.5),
        "na_rpb": nrm(ks[3], (DEPTH, NA_HEADS, 2 * NA_WIN_H - 1, 2 * NA_WIN_W - 1), 0.5),
        "gqa_q_norm_g": 1.0 + nrm(ks[4], (DEPTH, HEAD_DIM), 0.1),
        "gqa_k_norm_g": 1.0 + nrm(ks[5], (DEPTH, HEAD_DIM), 0.1),
        "w_proj_a": nrm(ks[6], (DEPTH, NA_WIDTH, D_MODEL), NA_WIDTH ** -0.5),
        "w_proj_b": nrm(ks[7], (DEPTH, GQA_Q_WIDTH, D_MODEL), GQA_Q_WIDTH ** -0.5),
        "w_out": nrm(ks[8], (DEPTH, D_MODEL, D_MODEL), D_MODEL ** -0.5),
        "norm2_g": 1.0 + nrm(ks[9], (DEPTH, D_MODEL), 0.1),
        "peer_w_q": nrm(ks[10], (DEPTH, D_MODEL, PEER_HEADS * PEER_QDIM), D_MODEL ** -0.5),
        "peer_sub_keys": nrm(ks[11], (DEPTH, PEER_HEADS, 2, PEER_NKEYS, PEER_HALF), PEER_HALF ** -0.5),
        "peer_u": nrm(ks[12], (DEPTH, PEER_EXPERTS, D_MODEL), D_MODEL ** -0.5),
        "peer_v": nrm(ks[13], (DEPTH, PEER_EXPERTS, D_MODEL), PEER_HEADS ** -0.5),
        "norm_f_g": 1.0 + nrm(ks[14], (D_MODEL,), 0.1),
    }

def second_block(x, norm1_g, w_in, na_rpb, gqa_q_norm_g, gqa_k_norm_g, w_proj_a, w_proj_b, w_out,
              norm2_g, peer_w_q, peer_sub_keys, peer_u, peer_v, norm_f_g):
    b, s, _ = x.shape
    for l in range(DEPTH):
        h = rmsnorm(x, norm1_g[l])
        proj = h @ w_in[l]
        qa, ka, va, qb, kb, vb, ga, gb = jnp.split(proj, IN_SPLIT_POINTS, axis=-1)
        ya = neighbourhood_attention(
            qa.reshape(b, s, NA_HEADS, HEAD_DIM),
            ka.reshape(b, s, NA_HEADS, HEAD_DIM),
            va.reshape(b, s, NA_HEADS, HEAD_DIM),
            na_rpb[l])
        qh = axial_rope(rmsnorm(qb.reshape(b, s, GQA_HEADS, HEAD_DIM), gqa_q_norm_g[l]))
        kh = axial_rope(rmsnorm(kb.reshape(b, s, GQA_KV_HEADS, HEAD_DIM), gqa_k_norm_g[l]))
        yb = gqa_attention(qh, kh, vb.reshape(b, s, GQA_KV_HEADS, HEAD_DIM))
        merged = jax.nn.sigmoid(ga) * (ya @ w_proj_a[l]) + jax.nn.sigmoid(gb) * (yb @ w_proj_b[l])
        x = x + merged @ w_out[l]
        x = x + peer(rmsnorm(x, norm2_g[l]), peer_w_q[l], peer_sub_keys[l], peer_u[l], peer_v[l])
    return rmsnorm(x, norm_f_g)


def setup_inputs(seed=0):
    out = dict(first_inputs(seed))
    for name, value in second_inputs(seed + 1).items():
        if name != "x":
            out[name + "_2"] = value
    return out


def reference(
    x, norm1_gain, w_in, gmlp_v_gain, gmlp_w_s, gmlp_b_s, hgrn_lower_bounds, hgrn_out_gain,
    w_out, norm2_gain, w_group_router, b_group_router, w_expert_router, b_expert_router, w_gate,
    w_up, w_down, final_gain, norm1_g_2, w_in_2, na_rpb_2, gqa_q_norm_g_2, gqa_k_norm_g_2,
    w_proj_a_2, w_proj_b_2, w_out_2, norm2_g_2, peer_w_q_2, peer_sub_keys_2, peer_u_2, peer_v_2,
    norm_f_g_2,
):
    x = first_block(
        x, norm1_gain, w_in, gmlp_v_gain, gmlp_w_s, gmlp_b_s, hgrn_lower_bounds, hgrn_out_gain,
        w_out, norm2_gain, w_group_router, b_group_router, w_expert_router, b_expert_router,
        w_gate, w_up, w_down, final_gain,
    )
    return second_block(
        x, norm1_g_2, w_in_2, na_rpb_2, gqa_q_norm_g_2, gqa_k_norm_g_2, w_proj_a_2, w_proj_b_2,
        w_out_2, norm2_g_2, peer_w_q_2, peer_sub_keys_2, peer_u_2, peer_v_2, norm_f_g_2,
    )


_drawn_inputs = setup_inputs


def setup_inputs(seed=0):
    import zlib

    import numpy as np

    out = dict(_drawn_inputs(seed))
    spreads = {}
    factors = {'hgrn_lower_bounds': 3.159,
     'b_group_router': 8.0,
     'b_expert_router': 2.845,
     'gqa_q_norm_g_2': 3.775,
     'gqa_k_norm_g_2': 3.196}
    for name, (base, spread) in spreads.items():
        noise = np.random.default_rng([zlib.crc32(name.encode()), seed]).standard_normal(out[name].shape)
        drawn = base * np.exp(spread * noise) if base else spread * noise
        out[name] = jnp.asarray(drawn.astype(out[name].dtype))
    for name, factor in factors.items():
        out[name] = (out[name] * factor).astype(out[name].dtype)
    return out
```

```python
from contextlib import ExitStack

import numpy as np

import concourse.bass as bass
from concourse import mybir

F32 = mybir.dt.float32
U32 = mybir.dt.uint32
I32 = mybir.dt.int32
ALU = mybir.AluOpType
ACT = mybir.ActivationFunctionType
AX_X = mybir.AxisListType.X

P = 128
T = 256
NT = T // P
D = 1024
KD = D // P
EPS = 1e-6
BIG = -3.0e38

HEADS = 4
CHUNK = 64
N_CHUNKS = T // CHUNK
N_GROUPS = 4
N_EXPERTS = 32
PER_GROUP = N_EXPERTS // N_GROUPS
D_EXPERT = 512
SLOTS = 2 * T
BLOCK = 64
BLOCKS_MAX = T // BLOCK
SLOTS_PAD = SLOTS + T

NA_HEADS = 8
DH = 64
GRID_W = 64
KROWS = T // GRID_W
WIN_W = 16
RPB_H, RPB_W = 15, 31
RPB_ROWS = 2 * KROWS - 1
GQA_HEADS = 8
KV_HEADS = 2
N_QK = GQA_HEADS + KV_HEADS
SCALE = DH ** -0.5
PEER_HEADS = 8
NKEYS = 128
TOPK = 16
HP = 2 * PEER_HEADS

RING = 6
CHUNK_COLS = 4096
IN1_ORDER = (3, 2, 5, 4, 1, 0)
CH_OUT1 = 6
CH_MOE = CH_OUT1 + 2
CH_IN2 = CH_MOE + 3 * N_EXPERTS
IN2_COLS = [(1536, 512), (2048, 256), (0, 512), (512, 512), (1024, 512),
            (2304, 512), (2816, 512), (3328, 512), (3840, 512)]
CH_PROJ = CH_IN2 + len(IN2_COLS)
CH_OUT2 = CH_PROJ + 2
CH_WQ = CH_OUT2 + 2
CH_END = CH_WQ + 4

CJ = 4
PEER_CHUNKS = NKEYS // CJ
HK = PEER_HEADS * TOPK
GT = 4
GROUPS = T // GT

PAIR = [(0, 0), (0, 1), (1, 0), (1, 1), (0, 2), (1, 2)]
PAIRS = N_EXPERTS // 2

CONST_PARTS = [("ident", P), ("causal", P), ("scanmask", T), ("iota", SLOTS), ("before", P), ("ones", P),
               ("window", GRID_W), ("cos", NT * DH), ("sin", NT * DH), ("group", N_EXPERTS)]
PARAM_PARTS = [("gain1", KD), ("vgain", HEADS), ("lb0", HEADS), ("lb1", HEADS), ("ogain", HEADS),
               ("gain2", KD), ("gain12", KD), ("gain22", KD)]
ROW_PARTS = [("b_s", HEADS * P), ("b_router", N_GROUPS + N_EXPERTS), ("qgain", DH), ("kgain", DH)]


def columns(parts):
    at, out = 0, {}
    for name, n in parts:
        out[name] = (at, at + n)
        at += n
    return out, at


CONST_AT, CONST_N = columns(CONST_PARTS)
PARAM_AT, PARAM_N = columns(PARAM_PARTS)
ROW_AT, ROW_N = columns(ROW_PARTS)


def constants():
    c = np.zeros((P, CONST_N), np.float32)

    def put(name, value):
        a, b = CONST_AT[name]
        c[:, a:b] = value

    p = np.arange(P)
    put("ident", np.eye(P))
    put("causal", (p[:, None] <= p[None, :]) & (p[:, None] // CHUNK == p[None, :] // CHUNK))
    put("scanmask", np.broadcast_to(np.arange(T) % CHUNK != 0, (P, T)))
    put("iota", np.broadcast_to(np.arange(SLOTS), (P, SLOTS)))
    put("before", p[:, None] < p[None, :])
    put("ones", 1.0)
    col = p % GRID_W
    start = np.clip(col - WIN_W // 2, 0, GRID_W - WIN_W)
    key = np.arange(GRID_W)
    inside = (key[None, :] >= start[:, None]) & (key[None, :] < start[:, None] + WIN_W)
    put("window", np.where(inside, 0.0, BIG))
    sec, nf = DH // 2, DH // 4
    t = np.arange(T)
    inv = np.float32(10000.0) ** (-np.arange(nf, dtype=np.float32) / np.float32(nf))
    ang_r = (t // GRID_W).astype(np.float32)[:, None] * inv[None, :]
    ang_c = (t % GRID_W).astype(np.float32)[:, None] * inv[None, :]
    cos = np.concatenate([np.cos(ang_r), np.cos(ang_r), np.cos(ang_c), np.cos(ang_c)], 1)
    sin = np.concatenate([-np.sin(ang_r), np.sin(ang_r), -np.sin(ang_c), np.sin(ang_c)], 1)
    put("cos", cos.reshape(NT, P, DH).transpose(1, 0, 2).reshape(P, NT * DH))
    put("sin", sin.reshape(NT, P, DH).transpose(1, 0, 2).reshape(P, NT * DH))
    put("group", np.broadcast_to(np.arange(N_EXPERTS) // PER_GROUP, (P, N_EXPERTS)))
    return c


def build(nc, dram, out):
    with ExitStack() as ctx:
        place = [16512]

        def keep(name, shape, dt=F32):
            n = 4
            for s in shape[1:]:
                n *= s
            t = nc.alloc_sbuf_tensor_at(name, shape, dt, offset=place[0])
            place[0] += (n + 31) // 32 * 32
            return t

        ARENA = 229344 - 176 * 1024
        ACTS = ARENA + RING * 16384

        def at(name, shape, offset, dt=F32):
            return nc.alloc_sbuf_tensor_at(name, shape, dt, offset=offset)

        def acts(name, shape, kib, dt=F32):
            return at(name, shape, ACTS + int(kib * 1024), dt)

        h = keep("h", [P, NT, D])
        nT = keep("nT", [P, KD, T])
        const = keep("const", [P, CONST_N])
        param = keep("param", [P, PARAM_N])
        rows = keep("rows", [P, ROW_N])
        w_router = keep("w_router", [P, KD, N_GROUPS + N_EXPERTS])

        def c(name):
            a, b = CONST_AT[name]
            return const[:, a:b]

        def pr(name, i):
            a = PARAM_AT[name][0]
            return param[:, a + i:a + i + 1]

        def prs(name):
            a, b = PARAM_AT[name]
            return param[:, a:b]

        def row(name):
            a, b = ROW_AT[name]
            return rows[:, a:b]

        ident = c("ident")
        stat_ss = keep("stat_ss", [P, NT])
        stat_ms = keep("stat_ms", [P, NT])
        stat_sd = keep("stat_sd", [P, NT])
        stat_rs = keep("stat_rs", [P, NT])

        ring = [at(f"ring{s}", [P, CHUNK_COLS], ARENA + 16384 * s) for s in range(RING)]

        def ring8(s):
            return ring[s][:, :].rearrange("p (k f) -> p k f", k=8)

        def ring4(s):
            return ring[s][:, :].rearrange("p (k f) -> p k f", k=4)

        xhat = acts("xhat", [P, NT, D], 0)
        mixT = acts("mixT", [P, 8, T], 0)
        hF = acts("hF", [P, HEADS, T], 8)
        hK = acts("hK", [P, HEADS, T], 12)
        hB = acts("hB", [P, HEADS, T], 16)
        hD1 = acts("hD1", [P, HEADS, T], 20)
        hD2 = acts("hD2", [P, HEADS, T], 24)
        hEB = acts("hEB", [P, HEADS, T], 28)
        hQ = acts("hQ", [P, HEADS, T], 32)
        hQE = acts("hQE", [P, HEADS, T], 36)
        hQO = acts("hQO", [P, HEADS, T], 40)
        hI = acts("hI", [P, NT, 512], 44)
        hKL = acts("hKL", [P, NT, HEADS, P], 48)
        hSC = acts("hSC", [P, NT, HEADS, P], 52)
        hS = acts("hS", [P, N_CHUNKS - 1, HEADS, P], 56)
        hG = acts("hG", [P, HEADS, T], 62)
        mU = acts("mU", [P, HEADS, T], 66)
        mV = acts("mV", [P, NT, 512], 70)
        mSQ = acts("mSQ", [P, NT, 512], 74)
        hON = acts("hON", [P, NT, 512], 16)
        w_sT = acts("w_sT", [P, HEADS, P], 78)
        lbd = keep("lbd", [P, HEADS])
        lb = keep("lb", [P, HEADS])
        omlb = keep("omlb", [P, HEADS])
        vss = keep("vss", [P, NT * HEADS])
        vrs = keep("vrs", [P, NT * HEADS])
        oss = keep("oss", [P, NT * HEADS])
        ors = keep("ors", [P, NT * HEADS])

        pick_slot = acts("pick_slot", [P, NT, SLOTS], 8)
        pick_wt = acts("pick_wt", [P, NT, SLOTS], 12)
        pick_tmp = acts("pick_tmp", [P, NT, SLOTS], 16)
        xs = acts("xs", [P, KD, SLOTS_PAD], 20)
        xb = [acts(f"xb{j}", [P, KD, BLOCK], 16 + 2 * j) for j in range(2)]
        hid = [acts(f"hid{j}", [BLOCK, D_EXPERT], 44 + 2 * j) for j in range(2)]
        hT = [acts(f"hT{j}", [P, 4, BLOCK], 48 + j) for j in range(2)]
        y_blk = [acts(f"y_blk{j}", [BLOCK, D], 8 + 4 * j) for j in range(2)]
        slot_wt = acts("slot_wt", [P, SLOTS // P, T], 72)
        y_rows = acts("y_rows", [P, SLOTS // P, D], 20)
        gain_row = acts("gain_row", [P, D], 76)
        NE = N_GROUPS + N_EXPERTS
        lg = keep("lg", [P, NT, NE])
        g8 = keep("g8", [P, NT, 8])
        gm8 = keep("gm8", [P, NT, 8])
        gi8 = keep("gi8", [P, NT, 8], U32)
        gneg = keep("gneg", [P, NT])
        gex = keep("gex", [P, NT, N_GROUPS])
        gsum = keep("gsum", [P, NT])
        gid = keep("gid", [P, NT])
        emask = keep("emask", [P, NT, N_EXPERTS], U32)
        em = keep("em", [P, NT, N_EXPERTS])
        ev8 = keep("ev8", [P, NT, 8])
        ei8 = keep("ei8", [P, NT, 8], U32)
        eneg = keep("eneg", [P, NT])
        e21 = keep("e21", [P, NT])
        wt = keep("wt", [P, 2, NT])
        eid = keep("eid", [P, NT, 2])
        chosen = keep("chosen", [P, 2, NT, N_EXPERTS])
        assigned = keep("assigned", [P, NT, N_EXPERTS])
        counts = keep("counts", [P, N_EXPERTS])
        starts = keep("starts", [P, N_EXPERTS])
        slot_of = keep("slot_of", [P, NT, N_EXPERTS])
        slot = keep("slot", [P, 2, NT])
        most = keep("most", [P, 1])
        starts_i = keep("starts_i", [1, N_EXPERTS], I32)
        most_i = keep("most_i", [1, 1], I32)

        y_sorted = nc.dram_tensor("y_sorted", (SLOTS_PAD, D), F32, kind="Internal").ap()

        QK = N_QK * DH
        sga = acts("sga", [P, KD, T], 0)
        qaT = acts("qaT", [P, NA_HEADS // 2, T], 8)
        kaT = acts("kaT", [P, NA_HEADS // 2, T], 12)
        va = acts("va", [P, NT, NA_HEADS * DH], 16)
        qk = acts("qk", [P, NT, QK], 20)
        vb = acts("vb", [P, NT, KV_HEADS * DH], 25)
        qk_sq = acts("qk_sq", [P, NT, QK], 26)
        qk_rot = acts("qk_rot", [P, NT, QK], 31)
        yaT = acts("yaT", [P, NA_HEADS // 2, T], 26)
        ybT = acts("ybT", [P, GQA_HEADS // 2, T], 30)
        qbT = acts("qbT", [P, GQA_HEADS // 2, T], 36)
        kk = acts("kk", [P, NT, KV_HEADS, 2, DH], 40)
        kbT = acts("kbT", [P, KV_HEADS, T], 42)
        sgb = acts("sgb", [P, KD, T], 44)
        rel_bias = acts("rel_bias", [P, NT, NA_HEADS, T], 52)
        prob_a = acts("prob_a", [P, NT, T], 68)
        prob_b = acts("prob_b", [P, NT, T], 70)
        prob_aT = acts("prob_aT", [P, NT, T], 72)
        prob_bT = acts("prob_bT", [P, NT, T], 74)
        rpb_wide = nc.dram_tensor("rpb_wide", (GRID_W, NA_HEADS, RPB_ROWS, GRID_W), F32, kind="Internal").ap()
        cos_gain = acts("cos_gain", [P, 2, NT, DH], 76)
        sin_gain = acts("sin_gain", [P, 2, NT, DH], 77)
        qk_ss = keep("qk_ss", [P, NT * N_QK])
        qk_rs = keep("qk_rs", [P, NT * N_QK])
        top_a = keep("top_a", [P, NT])
        top_b = keep("top_b", [P, NT])
        sum_a = keep("sum_a", [P, NT])
        sum_b = keep("sum_b", [P, NT])

        qT = acts("qT", [P, HP, T], 16)
        keysT = acts("keysT", [P, HP, NKEYS], 52)
        sc = acts("sc", [P, NT, HP, NKEYS], 60)
        cand = acts("cand", [P, NT, PEER_HEADS, TOPK, TOPK], 32)
        ts = acts("ts", [P, NT, HP, TOPK], 48)
        ti = acts("ti", [P, NT, HP, TOPK], 50, U32)
        match = acts("match", [P, HK, TOPK], 16)
        tif = acts("tif", [P, NT, HP, TOPK], 24)
        bpos = acts("bpos", [P, NT, HK], 26, U32)
        bdig = acts("bdig", [P, 2, NT, HK], 27, U32)
        bdigf = acts("bdigf", [P, 2, NT, HK], 29)
        WORK = ARENA + 2 * 16384
        best = at("best", [P, NT, HK], WORK)
        ij = at("ij", [P, 2, NT, HK], WORK + 1024)
        bestT = at("bestT", [P, T], WORK + 3072)
        ijT = at("ijT", [P, 2, T], WORK + 4096)
        hot = [at(f"hot{b}", [P, 2, GT, NKEYS], WORK + 6144 + 4096 * b) for b in range(2)]
        hidT = [at(f"hidT{b}", [P, 2, T], WORK + 6144 + 2048 * b) for b in range(2)]
        gain_f = at("gain_f", [P, D], WORK)
        A = at("A", [P, NKEYS, T], ARENA + 3 * 16384)
        best_sum = keep("best_sum", [P, NT * PEER_HEADS])
        cur_g = keep("cur_g", [P, 2, GT])
        assert place[0] <= ARENA

        bank = [ctx.enter_context(nc.psum_tensor(f"bank{i}", [P, 512], F32)) for i in range(8)]

        def sem(name):
            return ctx.enter_context(nc.semaphore(name))

        x_in = sem("x_in")
        const_in = sem("const_in")
        param_in = sem("param_in")
        rows_in = sem("rows_in")
        wr_in = sem("wr_in")
        ws_in = sem("ws_in")
        ring_full = [sem(f"ring_full{s}") for s in range(RING)]
        h_ready = sem("h_ready")
        stat_sum = sem("stat_sum")
        stat_mean = sem("stat_mean")
        stat_root = sem("stat_root")
        xhat_ready = sem("xhat_ready")
        xhat_turned = sem("xhat_turned")
        nT_act = sem("nT_act")
        nT_dve = sem("nT_dve")
        dve_step = sem("dve_step")
        act_step = sem("act_step")
        lb_diff = sem("lb_diff")
        lb_sig = sem("lb_sig")
        proj_done = sem("proj_done")
        proj_act = sem("proj_act")
        proj_dve = sem("proj_dve")
        f_ready = sem("f_ready")
        lf_ready = sem("lf_ready")
        d_ready = sem("d_ready")
        exp_ready = sem("exp_ready")
        qk_zero = sem("qk_zero")
        qk_ready = sem("qk_ready")
        sc_done = sem("sc_done")
        sc_masked = sem("sc_masked")
        kl_turned = sem("kl_turned")
        kl_ready = sem("kl_ready")
        state_done = sem("state_done")
        state_ready = sem("state_ready")
        o_done = sem("o_done")
        o_sq = sem("o_sq")
        o_ms = sem("o_ms")
        o_sd = sem("o_sd")
        on_ready = sem("on_ready")
        on_turned = sem("on_turned")
        v_ms = sem("v_ms")
        v_sd = sem("v_sd")
        vh_ready = sem("vh_ready")
        ws_masked = sem("ws_masked")
        mixed_done = sem("mixed_done")
        mix_g = sem("mix_g")
        mix_h = sem("mix_h")
        out1_done = sem("out1_done")
        stored = sem("stored")

        gain_in = sem("gain_in")
        xs_zero = sem("xs_zero")
        router_done = sem("router_done")
        gneg_ready = sem("gneg_ready")
        gsum_ready = sem("gsum_ready")
        eneg_ready = sem("eneg_ready")
        e21_ready = sem("e21_ready")
        assign_ready = sem("assign_ready")
        rank_done = sem("rank_done")
        starts_ready = sem("starts_ready")
        pick_ready = sem("pick_ready")
        gather_done = sem("gather_done")
        xs_act = sem("xs_act")
        xs_dve = sem("xs_dve")
        wt_turned = sem("wt_turned")
        slot_wt_ready = sem("slot_wt_ready")
        gate_done = sem("gate_done")
        up_done = sem("up_done")
        down_done = sem("down_done")
        xb_ready = sem("xb_ready")
        many_x = sem("many_x")
        sil_ready = sem("sil_ready")
        hid_ready = sem("hid_ready")
        hid_turned = sem("hid_turned")
        hT_ready = sem("hT_ready")
        y_act = sem("y_act")
        y_dve = sem("y_dve")
        y_stored = sem("y_stored")
        many_gate = sem("many_gate")
        many_up = sem("many_up")
        many_sil = sem("many_sil")
        many_hid = sem("many_hid")
        many_turned = sem("many_turned")
        many_hT = sem("many_hT")
        many_down = sem("many_down")
        many_y_act = sem("many_y_act")
        many_y_dve = sem("many_y_dve")
        many_stored = sem("many_stored")
        y_rows_in = sem("y_rows_in")
        moe_done = sem("moe_done")

        rpb_spread = sem("rpb_spread")
        bias_in = sem("bias_in")
        bias_ready = sem("bias_ready")
        p2_done = sem("p2_done")
        p2_act = sem("p2_act")
        p2_dve = sem("p2_dve")
        qk_ms = sem("qk_ms")
        qk_sd = sem("qk_sd")
        qk_roped = sem("qk_roped")
        qk_turned = sem("qk_turned")
        qbT_ready = sem("qbT_ready")
        kbT_ready = sem("kbT_ready")
        gate2_done = sem("gate2_done")
        gate2_act = sem("gate2_act")
        sg_ready = sem("sg_ready")
        sa_done = sem("sa_done")
        ta_ready = sem("ta_ready")
        ea_ready = sem("ea_ready")
        pa_ready = sem("pa_ready")
        pa_turned = sem("pa_turned")
        paT_ready = sem("paT_ready")
        ya_done = sem("ya_done")
        ya_ready = sem("ya_ready")
        sb_done = sem("sb_done")
        tb_ready = sem("tb_ready")
        eb_ready = sem("eb_ready")
        pb_ready = sem("pb_ready")
        pb_turned = sem("pb_turned")
        pbT_ready = sem("pbT_ready")
        yb_done = sem("yb_done")
        yb_ready = sem("yb_ready")
        branch_done = sem("branch_done")
        merged_ready = sem("merged_ready")
        out2_done = sem("out2_done")

        keys_in = sem("keys_in")
        query_done = sem("query_done")
        query_act = sem("query_act")
        query_dve = sem("query_dve")
        score_done = sem("score_done")
        score_ready = sem("score_ready")
        routed = sem("routed")
        best_exp = sem("best_exp")
        gates_ready = sem("gates_ready")
        route_turned = sem("route_turned")
        route_ready = sem("route_ready")
        u_full = [sem(f"u_full{b}") for b in range(2)]
        v_full = [sem(f"v_full{b}") for b in range(2)]
        act_done = sem("act_done")
        act_ready = sem("act_ready")
        hot_ready = sem("hot_ready")
        cur_ready = sem("cur_ready")
        hot_j_ready = sem("hot_j_ready")
        gates_done = sem("gates_done")
        gated = sem("gated")
        hid_ready2 = sem("hid_ready2")
        hid_used = sem("hid_used")
        gain_f_in = sem("gain_f_in")
        out_ready = sem("out_ready")

        def chain(eng, s):
            n = [0]

            def link(ins):
                n[0] += 1
                ins.then_inc(s, 1)
                eng.wait_ge(s, n[0])

            return link

        def ring_wait(pe, n):
            pe.wait_ge(ring_full[n % RING], 16 * (n // RING + 1))

        def chunk_read(n):
            if n < CH_OUT1:
                return proj_done, 2 * (n + 1)
            if n < CH_MOE:
                return out1_done, 2 * (n - CH_OUT1 + 1)
            if n < CH_IN2:
                pair, i = divmod(n - CH_MOE, RING)
                j, kind = PAIR[i]
                if kind == 2:
                    return down_done, 2 * (2 * pair + j + 1)
                return (gate_done, up_done)[kind], 2 * pair + j + 1
            if n < CH_PROJ:
                i = n - CH_IN2
                return (p2_done, (2, 3, 5, 7, 9)[i]) if i < 5 else (gate2_done, 2 * (i - 4))
            if n < CH_OUT2:
                return branch_done, 7 + n - CH_PROJ
            if n < CH_WQ:
                return out2_done, 2 * (n - CH_OUT2 + 1)
            return query_done, 2 * (n - CH_WQ + 1)

        def quad(t):
            return t[:, :].rearrange("p (m n) -> p m n", m=4)

        def spread(ap, shape):
            return ap.broadcast_to(shape)

        H_COUNT = [0, 4, 8, 10, 14, 18]

        def act_stats(act, n):
            if n == 0:
                act.wait_ge(x_in, 16)
            else:
                act.wait_ge(h_ready, H_COUNT[n])
            for t in range(NT):
                act.activation(xhat[:, t, :], h[:, t, :], ACT.Square,
                               accum_out=stat_ss[:, t:t + 1]).then_inc(stat_sum, 1)
            act.wait_ge(stat_mean, n + 1)
            act.activation(stat_sd[:, :], stat_ms[:, :], ACT.Sqrt).then_inc(stat_root, 1)

        def dve_stats(dve, link, n):
            dve.wait_ge(stat_sum, NT * (n + 1))
            dve.tensor_scalar(stat_ms[:, :], stat_ss[:, :], 1.0 / D, EPS, ALU.mult, ALU.add).then_inc(stat_mean, 1)
            dve.wait_ge(stat_root, n + 1)
            link(dve.reciprocal(stat_rs[:, :], stat_sd[:, :]))

        def dve_xhat(dve):
            for t in range(NT):
                dve.tensor_scalar(xhat[:, t, :], h[:, t, :], stat_rs[:, t:t + 1], None,
                                  ALU.mult).then_inc(xhat_ready, 1)

        def pe_turn(pe, m):
            pe.wait_ge(xhat_ready, NT * (m + 1))
            for b in range(4):
                for k in (2 * b, 2 * b + 1):
                    for t in range(NT):
                        last = pe.transpose(bank[b][:, (k % 2) * T + t * P:(k % 2) * T + (t + 1) * P],
                                            xhat[:, t, k * P:(k + 1) * P], ident)
                last.then_inc(xhat_turned, 1)

        def act_nT(act, m, gain):
            for b in (0, 2):
                act.wait_ge(xhat_turned, 4 * m + b + 1)
                for k in (2 * b, 2 * b + 1):
                    last = act.activation(nT[:, k, :], bank[b][:, (k % 2) * T:(k % 2 + 1) * T], ACT.Copy,
                                          scale=pr(gain, k))
                last.then_inc(nT_act, 1)

        def dve_nT(dve, m, gain):
            for b in (1, 3):
                dve.wait_ge(xhat_turned, 4 * m + b + 1)
                for k in (2 * b, 2 * b + 1):
                    last = dve.tensor_scalar(nT[:, k, :], bank[b][:, (k % 2) * T:(k % 2 + 1) * T], pr(gain, k),
                                             None, ALU.mult)
                last.then_inc(nT_dve, 1)

        def wait_nT(eng, m):
            eng.wait_ge(nT_act, 2 * (m + 1))
            eng.wait_ge(nT_dve, 2 * (m + 1))

        def pe_columns(pe, dst, s, m):
            for k in range(KD):
                last = pe.matmul(dst, ring8(s)[:, k, m * P:(m + 1) * P], nT[:, k, :],
                                 start=(k == 0), stop=(k == KD - 1))
            return last

        def pe_rows(pe, dst, s, t, width=512):
            w = ring[s][:, 0:KD * width].rearrange("p (k f) -> p k f", k=KD)
            for k in range(KD):
                last = pe.matmul(dst, nT[:, k, t * P:(t + 1) * P], w[:, k, :],
                                 start=(k == 0), stop=(k == KD - 1))
            return last

        def pair_fill(pair, i):
            return 16 * (pair + (CH_MOE + i) // RING + 1)

        GATHER_BANK = [0, 1, 2, 3, 6, 7, 0, 1]

        IN1_BANK = [4, 5, 6, 7, 0, 1, 2, 3, 4, 5, 6, 7]
        OUT1_BANK = [5, 6, 7, 0]

        QUERY_BANK = [4, 5, 6, 7, 0, 1, 2, 3]
        U_SPLIT = 16
        R_SPLIT = 12
        BRANCH_BANK = [(0, 1, 2, 3), (5, 6, 7, 4)]

        block = ctx.enter_context(nc.Block())

        @block.sync
        def _(sp):
            def load(n, src, cols=CHUNK_COLS, k=8):
                if n >= RING:
                    sp.wait_ge(*chunk_read(n - RING))
                dst = ring[n % RING][:, 0:cols].rearrange("p (k f) -> p k f", k=k)
                sp.dma_start(dst, src).then_inc(ring_full[n % RING], 16)

            sp.dma_start(h[:, :, :], dram["x"].rearrange("(t p) d -> p t d", p=P)).then_inc(x_in, 16)
            sp.dma_start(const[:, :], dram["const"]).then_inc(const_in, 16)
            sp.dma_start(param[:, :], dram["param"]).then_inc(param_in, 16)
            w_in = dram["w_in"]
            for n in range(2):
                f = IN1_ORDER[n] * 512
                load(n, w_in[:, f:f + 512].rearrange("(k p) f -> p k f", p=P))
            sp.dma_start(rows[:, :], dram["rows"].broadcast_to([P, ROW_N])).then_inc(rows_in, 16)
            sp.dma_start(w_sT[:, :, :], dram["w_sT"].rearrange("j (g i) -> j g i", g=HEADS)).then_inc(ws_in, 16)
            sp.dma_start(w_router[:, :, 0:N_GROUPS],
                         dram["w_group_router"].rearrange("(k p) f -> p k f", p=P)).then_inc(wr_in, 16)
            sp.dma_start(w_router[:, :, N_GROUPS:],
                         dram["w_expert_router"].rearrange("(k p) f -> p k f", p=P)).then_inc(wr_in, 16)
            for n in range(2, 6):
                f = IN1_ORDER[n] * 512
                load(n, w_in[:, f:f + 512].rearrange("(k p) f -> p k f", p=P))
            for n in range(2):
                load(CH_OUT1 + n, dram["w_out"][:, n * 512:n * 512 + 512].rearrange("(k p) f -> p k f", p=P))
            rpb = dram["rpb"]
            for i in range(RPB_ROWS):
                first = (RPB_H // 2 - (KROWS - 1) + i) * RPB_W + RPB_W // 2
                src = bass.AP(rpb.tensor, first, [[RPB_H * RPB_W, NA_HEADS], [-1, GRID_W], [1, GRID_W]])
                sp.dma_start(rpb_wide[:, :, i, :].rearrange("c a d -> a c d"), src).then_inc(rpb_spread, 16)
            sp.wait_ge(h_ready, 4)
            sp.dma_start(gain_row[:, :], dram["final_gain"].broadcast_to([P, D])).then_inc(gain_in, 16)
            sp.wait_ge(rpb_spread, 16 * RPB_ROWS)
            for r in range(KROWS):
                t, lo = r // 2, (r % 2) * GRID_W
                first = KROWS - 1 - r
                sp.dma_start(rel_bias[lo:lo + GRID_W, t, :, :],
                             rpb_wide[:, :, first:first + KROWS, :].rearrange("c a k d -> c a (k d)")).then_inc(bias_in, 16)

            def expert_source(i, pair):
                j, kind = PAIR[i]
                e = 2 * pair + j
                if kind == 2:
                    return dram["w_down"][bass.ds(e, 1)].rearrange("e (k p) f -> p (e k) f", p=P), 4
                w = dram["w_gate"] if kind == 0 else dram["w_up"]
                return w[bass.ds(e, 1)].rearrange("e (k p) f -> p (e k) f", p=P), 8

            for i in range(RING):
                src, k = expert_source(i, 0)
                load(CH_MOE + i, src, k=k)
            with sp.Fori(1, PAIRS) as pair:
                for i, (j, kind) in enumerate(PAIR):
                    s = (CH_MOE + i) % RING
                    if kind == 2:
                        sp.wait_ge(down_done, 4 * pair + 2 * j - 2)
                    else:
                        sp.wait_ge((gate_done, up_done)[kind], 2 * pair + j - 1)
                    src, k = expert_source(i, pair)
                    dst = ring[s][:, :].rearrange("p (k f) -> p k f", k=k)
                    sp.dma_start(dst, src).then_inc(ring_full[s], 16)
            for i, (first, width) in enumerate(IN2_COLS):
                load(CH_IN2 + i, dram["w_in_2"][:, first:first + width].rearrange("(k p) f -> p k f", p=P), KD * width)
            for i, name in enumerate(("w_proj_a", "w_proj_b")):
                load(CH_PROJ + i, dram[name].rearrange("(k p) f -> p k f", p=P), k=4)
            for i in range(2):
                load(CH_OUT2 + i, dram["w_out_2"][:, i * 512:i * 512 + 512].rearrange("(k p) f -> p k f", p=P))
            for i in range(4):
                load(CH_WQ + i, dram["w_q"][:, i * 512:i * 512 + 512].rearrange("(k p) f -> p k f", p=P))
            sp.wait_ge(h_ready, H_COUNT[4])
            sp.dma_start(keysT[:, :, :], dram["keysT"].rearrange("c (a n) -> c a n", n=NKEYS)).then_inc(keys_in, 16)

            def stream(table, chunk, b, full):
                sp.dma_start(ring[b][:, :], table[bass.ds(chunk, 1)].rearrange("e p f -> p (e f)")).then_inc(full[b], 16)

            for b in range(2):
                sp.wait_ge(*(chunk_read(CH_END - 1) if b == 0 else chunk_read(CH_OUT2)))
                stream(dram["u"], b, b, u_full)
            with sp.Fori(1, PEER_CHUNKS // 2) as c2:
                for b in range(2):
                    sp.wait_ge(act_done, 4 * c2 + 2 * b - 2)
                    stream(dram["u"], 2 * c2 + b, b, u_full)
            for b in range(2):
                sp.wait_ge(act_done, 2 * PEER_CHUNKS - 2 + 2 * b)
                stream(dram["v"], b, b, v_full)
            with sp.Fori(1, PEER_CHUNKS // 2) as c2:
                for b in range(2):
                    sp.wait_ge(hid_used, 4 * c2 + 2 * b - 2)
                    stream(dram["v"], 2 * c2 + b, b, v_full)
            sp.wait_ge(gates_done, GROUPS)
            sp.wait_ge(route_ready, 1)
            sp.dma_start(gain_f[:, :], dram["norm_f_g"].broadcast_to([P, D])).then_inc(gain_f_in, 16)
            for t in range(NT):
                sp.wait_ge(out_ready, t + 1)
                sp.dma_start(out[t * P:(t + 1) * P, :], h[:, t, :]).then_inc(stored, 16)
            sp.wait_ge(stored, 16 * NT)

        @block.gpsimd
        def _(pool):
            pool.memset(hQE[:, :, :], 0.0).then_inc(qk_zero, 1)
            pool.memset(hQO[:, :, :], 0.0).then_inc(qk_zero, 1)
            pool.memset(hSC[:, :, :, :], 0.0).then_inc(qk_zero, 1)
            pool.wait_ge(ws_in, 16)
            pool.wait_ge(qk_zero, 3)
            pool.memset(w_sT[CHUNK:P, :, 0:CHUNK], 0.0).then_inc(ws_masked, 1)
            pool.wait_ge(h_ready, 4)
            pool.memset(xs[:, :, SLOTS:], 0.0).then_inc(xs_zero, 1)
            pool.wait_ge(bias_in, 16 * KROWS)
            pool.wait_ge(const_in, 16)
            for t in range(NT):
                view = rel_bias[:, t, :, :].rearrange("p a (k c) -> p (a k) c", k=KROWS)
                pool.tensor_tensor(view, view, spread(c("window").unsqueeze(1), [P, NA_HEADS * KROWS, GRID_W]),
                                   ALU.add).then_inc(bias_ready, 1)
            pool.wait_ge(xs_act, KD // 2)
            pool.wait_ge(xs_dve, KD // 2)
            pool.wait_ge(xs_zero, 1)
            pool.wait_ge(starts_ready, 1)
            load_most = pool.value_load(most_i[0:1, 0:1], min_val=0, max_val=T)
            with pool.If(load_most > BLOCK):
                def many_copies(e, peeled):
                    first = pool.value_load(starts_i[0:1, bass.ds(e, 1)], min_val=0, max_val=SLOTS)
                    for b in range(BLOCKS_MAX):
                        if b or not peeled:
                            pool.wait_ge(many_up, e * BLOCKS_MAX + b)
                        pool.tensor_copy(xb[0][:, :, :], xs[:, :, bass.ds(first + b * BLOCK, BLOCK)]).then_inc(many_x, 1)

                many_copies(0, True)
                with pool.Fori(1, N_EXPERTS) as e:
                    many_copies(e, False)
            with pool.Else():
                def pair_copies(pair, peeled):
                    for j in range(2):
                        first = pool.value_load(starts_i[0:1, bass.ds(2 * pair + j, 1)], min_val=0, max_val=SLOTS)
                        if not peeled:
                            pool.wait_ge(up_done, 2 * pair + j - 1)
                        pool.tensor_copy(xb[j][:, :, :], xs[:, :, bass.ds(first, BLOCK)]).then_inc(xb_ready, 1)

                pair_copies(0, True)
                with pool.Fori(1, PAIRS) as pair:
                    pair_copies(pair, False)
            pool.wait_ge(route_ready, 1)

            def weigh_hot(g, b):
                pool.tensor_copy(cur_g[:, b, :], bestT[:, bass.ds(g * GT, GT)]).then_inc(cur_ready, 1)
                pool.wait_ge(cur_ready, g + 1)
                pool.wait_ge(hot_ready, g + 1)
                pool.tensor_tensor(hot[b][:, 1, :, :], hot[b][:, 1, :, :],
                                   spread(cur_g[:, b, :].unsqueeze(2), [P, GT, NKEYS]), ALU.mult).then_inc(hot_j_ready, 1)

            with pool.Fori(0, GROUPS // 2) as g2:
                for b in range(2):
                    weigh_hot(2 * g2 + b, b)

        @block.scalar
        def _(act):
            link = chain(act, act_step)
            act_stats(act, 0)
            act.wait_ge(lb_diff, 1)
            act.activation(lb[:, :], lbd[:, :], ACT.Sigmoid).then_inc(lb_sig, 1)
            act.wait_ge(param_in, 16)
            act_nT(act, 0, "gain1")
            for use, dst in enumerate((hF, hF, hQ, hQ, hG, hG)):
                act.wait_ge(proj_done, use + 1)
                half = use % 2
                act.activation(dst[:, 2 * half:2 * half + 2, :].rearrange("p a t -> p (a t)"),
                               bank[IN1_BANK[use]][:, :], ACT.Sigmoid).then_inc(proj_act, 1)
            for t in range(NT):
                act.wait_ge(proj_done, 7 + t)
                act.activation(hI[:, t, :], bank[IN1_BANK[6 + t]][:, :], ACT.Copy).then_inc(proj_act, 1)
            act.wait_ge(f_ready, 1)
            act.activation(hF[:, :, :], hF[:, :, :], ACT.Ln).then_inc(lf_ready, 1)
            act.wait_ge(d_ready, 1)
            act.activation(hF[:, :, :], hD1[:, :, :], ACT.Exp).then_inc(exp_ready, 1)
            act.activation(hD1[:, :, :], hD1[:, :, :], ACT.Exp, scale=-1.0).then_inc(exp_ready, 1)
            act.wait_ge(d_ready, 2)
            act.activation(hD2[:, :, :], hD2[:, :, :], ACT.Exp).then_inc(exp_ready, 1)
            act.activation(hEB[:, :, :], hB[:, :, :], ACT.Exp).then_inc(exp_ready, 1)
            for t in range(NT):
                act.wait_ge(proj_done, 9 + t)
                act.activation(mV[:, t, :], bank[IN1_BANK[8 + t]][:, :], ACT.Gelu).then_inc(proj_act, 1)
            for half in range(2):
                act.wait_ge(proj_done, 11 + half)
                act.activation(mU[:, 2 * half:2 * half + 2, :].rearrange("p a t -> p (a t)"),
                               bank[IN1_BANK[10 + half]][:, :], ACT.Gelu).then_inc(proj_act, 1)
            for t in range(NT):
                act.wait_ge(kl_turned, t + 1)
                act.activation(hKL[:, t, :, :], quad(bank[2 + t]), ACT.Copy).then_inc(kl_ready, 1)
            act.wait_ge(v_ms, 1)
            act.activation(vrs[:, :], vss[:, :], ACT.Sqrt).then_inc(v_sd, 1)
            act.wait_ge(vh_ready, 1)
            for t in range(NT):
                act.wait_ge(o_done, t + 1)
                act.activation(mSQ[:, t, :], bank[t][:, :], ACT.Square).then_inc(o_sq, 1)
            act.wait_ge(o_ms, 1)
            act.activation(ors[:, :], oss[:, :], ACT.Sqrt).then_inc(o_sd, 1)
            act_stats(act, 1)
            act_nT(act, 1, "gain2")
            act.wait_ge(gneg_ready, 1)
            for t in range(NT):
                act.activation(gex[:, t, :], lg[:, t, 0:N_GROUPS], ACT.Exp, bias=gneg[:, t:t + 1],
                               accum_out=gsum[:, t:t + 1]).then_inc(gsum_ready, 1)
            act.wait_ge(eneg_ready, 1)
            for t in range(NT):
                act.activation(e21[:, t:t + 1], ev8[:, t, 1:2], ACT.Exp,
                               bias=eneg[:, t:t + 1]).then_inc(e21_ready, 1)
            for k in range(0, KD, 2):
                act.wait_ge(gather_done, k + 1)
                act.activation(xs[:, k, 0:SLOTS], bank[GATHER_BANK[k]][:, :], ACT.Copy,
                               scale=pr("gain2", k)).then_inc(xs_act, 1)
            for half in range(2):
                act.wait_ge(wt_turned, half + 1)
                act.activation(slot_wt[:, 2 * half:2 * half + 2, :].rearrange("p s t -> p (s t)"),
                               bank[4 + half][:, :], ACT.Copy).then_inc(slot_wt_ready, 1)
            act.wait_ge(starts_ready, 1)
            load_most = act.value_load(most_i[0:1, 0:1], min_val=0, max_val=T)
            with act.If(load_most > BLOCK):
                def many_scalar(e, peeled):
                    first = act.value_load(starts_i[0:1, bass.ds(e, 1)], min_val=0, max_val=SLOTS)
                    for b in range(BLOCKS_MAX):
                        n = e * BLOCKS_MAX + b
                        act.wait_ge(many_gate, n + 1)
                        act.activation(hid[0][:, :], bank[0][0:BLOCK, :], ACT.Silu).then_inc(many_sil, 1)
                        act.wait_ge(many_turned, n + 1)
                        act.activation(hT[0][:, :, :].rearrange("p f s -> p (f s)"), bank[4][:, 0:4 * BLOCK],
                                       ACT.Copy).then_inc(many_hT, 1)
                        act.wait_ge(many_down, 2 * n + 1)
                        if b or not peeled:
                            act.wait_ge(many_stored, 16 * n)
                        act.activation(y_blk[0][:, 0:512], bank[6][0:BLOCK, :], ACT.Copy).then_inc(many_y_act, 1)
                        act.wait_ge(many_y_act, n + 1)
                        act.wait_ge(many_y_dve, n + 1)
                        act.dma_start(y_sorted[bass.ds(first + b * BLOCK, BLOCK)], y_blk[0][:, :]).then_inc(many_stored, 16)

                many_scalar(0, True)
                with act.Fori(1, N_EXPERTS) as e:
                    many_scalar(e, False)
                act.wait_ge(many_stored, 16 * N_EXPERTS * BLOCKS_MAX)
                act.nop().then_inc(y_stored, 16 * N_EXPERTS)
            with act.Else():
                def pair_scalar(pair, peeled):
                    first = [act.value_load(starts_i[0:1, bass.ds(2 * pair + j, 1)], min_val=0, max_val=SLOTS)
                             for j in range(2)]

                    def silu(j):
                        act.wait_ge(gate_done, 2 * pair + j + 1)
                        act.activation(hid[j][:, :], bank[j][0:BLOCK, :], ACT.Silu).then_inc(sil_ready, 1)

                    def turn(j):
                        act.wait_ge(hid_turned, 2 * pair + j + 1)
                        act.activation(hT[j][:, :, :].rearrange("p f s -> p (f s)"), bank[4 + j][:, 0:4 * BLOCK],
                                       ACT.Copy).then_inc(hT_ready, 1)

                    def copy(j):
                        act.wait_ge(down_done, 4 * pair + 2 * j + 1)
                        if not peeled:
                            act.wait_ge(y_stored, 32 * pair + 16 * j - 16)
                        act.activation(y_blk[j][:, 0:512], bank[6][0:BLOCK, :], ACT.Copy).then_inc(y_act, 1)

                    def store(j):
                        act.wait_ge(y_act, 2 * pair + j + 1)
                        act.wait_ge(y_dve, 2 * pair + j + 1)
                        if j or not peeled:
                            act.wait_ge(y_stored, 32 * pair + 16 * j)
                        act.dma_start(y_sorted[bass.ds(first[j], BLOCK)], y_blk[j][:, :]).then_inc(y_stored, 16)

                    silu(0)
                    turn(0)
                    silu(1)
                    copy(0)
                    turn(1)
                    store(0)
                    copy(1)
                    store(1)

                pair_scalar(0, True)
                with act.Fori(1, PAIRS) as pair:
                    pair_scalar(pair, False)
            act.wait_ge(y_stored, 16 * N_EXPERTS)
            act.dma_start(y_rows[:, :, :],
                          y_sorted[0:SLOTS].rearrange("(s p) d -> p s d", p=P)).then_inc(y_rows_in, 16)
            act_stats(act, 2)
            act_stats(act, 3)
            act_nT(act, 2, "gain12")
            for t in range(NT):
                act.wait_ge(p2_done, t + 1)
                act.activation(qk_sq[:, t, 0:512], bank[4 + t][:, :], ACT.Square)
                act.activation(qk[:, t, 0:512], bank[4 + t][:, :], ACT.Copy).then_inc(p2_act, 1)
            act.wait_ge(p2_done, 3)
            kv = bank[6][:, :].rearrange("p (t f) -> p t f", t=NT)
            act.activation(qk_sq[:, :, 512:], kv[:, :, 0:KV_HEADS * DH], ACT.Square)
            act.activation(qk[:, :, 512:], kv[:, :, 0:KV_HEADS * DH], ACT.Copy)
            act.activation(vb[:, :, :], kv[:, :, KV_HEADS * DH:], ACT.Copy).then_inc(p2_act, 1)
            act.wait_ge(qk_ms, 1)
            act.activation(qk_rs[:, :], qk_ss[:, :], ACT.Sqrt).then_inc(qk_sd, 1)
            for i in range(2):
                act.wait_ge(p2_done, 6 + i)
                act.activation(kaT[:, 2 * i:2 * i + 2, :].rearrange("p a t -> p (a t)"), bank[1 + i][:, :],
                               ACT.Copy).then_inc(p2_act, 1)
            for i in range(2):
                act.wait_ge(qk_turned, i + 1)
                act.activation(qbT[:, 2 * i:2 * i + 2, :].rearrange("p a t -> p (a t)"), bank[5 + i][:, :],
                               ACT.Copy).then_inc(qbT_ready, 1)
            for i in range(NA_HEADS):
                act.wait_ge(ta_ready, i + 1)
                for t in range(NT):
                    act.activation(prob_a[:, t, :], prob_a[:, t, :], ACT.Exp, bias=top_a[:, t:t + 1],
                                   accum_out=sum_a[:, t:t + 1]).then_inc(ea_ready, 1)
                act.wait_ge(tb_ready, i + 1)
                if i:
                    act.wait_ge(pb_turned, i)
                for t in range(NT):
                    act.activation(prob_b[:, t, :], bank[1][:, t * T:(t + 1) * T], ACT.Exp, bias=top_b[:, t:t + 1],
                                   scale=SCALE, accum_out=sum_b[:, t:t + 1]).then_inc(eb_ready, 1)
                act.wait_ge(gate2_done, i + 1)
                dst, half = (sga, i) if i < 4 else (sgb, i - 4)
                act.activation(dst[:, 2 * half:2 * half + 2, :].rearrange("p a t -> p (a t)"), bank[5 + i % 3][:, :],
                               ACT.Copy).then_inc(gate2_act, 1)
                act.wait_ge(pa_turned, i + 1)
                act.activation(prob_aT[:, :, :].rearrange("p k q -> p (k q)"), bank[2][:, :], ACT.Copy).then_inc(paT_ready, 1)
                part = slice((i % 2) * DH, (i % 2) * DH + DH)
                act.wait_ge(ya_done, i + 1)
                act.activation(yaT[part, i // 2, :], bank[4][0:DH, 0:T], ACT.Copy).then_inc(ya_ready, 1)
                act.wait_ge(yb_done, i + 1)
                act.activation(ybT[part, i // 2, :], bank[4][DH:P, 0:T], ACT.Copy).then_inc(yb_ready, 1)
            act.wait_ge(gate2_act, 8)
            for dst in (sga, sgb):
                act.activation(dst[:, :, :], dst[:, :, :], ACT.Sigmoid).then_inc(sg_ready, 1)
            act_stats(act, 4)
            act_nT(act, 3, "gain22")
            for use in range(0, 8, 2):
                act.wait_ge(query_done, use + 1)
                act.activation(qT[:, 2 * use:2 * use + 2, :].rearrange("p a t -> p (a t)"), bank[QUERY_BANK[use]][:, :],
                               ACT.Copy).then_inc(query_act, 1)
            for use in range(8):
                t, part = divmod(use, 4)
                act.wait_ge(score_done, use + 1)
                act.activation(sc[:, t, 4 * part:4 * part + 4, :].rearrange("p a n -> p (a n)"), bank[QUERY_BANK[use]][:, :],
                               ACT.Copy).then_inc(score_ready, 1)

            def act_columns(chunk):
                for b in range(2):
                    act.wait_ge(act_done, 2 * chunk + b + 1)
                    dst = A[:, bass.ds(chunk * CJ + 2 * b, 2), :].rearrange("p j t -> p (j t)")
                    act.activation(dst, bank[4 + b][:, :], ACT.Gelu).then_inc(act_ready, 1)

            with act.Fori(0, U_SPLIT) as chunk:
                act_columns(chunk)
            act.wait_ge(routed, 1)
            act.activation(best[:, :, :], best[:, :, :], ACT.Exp).then_inc(best_exp, 1)
            with act.Fori(U_SPLIT, PEER_CHUNKS) as chunk:
                act_columns(chunk)

            def hid_columns(chunk, peeled):
                for b in range(2):
                    if not peeled:
                        act.wait_ge(hid_used, 2 * chunk + b - 1)
                    act.activation(hidT[b][:, :, :].rearrange("p j t -> p (j t)"),
                                   A[:, bass.ds(chunk * CJ + 2 * b, 2), :].rearrange("p j t -> p (j t)"),
                                   ACT.Copy).then_inc(hid_ready2, 1)

            act.wait_ge(gated, GROUPS)
            act.wait_ge(gates_done, GROUPS)
            hid_columns(0, True)
            with act.Fori(1, PEER_CHUNKS) as chunk:
                hid_columns(chunk, False)
            act_stats(act, 5)

        @block.tensor
        def _(pe):
            pe.wait_ge(const_in, 16)
            pe_turn(pe, 0)
            wait_nT(pe, 0)
            for n, part in enumerate(IN1_ORDER):
                ring_wait(pe, n)
                for use in (2 * n, 2 * n + 1):
                    dst = bank[IN1_BANK[use]]
                    if use == 8:
                        pe.wait_ge(proj_act, 2)
                    if use == 10:
                        pe.wait_ge(proj_dve, 2)
                    if part in (4, 1):
                        last = pe_rows(pe, dst[:, :], n, use % 2)
                    else:
                        for m in range(2):
                            last = pe_columns(pe, dst[:, m * T:(m + 1) * T], n, 2 * (use % 2) + m)
                    last.then_inc(proj_done, 1)
            pe.wait_ge(proj_dve, 4)
            pe.wait_ge(qk_ready, 2)
            for t in range(NT):
                for hd in range(HEADS):
                    last = pe.matmul(bank[t][:, hd * P:(hd + 1) * P], hD1[:, hd, t * P:(t + 1) * P],
                                     hF[:, hd, t * P:(t + 1) * P], start=True, stop=True)
                last.then_inc(sc_done, 1)
            pe.wait_ge(qk_ready, 3)
            pe.wait_ge(proj_act, 8)
            for t in range(NT):
                for hd in range(HEADS):
                    last = pe.transpose(bank[2 + t][:, hd * P:(hd + 1) * P], hD2[:, hd, t * P:(t + 1) * P], ident)
                last.then_inc(kl_turned, 1)
            pe.wait_ge(proj_act, 12)
            for n in range(N_CHUNKS - 1):
                t, lo = n // 2, (n % 2) * CHUNK
                pe.wait_ge(kl_ready, t + 1)
                for hd in range(HEADS):
                    last = pe.matmul(bank[4 + n][:, hd * P:(hd + 1) * P], hKL[lo:lo + CHUNK, t, hd, :],
                                     hI[lo:lo + CHUNK, t, hd * P:(hd + 1) * P], start=True, stop=True)
                last.then_inc(state_done, 1)
            pe.wait_ge(ws_masked, 1)
            pe.wait_ge(vh_ready, 1)
            for pair in range(2):
                if pair:
                    pe.wait_ge(state_ready, 1)
                dst = bank[7 if pair == 0 else 4]
                for g in (2 * pair, 2 * pair + 1):
                    for t in range(NT):
                        o = (g % 2) * T + t * P
                        last = pe.matmul(dst[:, o:o + P], mV[:, t, g * P:(g + 1) * P], w_sT[:, g, :],
                                         start=True, stop=True)
                last.then_inc(mixed_done, 1)
            for t in range(NT):
                pe.wait_ge(sc_masked, t + 1)
                pe.wait_ge(qk_ready, 5)
                pe.wait_ge(state_ready, 1 if t == 0 else 3)
                for hd in range(HEADS):
                    dst = bank[t][:, hd * P:(hd + 1) * P]
                    tok = slice(t * P, (t + 1) * P)
                    pe.matmul(dst, hSC[:, t, hd, :], hI[:, t, hd * P:(hd + 1) * P], start=True, stop=False)
                    if t:
                        pe.matmul(dst, hQE[:, hd, tok], hS[:, 2 * t - 1, hd, :], start=False, stop=False)
                    last = pe.matmul(dst, hQO[:, hd, tok], hS[:, 2 * t, hd, :], start=False, stop=True)
                last.then_inc(o_done, 1)
            pe.wait_ge(on_ready, 1)
            for hd in range(HEADS):
                for t in range(NT):
                    o = (hd % 2) * T + t * P
                    last = pe.transpose(bank[2 + hd // 2][:, o:o + P], hON[:, t, hd * P:(hd + 1) * P], ident)
                if hd % 2:
                    last.then_inc(on_turned, 1)
            pe.wait_ge(mix_g, HEADS)
            pe.wait_ge(mix_h, HEADS)
            for half in range(2):
                n = CH_OUT1 + half
                ring_wait(pe, n)
                for t in range(NT):
                    for k in range(8):
                        last = pe.matmul(bank[OUT1_BANK[2 * half + t]][:, :], mixT[:, k, t * P:(t + 1) * P],
                                         ring8(n % RING)[:, k, :], start=(k == 0), stop=(k == 7))
                    last.then_inc(out1_done, 1)
            pe_turn(pe, 1)
            wait_nT(pe, 1)
            pe.wait_ge(wr_in, 32)
            for t in range(NT):
                for k in range(KD):
                    last = pe.matmul(bank[4][:, t * 64:t * 64 + NE], nT[:, k, t * P:(t + 1) * P], w_router[:, k, :],
                                     start=(k == 0), stop=(k == KD - 1))
            last.then_inc(router_done, 1)
            pe.wait_ge(assign_ready, 1)
            pe.matmul(bank[5][:, 0:32], c("before"), assigned[:, 0, :], start=True, stop=True)
            pe.matmul(bank[5][:, 32:64], c("before"), assigned[:, 1, :], start=True, stop=False)
            pe.matmul(bank[5][:, 32:64], c("ones"), assigned[:, 0, :], start=False, stop=True)
            pe.matmul(bank[5][:, 64:96], c("ones"), assigned[:, 0, :], start=True, stop=False)
            pe.matmul(bank[5][:, 64:96], c("ones"), assigned[:, 1, :], start=False, stop=True).then_inc(rank_done, 1)
            pe.wait_ge(pick_ready, NT)
            for k in range(KD):
                if k == 6:
                    pe.wait_ge(xs_act, 1)
                if k == 7:
                    pe.wait_ge(xs_dve, 1)
                for t in range(NT):
                    last = pe.matmul(bank[GATHER_BANK[k]][:, :], xhat[:, t, k * P:(k + 1) * P], pick_slot[:, t, :],
                                     start=(t == 0), stop=(t == NT - 1))
                last.then_inc(gather_done, 1)
            pe.wait_ge(pick_ready, 2 * NT)
            for s in range(SLOTS // P):
                for t in range(NT):
                    o = (s % 2) * T + t * P
                    last = pe.transpose(bank[4 + s // 2][:, o:o + P], pick_wt[:, t, s * P:(s + 1) * P], ident)
                if s % 2:
                    last.then_inc(wt_turned, 1)
            pe.wait_ge(starts_ready, 1)

            def expert_in(dst, w, block_in):
                for k in range(KD):
                    last = pe.matmul(dst[0:BLOCK, :], block_in[:, k, :], ring8(w)[:, k, :],
                                     start=(k == 0), stop=(k == KD - 1))
                return last

            def expert_turn(dst, hidden):
                for f in range(4):
                    last = pe.matmul(dst[:, f * BLOCK:(f + 1) * BLOCK], hidden[:, f * P:(f + 1) * P],
                                     ident[0:BLOCK, 0:BLOCK], start=True, stop=True)
                return last

            def expert_out(half, w, hidden_t):
                for f in range(4):
                    last = pe.matmul(bank[6 + half][0:BLOCK, :], hidden_t[:, f, :],
                                     ring4(w)[:, f, half * 512:(half + 1) * 512], start=(f == 0), stop=(f == 3))
                return last

            W_SLOT = [(CH_MOE + i) % RING for i in range(RING)]
            load_most = pe.value_load(most_i[0:1, 0:1], min_val=0, max_val=T)
            with pe.If(load_most > BLOCK):
                def many_products(pair, peeled):
                    for i in range(RING):
                        pe.wait_ge(ring_full[W_SLOT[i]], pair_fill(pair, i))
                    for j in range(2):
                        w_g, w_u, w_d = [W_SLOT[PAIR.index((j, kind))] for kind in range(3)]
                        for b in range(BLOCKS_MAX):
                            n = (2 * pair + j) * BLOCKS_MAX + b
                            pe.wait_ge(many_x, n + 1)
                            expert_in(bank[0], w_g, xb[0]).then_inc(many_gate, 1)
                            expert_in(bank[2], w_u, xb[0]).then_inc(many_up, 1)
                            pe.wait_ge(many_hid, n + 1)
                            expert_turn(bank[4], hid[0]).then_inc(many_turned, 1)
                            pe.wait_ge(many_hT, n + 1)
                            if b or j or not peeled:
                                pe.wait_ge(many_y_act, n)
                                pe.wait_ge(many_y_dve, n)
                            for half in range(2):
                                expert_out(half, w_d, hT[0]).then_inc(many_down, 1)
                    pe.wait_ge(many_down, 2 * (2 * pair + 2) * BLOCKS_MAX)
                    pe.nop().then_inc(gate_done, 2)
                    pe.nop().then_inc(up_done, 2)
                    pe.nop().then_inc(down_done, 4)

                many_products(0, True)
                with pe.Fori(1, PAIRS) as pair:
                    many_products(pair, False)
            with pe.Else():
                def pair_products(pair, peeled):
                    def gate(j):
                        pe.wait_ge(ring_full[W_SLOT[2 * j]], pair_fill(pair, 2 * j))
                        pe.wait_ge(xb_ready, 2 * pair + j + 1)
                        if not peeled:
                            pe.wait_ge(sil_ready, 2 * pair + j - 1)
                        expert_in(bank[j], W_SLOT[2 * j], xb[j]).then_inc(gate_done, 1)

                    def up(j):
                        pe.wait_ge(ring_full[W_SLOT[2 * j + 1]], pair_fill(pair, 2 * j + 1))
                        if not peeled:
                            pe.wait_ge(hid_ready, 2 * pair + j - 1)
                        expert_in(bank[2 + j], W_SLOT[2 * j + 1], xb[j]).then_inc(up_done, 1)

                    def turn(j):
                        pe.wait_ge(hid_ready, 2 * pair + j + 1)
                        if not peeled:
                            pe.wait_ge(hT_ready, 2 * pair + j - 1)
                        expert_turn(bank[4 + j], hid[j]).then_inc(hid_turned, 1)

                    def down(j, half):
                        if half == 0:
                            pe.wait_ge(ring_full[W_SLOT[4 + j]], pair_fill(pair, 4 + j))
                            pe.wait_ge(hT_ready, 2 * pair + j + 1)
                        if j or not peeled:
                            pe.wait_ge((y_act, y_dve)[half], 2 * pair + j)
                        expert_out(half, W_SLOT[4 + j], hT[j]).then_inc(down_done, 1)

                    gate(0)
                    up(0)
                    gate(1)
                    turn(0)
                    up(1)
                    down(0, 0)
                    turn(1)
                    down(0, 1)
                    down(1, 0)
                    down(1, 1)

                pair_products(0, True)
                with pe.Fori(1, PAIRS) as pair:
                    pair_products(pair, False)
            pe.wait_ge(y_rows_in, 16)
            pe.wait_ge(slot_wt_ready, 2)
            for use in range(4):
                half, t = divmod(use, NT)
                for s in range(SLOTS // P):
                    last = pe.matmul(bank[use][:, :], slot_wt[:, s, t * P:(t + 1) * P],
                                     y_rows[:, s, half * 512:(half + 1) * 512],
                                     start=(s == 0), stop=(s == SLOTS // P - 1))
                last.then_inc(moe_done, 1)
            pe_turn(pe, 2)
            wait_nT(pe, 2)
            n = CH_IN2
            ring_wait(pe, n)
            for t in range(NT):
                pe_rows(pe, bank[4 + t][:, :], n % RING, t).then_inc(p2_done, 1)
            ring_wait(pe, n + 1)
            for t in range(NT):
                last = pe_rows(pe, bank[6][:, t * 256:(t + 1) * 256], (n + 1) % RING, t, 256)
            last.then_inc(p2_done, 1)
            for i, banks in ((2, (7, 0)), (3, (1, 2))):
                ring_wait(pe, n + i)
                for half in range(2):
                    for m in range(2):
                        last = pe_columns(pe, bank[banks[half]][:, m * T:(m + 1) * T], (n + i) % RING, 2 * half + m)
                    last.then_inc(p2_done, 1)
            ring_wait(pe, n + 4)
            for t in range(NT):
                if t:
                    pe.wait_ge(p2_act, 1)
                pe_rows(pe, bank[3 + t][:, :], (n + 4) % RING, t).then_inc(p2_done, 1)
            pe.wait_ge(qk_roped, 1)
            pe.wait_ge(p2_act, 3)
            for i in range(2):
                for a in (2 * i, 2 * i + 1):
                    for t in range(NT):
                        o = (a % 2) * T + t * P
                        last = pe.transpose(bank[5 + i][:, o:o + P], qk[:, t, a * P:(a + 1) * P], ident)
                last.then_inc(qk_turned, 1)
            pe.wait_ge(p2_dve, 1)
            for a in range(KV_HEADS):
                for t in range(NT):
                    last = pe.transpose(bank[7][:, a * T + t * P:a * T + (t + 1) * P],
                                        kk[:, t, a, :, :].rearrange("p r d -> p (r d)"), ident)
            last.then_inc(qk_turned, 1)

            def scores(dst, qT, kT, key_pair, i):
                part = slice((i % 2) * DH, (i % 2) * DH + DH)
                for t in range(NT):
                    last = pe.matmul(dst[:, t * T:(t + 1) * T], qT[part, i // 2, t * P:(t + 1) * P], kT[part, key_pair, :],
                                     start=True, stop=True)
                return last

            def turn_probs(dst, prob):
                for k in range(NT):
                    for t in range(NT):
                        last = pe.transpose(dst[:, k * T + t * P:k * T + (t + 1) * P], prob[:, t, k * P:(k + 1) * P], ident)
                return last

            def weigh(dst, v, first, prob_t):
                for k in range(NT):
                    last = pe.matmul(dst, v[:, k, first:first + DH], prob_t[:, k, :], start=(k == 0), stop=(k == NT - 1))
                return last

            def both_scores(i):
                scores(bank[0], qaT, kaT, i // 2, i).then_inc(sa_done, 1)
                scores(bank[1], qbT, kbT, i // 4, i).then_inc(sb_done, 1)

            pe.wait_ge(p2_act, 5)
            pe.wait_ge(p2_dve, 4)
            pe.wait_ge(qbT_ready, 2)
            pe.wait_ge(kbT_ready, 1)
            both_scores(0)
            for i in range(NA_HEADS):
                if i % 2 == 0:
                    ring_wait(pe, CH_IN2 + 5 + i // 2)
                if i >= 3:
                    pe.wait_ge(gate2_act, i - 2)
                for m in range(2):
                    last = pe_columns(pe, bank[5 + i % 3][:, m * T:(m + 1) * T], (CH_IN2 + 5 + i // 2) % RING, 2 * (i % 2) + m)
                last.then_inc(gate2_done, 1)
                pe.wait_ge(pa_ready, i + 1)
                turn_probs(bank[2], prob_a).then_inc(pa_turned, 1)
                pe.wait_ge(pb_ready, i + 1)
                turn_probs(bank[3], prob_b).then_inc(pb_turned, 1)
                if i + 1 < NA_HEADS:
                    both_scores(i + 1)
                pe.wait_ge(paT_ready, i + 1)
                if i:
                    pe.wait_ge(ya_ready, i)
                    pe.wait_ge(yb_ready, i)
                weigh(bank[4][0:DH, 0:T], va, i * DH, prob_aT).then_inc(ya_done, 1)
                pe.wait_ge(pbT_ready, i + 1)
                weigh(bank[4][DH:P, 0:T], vb, (i // 4) * DH, prob_bT).then_inc(yb_done, 1)
            pe.wait_ge(ya_ready, NA_HEADS)
            pe.wait_ge(yb_ready, GQA_HEADS)
            pe.wait_ge(gate2_act, 8)
            ring_wait(pe, CH_PROJ)
            ring_wait(pe, CH_PROJ + 1)
            for i in range(4):
                for b, y in enumerate((yaT, ybT)):
                    for m in range(2):
                        for k in range(4):
                            mt = 2 * i + m
                            last = pe.matmul(bank[BRANCH_BANK[b][i]][:, m * T:(m + 1) * T],
                                             ring4((CH_PROJ + b) % RING)[:, k, mt * P:(mt + 1) * P], y[:, k, :],
                                             start=(k == 0), stop=(k == 3))
                    last.then_inc(branch_done, 1)
            pe.wait_ge(merged_ready, 4)
            for half in range(2):
                ring_wait(pe, CH_OUT2 + half)
                for t in range(NT):
                    for k in range(KD):
                        last = pe.matmul(bank[2 * half + t][:, :], sga[:, k, t * P:(t + 1) * P],
                                         ring8((CH_OUT2 + half) % RING)[:, k, :], start=(k == 0), stop=(k == KD - 1))
                    last.then_inc(out2_done, 1)
            pe_turn(pe, 3)
            wait_nT(pe, 3)
            for use in range(8):
                n = CH_WQ + use // 2
                if use % 2 == 0:
                    ring_wait(pe, n)
                for m in range(2):
                    last = pe_columns(pe, bank[QUERY_BANK[use]][:, m * T:(m + 1) * T], n % RING, 2 * (use % 2) + m)
                last.then_inc(query_done, 1)
            pe.wait_ge(query_act, 4)
            pe.wait_ge(query_dve, 4)
            pe.wait_ge(keys_in, 16)
            for use in range(8):
                t, part = divmod(use, 4)
                for a in range(4):
                    hp = 4 * part + a
                    last = pe.matmul(bank[QUERY_BANK[use]][:, a * NKEYS:(a + 1) * NKEYS], qT[:, hp, t * P:(t + 1) * P],
                                     keysT[:, hp, :], start=True, stop=True)
                last.then_inc(score_done, 1)

            def act_products(c2, peeled):
                for s in range(2):
                    u = ring[s][:, :].rearrange("p (k j i) -> p k j i", k=KD, j=CJ)
                    pe.wait_ge(u_full[s], 16 * (c2 + 1))
                    for b in range(2):
                        if s or not peeled:
                            pe.wait_ge(act_ready, 4 * c2 + 2 * s + b - 1)
                        for j in range(2):
                            for k in range(KD):
                                last = pe.matmul(bank[4 + b][:, j * T:(j + 1) * T], u[:, k, 2 * b + j, :], nT[:, k, :],
                                                 start=(k == 0), stop=(k == KD - 1))
                        last.then_inc(act_done, 1)

            pe.wait_ge(score_ready, 8)
            act_products(0, True)
            with pe.Fori(1, R_SPLIT) as c2:
                act_products(c2, False)
            pe.wait_ge(gates_ready, 1)
            for i, src in enumerate((best, ij[:, 0], ij[:, 1])):
                for t in range(NT):
                    last = pe.transpose(bank[6 + i // 2][:, (i % 2) * T + t * P:(i % 2) * T + (t + 1) * P], src[:, t, :], ident)
            last.then_inc(route_turned, 1)
            with pe.Fori(R_SPLIT, PEER_CHUNKS // 2) as c2:
                act_products(c2, False)

            def gate_products(g, b, peeled):
                pe.wait_ge(hot_j_ready, g + 1)
                if not peeled:
                    pe.wait_ge(gated, g - 1)
                for t in range(GT):
                    last = pe.matmul(bank[6 + b][:, t * NKEYS:(t + 1) * NKEYS], hot[b][:, 0, t, :], hot[b][:, 1, t, :],
                                     start=True, stop=True)
                last.then_inc(gates_done, 1)

            pe.wait_ge(route_ready, 1)
            for b in range(2):
                gate_products(b, b, True)
            with pe.Fori(1, GROUPS // 2) as g2:
                for b in range(2):
                    gate_products(2 * g2 + b, b, False)

            def out_products(c2, first, last):
                for s in range(2):
                    v = ring[s][:, :].rearrange("p (j d) -> p j d", j=CJ)
                    pe.wait_ge(v_full[s], 16 * (c2 + 1))
                    for b in range(2):
                        pe.wait_ge(hid_ready2, 4 * c2 + 2 * s + b + 1)
                        for j in range(2):
                            for t in range(NT):
                                for half in range(2):
                                    ins = pe.matmul(bank[2 * half + t][:, :], hidT[b][:, j, t * P:(t + 1) * P],
                                                    v[:, 2 * b + j, half * 512:(half + 1) * 512],
                                                    start=(first and s == 0 and b == 0 and j == 0),
                                                    stop=(last and s == 1 and b == 1 and j == 1))
                        ins.then_inc(hid_used, 1)

            out_products(0, True, False)
            with pe.Fori(1, PEER_CHUNKS // 2 - 1) as c2:
                out_products(c2, False, False)
            out_products(PEER_CHUNKS // 2 - 1, False, True)

        @block.vector
        def _(dve):
            link = chain(dve, dve_step)
            dve_stats(dve, link, 0)
            dve_xhat(dve)
            dve.wait_ge(param_in, 16)
            dve.tensor_tensor(lbd[:, :], prs("lb0"), prs("lb1"), ALU.subtract).then_inc(lb_diff, 1)
            dve_nT(dve, 0, "gain1")
            dve.wait_ge(lb_sig, 1)
            link(dve.tensor_scalar(omlb[:, :], lb[:, :], -1.0, 1.0, ALU.mult, ALU.add))
            dve.wait_ge(proj_act, 2)
            for hd in range(HEADS):
                last = dve.tensor_scalar(hF[:, hd, :], hF[:, hd, :], omlb[:, hd:hd + 1], lb[:, hd:hd + 1],
                                         ALU.mult, ALU.add)
            link(last)
            dve.tensor_scalar(hK[:, :, :], hF[:, :, :], -1.0, 1.0, ALU.mult, ALU.add).then_inc(f_ready, 1)
            for use, dst in ((2, hQ), (3, hQ), (4, hG), (5, hG)):
                dve.wait_ge(proj_act, use + 1)
                half = use % 2
                view = dst[:, 2 * half:2 * half + 2, :].rearrange("p a t -> p (a t)")
                dve.tensor_tensor(view, bank[IN1_BANK[use]][:, :], view, ALU.mult).then_inc(proj_dve, 1)
            dve.wait_ge(lf_ready, 1)
            for hd in range(HEADS):
                last = dve.tensor_tensor_scan(hB[:, hd, :], c("scanmask"), hF[:, hd, :], 0.0, ALU.mult, ALU.add)
            link(last)

            def chunks(tile):
                return tile[:, :, :].rearrange("p a (n s) -> p (a n) s", s=CHUNK)

            b_all = chunks(hB)
            shape = [P, HEADS * N_CHUNKS, CHUNK]
            mid = spread(b_all[:, :, CHUNK // 2 - 1:CHUNK // 2], shape)
            end = spread(b_all[:, :, CHUNK - 1:CHUNK], shape)
            dve.tensor_tensor(chunks(hD1), b_all, mid, ALU.subtract).then_inc(d_ready, 1)
            dve.tensor_tensor(chunks(hD2), end, b_all, ALU.subtract).then_inc(d_ready, 1)
            dve.wait_ge(exp_ready, 1)
            dve.wait_ge(proj_dve, 4)
            dve.tensor_tensor(hF[:, :, :], hQ[:, :, :], hF[:, :, :], ALU.mult).then_inc(qk_ready, 1)
            dve.wait_ge(exp_ready, 2)
            dve.tensor_tensor(hD1[:, :, :], hK[:, :, :], hD1[:, :, :], ALU.mult).then_inc(qk_ready, 1)
            dve.wait_ge(exp_ready, 3)
            dve.tensor_tensor(hD2[:, :, :], hK[:, :, :], hD2[:, :, :], ALU.mult).then_inc(qk_ready, 1)
            dve.wait_ge(exp_ready, 4)
            dve.wait_ge(qk_zero, 2)
            for odd, dst in enumerate((hQE, hQO)):
                def pick(tile):
                    return tile[:, :, :].rearrange("p a (n e s) -> p (a n) e s", e=2, s=CHUNK)[:, :, odd, :]
                dve.tensor_tensor(pick(dst), pick(hQ), pick(hEB), ALU.mult).then_inc(qk_ready, 1)
            dve.wait_ge(qk_zero, 3)
            mask = spread(c("causal").bitcast(U32).unsqueeze(1), [P, HEADS, P])
            for t in range(NT):
                dve.wait_ge(sc_done, t + 1)
                dve.copy_predicated(hSC[:, t, :, :], mask, quad(bank[t])).then_inc(sc_masked, 1)
            dve.wait_ge(proj_act, 10)
            link(dve.tensor_tensor(mSQ[:, :, :], mV[:, :, :], mV[:, :, :], ALU.mult))
            link(dve.tensor_reduce(vss[:, :], mSQ[:, :, :].rearrange("p t (g c) -> p (t g) c", g=HEADS), AX_X, ALU.add))
            dve.tensor_scalar(vss[:, :], vss[:, :], 1.0 / P, EPS, ALU.mult, ALU.add).then_inc(v_ms, 1)
            dve.wait_ge(v_sd, 1)
            link(dve.reciprocal(vrs[:, :], vrs[:, :]))
            v8 = mV[:, :, :].rearrange("p t (g c) -> p (t g) c", g=HEADS)
            dve.tensor_tensor(v8, v8, spread(vrs[:, :].unsqueeze(2), [P, NT * HEADS, P]), ALU.mult).then_inc(vh_ready, 1)
            dve.wait_ge(state_done, 1)
            dve.tensor_copy(hS[:, 0, :, :], quad(bank[4])).then_inc(state_ready, 1)
            eb = hEB[:, :, :].rearrange("p a (n s) -> p a n s", s=CHUNK)
            for n in (1, 2):
                dve.wait_ge(state_ready, n)
                decay = spread(eb[:, :, n, CHUNK - 1:CHUNK], [P, HEADS, P])
                link(dve.tensor_tensor(hS[:, n, :, :], hS[:, n - 1, :, :], decay, ALU.mult))
                dve.wait_ge(state_done, n + 1)
                dve.tensor_tensor(hS[:, n, :, :], quad(bank[4 + n]), hS[:, n, :, :], ALU.add).then_inc(state_ready, 1)
            dve.wait_ge(rows_in, 16)
            dve.wait_ge(proj_act, 12)
            for g in range(HEADS):
                dve.wait_ge(mixed_done, g // 2 + 1)
                src = bank[7 if g < 2 else 4][:, (g % 2) * T:(g % 2 + 1) * T].rearrange("p (t i) -> p t i", t=NT)
                bias = spread(row("b_s")[:, g * P:(g + 1) * P].unsqueeze(1), [P, NT, P])
                dst = mixT[:, g, :].rearrange("p (t i) -> p t i", t=NT)
                link(dve.scalar_tensor_tensor(dst, src, pr("vgain", g), bias, ALU.mult, ALU.add))
                dve.tensor_tensor(mixT[:, g, :], mixT[:, g, :], mU[:, g, :], ALU.mult).then_inc(mix_g, 1)
            dve.wait_ge(o_sq, NT)
            link(dve.tensor_reduce(oss[:, :], mSQ[:, :, :].rearrange("p t (g c) -> p (t g) c", g=HEADS), AX_X, ALU.add))
            dve.tensor_scalar(oss[:, :], oss[:, :], 1.0 / P, EPS, ALU.mult, ALU.add).then_inc(o_ms, 1)
            dve.wait_ge(o_sd, 1)
            link(dve.reciprocal(ors[:, :], ors[:, :]))
            for t in range(NT):
                last = dve.tensor_tensor(hON[:, t, :].rearrange("p (g c) -> p g c", g=HEADS), quad(bank[t]),
                                         spread(ors[:, t * HEADS:(t + 1) * HEADS].unsqueeze(2), [P, HEADS, P]), ALU.mult)
            last.then_inc(on_ready, 1)
            for hd in range(HEADS):
                dve.wait_ge(on_turned, hd // 2 + 1)
                dve.scalar_tensor_tensor(mixT[:, HEADS + hd, :], bank[2 + hd // 2][:, (hd % 2) * T:(hd % 2 + 1) * T],
                                         pr("ogain", hd), hG[:, hd, :], ALU.mult, ALU.mult).then_inc(mix_h, 1)
            for half in range(2):
                for t in range(NT):
                    dve.wait_ge(out1_done, 2 * half + t + 1)
                    dst = h[:, t, half * 512:(half + 1) * 512]
                    dve.tensor_tensor(dst, bank[OUT1_BANK[2 * half + t]][:, :], dst, ALU.add).then_inc(h_ready, 1)
            dve_stats(dve, link, 1)
            dve_xhat(dve)
            dve_nT(dve, 1, "gain2")
            dve.memset(g8[:, :, :], BIG)
            dve.memset(em[:, :, :], BIG)
            dve.wait_ge(router_done, 1)
            link(dve.tensor_tensor(lg[:, :, :], bank[4][:, 0:2 * 64].rearrange("p (t e) -> p t e", t=NT)[:, :, 0:NE],
                                   spread(row("b_router").unsqueeze(1), [P, NT, NE]), ALU.add))
            link(dve.tensor_copy(g8[:, :, 0:N_GROUPS], lg[:, :, 0:N_GROUPS]))
            for t in range(NT):
                last = dve.max(gm8[:, t, :], g8[:, t, :])
            link(last)
            for t in range(NT):
                last = dve.max_index(gi8[:, t, :], gm8[:, t, :], g8[:, t, :])
            link(last)
            dve.tensor_scalar(gneg[:, :].unsqueeze(2), gm8[:, :, 0:1], -1.0, None, ALU.mult).then_inc(gneg_ready, 1)
            link(dve.tensor_copy(gid[:, :].unsqueeze(2), gi8[:, :, 0:1]))
            for t in range(NT):
                last = dve.tensor_scalar(emask[:, t, :], c("group"), gid[:, t:t + 1], None, ALU.is_equal)
            link(last)
            link(dve.copy_predicated(em[:, :, :], emask[:, :, :], lg[:, :, N_GROUPS:]))
            for t in range(NT):
                last = dve.max(ev8[:, t, :], em[:, t, :])
            link(last)
            for t in range(NT):
                last = dve.max_index(ei8[:, t, :], ev8[:, t, :], em[:, t, :])
            link(last)
            dve.tensor_scalar(eneg[:, :].unsqueeze(2), ev8[:, :, 0:1], -1.0, None, ALU.mult).then_inc(eneg_ready, 1)
            link(dve.tensor_copy(eid[:, :, :], ei8[:, :, 0:2]))
            for k in range(2):
                for t in range(NT):
                    last = dve.tensor_scalar(chosen[:, k, t, :], c("iota")[:, 0:N_EXPERTS], eid[:, t, k:k + 1], None,
                                             ALU.is_equal)
            link(last)
            dve.tensor_tensor(assigned[:, :, :], chosen[:, 0, :, :], chosen[:, 1, :, :], ALU.add).then_inc(assign_ready, 1)
            dve.wait_ge(gsum_ready, NT)
            dve.wait_ge(e21_ready, NT)
            link(dve.scalar_tensor_tensor(wt[:, 0, :], e21[:, :], 1.0, gsum[:, :], ALU.add, ALU.mult))
            link(dve.reciprocal(wt[:, 0, :], wt[:, 0, :]))
            link(dve.tensor_tensor(wt[:, 1, :], wt[:, 0, :], e21[:, :], ALU.mult))
            dve.wait_ge(rank_done, 1)
            link(dve.tensor_copy(counts[:, :], bank[5][:, 64:96]))
            link(dve.tensor_tensor_scan(starts[:, :], c("ones")[:, 0:N_EXPERTS], counts[:, :], 0.0, ALU.mult, ALU.add))
            dve.tensor_reduce(most[:, :], counts[:, :], AX_X, ALU.max)
            link(dve.tensor_tensor(starts[:, :], starts[:, :], counts[:, :], ALU.subtract))
            dve.tensor_copy(most_i[:, :], most[0:1, :])
            dve.tensor_copy(starts_i[:, :], starts[0:1, :]).then_inc(starts_ready, 1)
            link(dve.tensor_tensor(slot_of[:, :, :], bank[5][:, 0:64].rearrange("p (t e) -> p t e", t=NT),
                                   spread(starts[:, :].unsqueeze(1), [P, NT, N_EXPERTS]), ALU.add))
            for k in range(2):
                last = dve.tensor_tensor(chosen[:, k, :, :], chosen[:, k, :, :], slot_of[:, :, :], ALU.mult)
            link(last)
            link(dve.tensor_reduce(slot[:, :, :], chosen[:, :, :, :], AX_X, ALU.add))
            for t in range(NT):
                link(dve.tensor_scalar(pick_slot[:, t, :], c("iota"), slot[:, 0, t:t + 1], None, ALU.is_equal))
                dve.scalar_tensor_tensor(pick_slot[:, t, :], c("iota"), slot[:, 1, t:t + 1], pick_slot[:, t, :],
                                         ALU.is_equal, ALU.add).then_inc(pick_ready, 1)
            for t in range(NT):
                dve.tensor_scalar(pick_wt[:, t, :], c("iota"), slot[:, 0, t:t + 1], wt[:, 0, t:t + 1],
                                  ALU.is_equal, ALU.mult)
                link(dve.tensor_scalar(pick_tmp[:, t, :], c("iota"), slot[:, 1, t:t + 1], wt[:, 1, t:t + 1],
                                       ALU.is_equal, ALU.mult))
                dve.tensor_tensor(pick_wt[:, t, :], pick_wt[:, t, :], pick_tmp[:, t, :], ALU.add).then_inc(pick_ready, 1)
            for k in range(1, KD, 2):
                dve.wait_ge(gather_done, k + 1)
                dve.tensor_scalar(xs[:, k, 0:SLOTS], bank[GATHER_BANK[k]][:, :], pr("gain2", k), None,
                                  ALU.mult).then_inc(xs_dve, 1)

            dve.wait_ge(starts_ready, 1)
            load_most = dve.value_load(most_i[0:1, 0:1], min_val=0, max_val=T)
            with dve.If(load_most > BLOCK):
                def many_vector(e, peeled):
                    for b in range(BLOCKS_MAX):
                        n = e * BLOCKS_MAX + b
                        dve.wait_ge(many_up, n + 1)
                        dve.wait_ge(many_sil, n + 1)
                        dve.tensor_tensor(hid[0][:, :], bank[2][0:BLOCK, :], hid[0][:, :], ALU.mult).then_inc(many_hid, 1)
                        dve.wait_ge(many_down, 2 * n + 2)
                        if b or not peeled:
                            dve.wait_ge(many_stored, 16 * n)
                        dve.tensor_copy(y_blk[0][:, 512:], bank[7][0:BLOCK, :]).then_inc(many_y_dve, 1)

                many_vector(0, True)
                with dve.Fori(1, N_EXPERTS) as e:
                    many_vector(e, False)
            with dve.Else():
                def pair_vector(pair, peeled):
                    for j in range(2):
                        dve.wait_ge(up_done, 2 * pair + j + 1)
                        dve.wait_ge(sil_ready, 2 * pair + j + 1)
                        dve.tensor_tensor(hid[j][:, :], bank[2 + j][0:BLOCK, :], hid[j][:, :], ALU.mult).then_inc(hid_ready, 1)
                    for j in range(2):
                        dve.wait_ge(down_done, 4 * pair + 2 * j + 2)
                        if not peeled:
                            dve.wait_ge(y_stored, 32 * pair + 16 * j - 16)
                        dve.tensor_copy(y_blk[j][:, 512:], bank[7][0:BLOCK, :]).then_inc(y_dve, 1)

                pair_vector(0, True)
                with dve.Fori(1, PAIRS) as pair:
                    pair_vector(pair, False)
            for use in range(4):
                half, t = divmod(use, NT)
                dve.wait_ge(moe_done, use + 1)
                dst = h[:, t, half * 512:(half + 1) * 512]
                dve.tensor_tensor(dst, bank[use][:, :], dst, ALU.add).then_inc(h_ready, 1)
            dve_stats(dve, link, 2)
            dve.wait_ge(gain_in, 16)
            for t in range(NT):
                dve.scalar_tensor_tensor(h[:, t, :], h[:, t, :], stat_rs[:, t:t + 1], gain_row[:, :],
                                         ALU.mult, ALU.mult).then_inc(h_ready, 1)
            dve_stats(dve, link, 3)
            dve_xhat(dve)
            dve_nT(dve, 2, "gain12")
            def halves(ap, half):
                return ap.rearrange("p (s e f) -> p s e f", s=2, e=2)[:, :, half, :]

            dve.wait_ge(h_ready, H_COUNT[3])
            for i, gain in enumerate(("qgain", "kgain")):
                for t in range(NT):
                    cs = c("cos")[:, t * DH:(t + 1) * DH]
                    sn = c("sin")[:, t * DH:(t + 1) * DH]
                    dve.tensor_tensor(cos_gain[:, i, t, :], cs, row(gain), ALU.mult)
                    for half in range(2):
                        last = dve.tensor_tensor(halves(sin_gain[:, i, t, :], half), halves(sn, half),
                                                 halves(row(gain), 1 - half), ALU.mult)
            link(last)
            dve.wait_ge(p2_act, 3)
            link(dve.tensor_reduce(qk_ss[:, :], qk_sq[:, :, :].rearrange("p t (a d) -> p (t a) d", d=DH), AX_X, ALU.add))
            dve.tensor_scalar(qk_ss[:, :], qk_ss[:, :], 1.0 / DH, EPS, ALU.mult, ALU.add).then_inc(qk_ms, 1)
            dve.wait_ge(qk_sd, 1)
            link(dve.reciprocal(qk_rs[:, :], qk_rs[:, :]))
            heads = qk[:, :, :].rearrange("p t (a d) -> p (t a) d", d=DH)
            link(dve.tensor_tensor(heads, heads, spread(qk_rs[:, :].unsqueeze(2), [P, NT * N_QK, DH]), ALU.mult))
            for t in range(NT):
                for i, (a, b) in enumerate(((0, GQA_HEADS), (GQA_HEADS, N_QK))):
                    src = qk[:, t, a * DH:b * DH].rearrange("p (a s e f) -> p (a s) e f", s=2, e=2, f=DH // 4)
                    dst = qk_rot[:, t, a * DH:b * DH].rearrange("p (a s e f) -> p (a s) e f", s=2, e=2, f=DH // 4)
                    for half in range(2):
                        table = spread(halves(sin_gain[:, i, t, :], half).unsqueeze(1), [P, b - a, 2, DH // 4])
                        last = dve.tensor_tensor(dst[:, :, half, :].rearrange("p (a s) f -> p a s f", s=2),
                                                 src[:, :, 1 - half, :].rearrange("p (a s) f -> p a s f", s=2), table, ALU.mult)
            link(last)
            for t in range(NT):
                for i, (a, b) in enumerate(((0, GQA_HEADS), (GQA_HEADS, N_QK))):
                    view = qk[:, t, a * DH:b * DH].rearrange("p (a d) -> p a d", d=DH)
                    last = dve.tensor_tensor(view, view, spread(cos_gain[:, i, t, :].unsqueeze(1), [P, b - a, DH]), ALU.mult)
            link(last)
            nq = GQA_HEADS * DH
            for copy in range(2):
                dve.tensor_tensor(kk[:, :, :, copy, :], qk[:, :, nq:].rearrange("p t (a d) -> p t a d", d=DH),
                                  qk_rot[:, :, nq:].rearrange("p t (a d) -> p t a d", d=DH), ALU.add)
            dve.tensor_tensor(qk[:, :, 0:nq], qk[:, :, 0:nq], qk_rot[:, :, 0:nq], ALU.add).then_inc(qk_roped, 1)
            for i, dst in enumerate((qaT[:, 0:2, :].rearrange("p a t -> p (a t)"),
                                     qaT[:, 2:4, :].rearrange("p a t -> p (a t)"), va[:, 0, :], va[:, 1, :])):
                dve.wait_ge(p2_done, (4, 5, 8, 9)[i])
                dve.tensor_copy(dst, bank[(7, 0, 3, 4)[i]][:, :]).then_inc(p2_dve, 1)
            dve.wait_ge(qk_turned, 3)
            dve.tensor_copy(kbT[:, :, :].rearrange("p a t -> p (a t)"), bank[7][:, :]).then_inc(kbT_ready, 1)
            dve.wait_ge(bias_ready, NT)
            sa = bank[0][:, :].rearrange("p (t k) -> p t k", t=NT)
            sb = bank[1][:, :].rearrange("p (t k) -> p t k", t=NT)
            for i in range(NA_HEADS):
                dve.wait_ge(sa_done, i + 1)
                if i:
                    dve.wait_ge(pa_turned, i)
                link(dve.scalar_tensor_tensor(prob_a[:, :, :], sa, SCALE, rel_bias[:, :, i, :], ALU.mult, ALU.add))
                link(dve.tensor_reduce(top_a[:, :], prob_a[:, :, :], AX_X, ALU.max))
                dve.tensor_scalar(top_a[:, :], top_a[:, :], -1.0, None, ALU.mult).then_inc(ta_ready, 1)
                dve.wait_ge(sb_done, i + 1)
                link(dve.tensor_reduce(top_b[:, :], sb, AX_X, ALU.max))
                dve.tensor_scalar(top_b[:, :], top_b[:, :], -SCALE, None, ALU.mult).then_inc(tb_ready, 1)
                dve.wait_ge(ea_ready, 2 * (i + 1))
                link(dve.reciprocal(sum_a[:, :], sum_a[:, :]))
                dve.tensor_tensor(prob_a[:, :, :], prob_a[:, :, :], spread(sum_a[:, :].unsqueeze(2), [P, NT, T]),
                                  ALU.mult).then_inc(pa_ready, 1)
                dve.wait_ge(eb_ready, 2 * (i + 1))
                link(dve.reciprocal(sum_b[:, :], sum_b[:, :]))
                dve.tensor_tensor(prob_b[:, :, :], prob_b[:, :, :], spread(sum_b[:, :].unsqueeze(2), [P, NT, T]),
                                  ALU.mult).then_inc(pb_ready, 1)
                dve.wait_ge(pb_turned, i + 1)
                if i:
                    dve.wait_ge(yb_done, i)
                dve.tensor_copy(prob_bT[:, :, :].rearrange("p k q -> p (k q)"), bank[3][:, :]).then_inc(pbT_ready, 1)
            dve.wait_ge(sg_ready, 2)
            for i in range(4):
                part = slice(2 * i, 2 * i + 2)
                for b, gate in enumerate((sga, sgb)):
                    dve.wait_ge(branch_done, 2 * i + b + 1)
                    view = gate[:, part, :].rearrange("p a t -> p (a t)")
                    last = dve.tensor_tensor(view, bank[BRANCH_BANK[b][i]][:, :], view, ALU.mult)
                link(last)
                dve.tensor_tensor(sga[:, part, :], sga[:, part, :], sgb[:, part, :], ALU.add).then_inc(merged_ready, 1)
            for half in range(2):
                for t in range(NT):
                    dve.wait_ge(out2_done, 2 * half + t + 1)
                    dst = h[:, t, half * 512:(half + 1) * 512]
                    dve.tensor_tensor(dst, bank[2 * half + t][:, :], dst, ALU.add).then_inc(h_ready, 1)
            dve_stats(dve, link, 4)
            dve_xhat(dve)
            dve_nT(dve, 3, "gain22")
            for use in range(1, 8, 2):
                dve.wait_ge(query_done, use + 1)
                dve.tensor_copy(qT[:, 2 * use:2 * use + 2, :].rearrange("p a t -> p (a t)"),
                                bank[QUERY_BANK[use]][:, :]).then_inc(query_dve, 1)

            def best_of(views):
                for lo in (0, 8):
                    for score, value, _ in views:
                        last = dve.max(value[:, lo:lo + 8], score)
                    link(last)
                    for score, value, place in views:
                        last = dve.max_index(place[:, lo:lo + 8], value[:, lo:lo + 8], score)
                    link(last)
                    if lo == 0:
                        for score, value, _ in views:
                            last = dve.match_replace(score, value[:, 0:8], score, BIG)
                        link(last)

            for use in range(8):
                t, part = divmod(use, 4)
                dve.wait_ge(score_ready, use + 1)
                best_of([(sc[:, t, hp, :], ts[:, t, hp, :], ti[:, t, hp, :]) for hp in range(4 * part, 4 * part + 4)])
            link(dve.tensor_copy(tif[:, :, :, :], ti[:, :, :, :]))
            wide = [P, PEER_HEADS, TOPK, TOPK]

            def half_of(tile, t, half):
                return tile[:, t, :, :].rearrange("p (a e) k -> p a e k", e=2)[:, :, half, :]

            for t in range(NT):
                last = dve.tensor_tensor(cand[:, t, :, :, :], spread(half_of(ts, t, 0).unsqueeze(3), wide),
                                         spread(half_of(ts, t, 1).unsqueeze(2), wide), ALU.add)
            link(last)
            for t in range(NT):
                best_of([(cand[:, t, a, :, :].rearrange("p x y -> p (x y)"), best[:, t, a * TOPK:(a + 1) * TOPK],
                          bpos[:, t, a * TOPK:(a + 1) * TOPK]) for a in range(PEER_HEADS)])
            dve.tensor_scalar(bdig[:, 0, :, :], bpos[:, :, :], 4, None, ALU.logical_shift_right)
            link(dve.tensor_scalar(bdig[:, 1, :, :], bpos[:, :, :], TOPK - 1, None, ALU.bitwise_and))
            link(dve.tensor_copy(bdigf[:, :, :, :], bdig[:, :, :, :]))
            for half in range(2):
                for t in range(NT):
                    link(dve.tensor_tensor(match[:, :, :], spread(c("iota")[:, 0:TOPK].unsqueeze(1), [P, HK, TOPK]),
                                           spread(bdigf[:, half, t, :].unsqueeze(2), [P, HK, TOPK]), ALU.is_equal))
                    by_head = match[:, :, :].rearrange("p (a k) x -> p a k x", a=PEER_HEADS)
                    link(dve.tensor_tensor(by_head, by_head, spread(half_of(tif, t, half).unsqueeze(2), wide), ALU.mult))
                    link(dve.tensor_reduce(ij[:, half, t, :], match[:, :, :], AX_X, ALU.add))
            by_head = best[:, :, :].rearrange("p t (a k) -> p (t a) k", k=TOPK)
            flat = [P, NT * PEER_HEADS, TOPK]
            link(dve.tensor_copy(best_sum[:, :].unsqueeze(2), by_head[:, :, 0:1]))
            dve.tensor_tensor(by_head, by_head, spread(best_sum[:, :].unsqueeze(2), flat), ALU.subtract).then_inc(routed, 1)
            dve.wait_ge(best_exp, 1)
            link(dve.tensor_reduce(best_sum[:, :], by_head, AX_X, ALU.add))
            link(dve.reciprocal(best_sum[:, :], best_sum[:, :]))
            dve.tensor_tensor(by_head, by_head, spread(best_sum[:, :].unsqueeze(2), flat), ALU.mult).then_inc(gates_ready, 1)
            dve.wait_ge(route_turned, 1)
            dve.tensor_copy(bestT[:, :], bank[6][:, 0:T])
            dve.tensor_copy(ijT[:, 0, :], bank[6][:, T:])
            dve.tensor_copy(ijT[:, 1, :], bank[7][:, 0:T]).then_inc(route_ready, 1)

            def one_hots(g, b):
                whole = [P, 2, GT, NKEYS]
                dve.tensor_tensor(hot[b][:, :, :, :], spread(c("iota")[:, 0:NKEYS].unsqueeze(1).unsqueeze(1), whole),
                                  spread(ijT[:, :, bass.ds(g * GT, GT)].unsqueeze(3), whole),
                                  ALU.is_equal).then_inc(hot_ready, 1)

            def gate_columns(g, b):
                dve.wait_ge(gates_done, g + 1)
                view = A[:, :, bass.ds(g * GT, GT)]
                dve.tensor_tensor(view, bank[6 + b][:, :].rearrange("p (t j) -> p j t", t=GT), view, ALU.mult).then_inc(gated, 1)

            dve.wait_ge(route_ready, 1)
            for b in range(2):
                one_hots(b, b)
            dve.wait_ge(act_ready, 2 * PEER_CHUNKS)
            with dve.Fori(0, GROUPS // 2 - 1) as g2:
                for b in range(2):
                    gate_columns(2 * g2 + b, b)
                    one_hots(2 * g2 + b + 2, b)
            for b in range(2):
                gate_columns(GROUPS - 2 + b, b)
            for use in range(4):
                half, t = divmod(use, NT)
                dve.wait_ge(hid_used, 2 * PEER_CHUNKS)
                dst = h[:, t, half * 512:(half + 1) * 512]
                dve.tensor_tensor(dst, bank[2 * half + t][:, :], dst, ALU.add).then_inc(h_ready, 1)
            dve_stats(dve, link, 5)
            dve.wait_ge(gain_f_in, 16)
            for t in range(NT):
                dve.scalar_tensor_tensor(h[:, t, :], h[:, t, :], stat_rs[:, t:t + 1], gain_f[:, :],
                                         ALU.mult, ALU.mult).then_inc(out_ready, 1)

        return locals()


def layouts(inputs):
    g = {k: np.asarray(v) for k, v in inputs.items()}

    def across(a):
        return a.reshape(-1, P).T

    out = {
        "x": g["x"][0],
        "const": constants(),
        "param": np.concatenate([
            across(g["norm1_gain"][0]), across(g["gmlp_v_gain"][0]), across(g["hgrn_lower_bounds"][0]),
            across(g["hgrn_lower_bounds"][1]), across(g["hgrn_out_gain"][0]), across(g["norm2_gain"][0]),
            across(g["norm1_g_2"][0]), across(g["norm2_g_2"][0])], axis=1),
        "rows": np.concatenate([g["gmlp_b_s"][0].reshape(-1), g["b_group_router"][0], g["b_expert_router"][0],
                                g["gqa_q_norm_g_2"][0], g["gqa_k_norm_g_2"][0]])[None],
        "w_in": g["w_in"][0],
        "w_sT": g["gmlp_w_s"][0].transpose(2, 0, 1).reshape(P, HEADS * P),
        "w_out": g["w_out"][0],
        "w_group_router": g["w_group_router"][0],
        "w_expert_router": g["w_expert_router"][0],
        "w_gate": g["w_gate"][0],
        "w_up": g["w_up"][0],
        "w_down": g["w_down"][0],
        "final_gain": g["final_gain"][None],
        "w_in_2": g["w_in_2"][0],
        "rpb": g["na_rpb_2"][0].reshape(-1),
        "w_proj_a": g["w_proj_a_2"][0],
        "w_proj_b": g["w_proj_b_2"][0],
        "w_out_2": g["w_out_2"][0],
        "w_q": g["peer_w_q_2"][0],
        "keysT": g["peer_sub_keys_2"][0].transpose(3, 0, 1, 2).reshape(P, HP * NKEYS),
        "u": g["peer_u_2"][0].reshape(NKEYS, PEER_CHUNKS, CJ, KD, P).transpose(1, 4, 3, 2, 0).reshape(PEER_CHUNKS, P, -1),
        "v": g["peer_v_2"][0].reshape(NKEYS, PEER_CHUNKS, CJ * D).transpose(1, 0, 2),
        "norm_f_g": g["norm_f_g_2"][None],
    }
    return {k: np.ascontiguousarray(v) for k, v in out.items()}


def kernel(**inputs):
    import concourse.bacc as bacc
    from concourse.bass_utils import run_bass_kernel_spmd

    arrays = layouts(inputs)
    nc = bacc.Bacc("TRN2", target_bir_lowering=False, num_devices=1)
    dram = {k: nc.dram_tensor(f"in_{k}", v.shape, mybir.dt.from_np(v.dtype), kind="ExternalInput").ap()
            for k, v in arrays.items()}
    out = nc.dram_tensor("out", (T, D), F32, kind="ExternalOutput").ap()
    build(nc, dram, out)
    r = run_bass_kernel_spmd(nc, [{f"in_{k}": v for k, v in arrays.items()}], core_ids=[0])
    return r.results[0]["out"].reshape(1, T, D)
```

```python
from contextlib import ExitStack

import numpy as np

import concourse.bass as bass
from concourse import mybir

F32 = mybir.dt.float32
F32R = mybir.dt.float32r
U32 = mybir.dt.uint32
I32 = mybir.dt.int32
ALU = mybir.AluOpType
ACT = mybir.ActivationFunctionType
AX_X = mybir.AxisListType.X

P = 128
T = 256
NT = T // P
D = 1024
KD = D // P
EPS = 1e-6
BIG = -3.0e38

HEADS = 4
CHUNK = 64
N_CHUNKS = T // CHUNK
N_GROUPS = 4
N_EXPERTS = 32
PER_GROUP = N_EXPERTS // N_GROUPS
D_EXPERT = 512
SLOTS = 2 * T
BLOCK = 64
BLOCKS_MAX = T // BLOCK
SLOTS_PAD = SLOTS + T

NA_HEADS = 8
DH = 64
GRID_W = 64
KROWS = T // GRID_W
WIN_W = 16
RPB_H, RPB_W = 15, 31
RPB_ROWS = 2 * KROWS - 1
GQA_HEADS = 8
KV_HEADS = 2
N_QK = GQA_HEADS + KV_HEADS
SCALE = DH ** -0.5
PEER_HEADS = 8
NKEYS = 128
TOPK = 16
HP = 2 * PEER_HEADS

RING = 6
CHUNK_COLS = 4096
IN1_ORDER = (3, 2, 5, 4, 1, 0)
CH_OUT1 = 6
CH_MOE = CH_OUT1 + 2
CH_IN2 = CH_MOE + 3 * N_EXPERTS
IN2_COLS = [(1536, 512), (2048, 256), (0, 512), (512, 512), (1024, 512),
            (2304, 512), (2816, 512), (3328, 512), (3840, 512)]
CH_PROJ = CH_IN2 + len(IN2_COLS)
CH_OUT2 = CH_PROJ + 2
CH_WQ = CH_OUT2 + 2
CH_END = CH_WQ + 4

CJ = 2
RAW_SLOTS = 3
UNROLL = 6
PLAIN = 16
PEER_CHUNKS = NKEYS // CJ
HK = PEER_HEADS * TOPK
GT = 4
GROUPS = T // GT

PAIR = [(0, 0), (0, 1), (0, 2), (1, 0), (1, 1), (1, 2)]
PAIRS = N_EXPERTS // 2

CONST_PARTS = [("ident", P), ("iota", SLOTS), ("causal", P), ("scanmask", T), ("before", P), ("ones", P),
               ("window", GRID_W), ("cos", NT * DH), ("sin", NT * DH), ("group", N_EXPERTS)]
PARAM_PARTS = [("gain1", KD), ("vgain", HEADS), ("lb0", HEADS), ("lb1", HEADS), ("ogain", HEADS),
               ("gain2", KD), ("gain12", KD), ("gain22", KD)]
ROW_PARTS = [("b_s", HEADS * P), ("b_router", N_GROUPS + N_EXPERTS), ("qgain", DH), ("kgain", DH)]


def columns(parts):
    at, out = 0, {}
    for name, n in parts:
        out[name] = (at, at + n)
        at += n
    return out, at


CONST_AT, CONST_N = columns(CONST_PARTS)
PARAM_AT, PARAM_N = columns(PARAM_PARTS)
ROW_AT, ROW_N = columns(ROW_PARTS)


def constants():
    c = np.zeros((P, CONST_N), np.float32)

    def put(name, value):
        a, b = CONST_AT[name]
        c[:, a:b] = value

    p = np.arange(P)
    put("ident", np.eye(P))
    put("causal", (p[:, None] <= p[None, :]) & (p[:, None] // CHUNK == p[None, :] // CHUNK))
    put("scanmask", np.broadcast_to(np.arange(T) % CHUNK != 0, (P, T)))
    put("iota", np.broadcast_to(np.arange(SLOTS), (P, SLOTS)))
    put("before", p[:, None] < p[None, :])
    put("ones", 1.0)
    col = p % GRID_W
    start = np.clip(col - WIN_W // 2, 0, GRID_W - WIN_W)
    key = np.arange(GRID_W)
    inside = (key[None, :] >= start[:, None]) & (key[None, :] < start[:, None] + WIN_W)
    put("window", np.where(inside, 0.0, BIG))
    sec, nf = DH // 2, DH // 4
    t = np.arange(T)
    inv = np.float32(10000.0) ** (-np.arange(nf, dtype=np.float32) / np.float32(nf))
    ang_r = (t // GRID_W).astype(np.float32)[:, None] * inv[None, :]
    ang_c = (t % GRID_W).astype(np.float32)[:, None] * inv[None, :]
    cos = np.concatenate([np.cos(ang_r), np.cos(ang_r), np.cos(ang_c), np.cos(ang_c)], 1)
    sin = np.concatenate([-np.sin(ang_r), np.sin(ang_r), -np.sin(ang_c), np.sin(ang_c)], 1)
    put("cos", cos.reshape(NT, P, DH).transpose(1, 0, 2).reshape(P, NT * DH))
    put("sin", sin.reshape(NT, P, DH).transpose(1, 0, 2).reshape(P, NT * DH))
    put("group", np.broadcast_to(np.arange(N_EXPERTS) // PER_GROUP, (P, N_EXPERTS)))
    return c


def build(nc, dram, out):
    with ExitStack() as ctx:
        place = [16512]

        def keep(name, shape, dt=F32):
            n = 4
            for s in shape[1:]:
                n *= s
            t = nc.alloc_sbuf_tensor_at(name, shape, dt, offset=place[0])
            place[0] += (n + 31) // 32 * 32
            return t

        ARENA = 229344 - 176 * 1024
        ACTS = ARENA + RING * 16384

        def at(name, shape, offset, dt=F32):
            return nc.alloc_sbuf_tensor_at(name, shape, dt, offset=offset)

        def acts(name, shape, kib, dt=F32):
            return at(name, shape, ACTS + int(kib * 1024), dt)

        h = keep("h", [P, NT, D])
        NT_AT = place[0]
        nT = keep("nT", [P, KD, T])
        param = keep("param", [P, PARAM_N])
        stat_ss = keep("stat_ss", [P, NT])
        stat_ms = keep("stat_ms", [P, NT])
        stat_sd = keep("stat_sd", [P, NT])
        stat_rs = keep("stat_rs", [P, NT])
        DEAD_AT = place[0] + 4 * CONST_AT["causal"][0]
        const = keep("const", [P, CONST_N])
        rows = keep("rows", [P, ROW_N])
        w_router = keep("w_router", [P, KD, N_GROUPS + N_EXPERTS])

        def c(name):
            a, b = CONST_AT[name]
            return const[:, a:b]

        def pr(name, i):
            a = PARAM_AT[name][0]
            return param[:, a + i:a + i + 1]

        def prs(name):
            a, b = PARAM_AT[name]
            return param[:, a:b]

        def row(name):
            a, b = ROW_AT[name]
            return rows[:, a:b]

        ident = c("ident")

        ring = [at(f"ring{s}", [P, CHUNK_COLS], ARENA + 16384 * s) for s in range(RING)]

        def ring8(s):
            return ring[s][:, :].rearrange("p (k f) -> p k f", k=8)

        ring_rest = [at(f"ring_rest{s}", [P, CHUNK_COLS], ARENA + 16384 * s, F32R) for s in range(RING)]

        def ring_rest8(s):
            return ring_rest[s][:, :].rearrange("p (k f) -> p k f", k=8)

        def ring4(s):
            return ring[s][:, :].rearrange("p (k f) -> p k f", k=4)

        xhat = acts("xhat", [P, NT, D], 0)
        mixT = acts("mixT", [P, 8, T], 0)
        hF = acts("hF", [P, HEADS, T], 8)
        hK = acts("hK", [P, HEADS, T], 12)
        hB = acts("hB", [P, HEADS, T], 16)
        hD1 = acts("hD1", [P, HEADS, T], 20)
        hD2 = acts("hD2", [P, HEADS, T], 24)
        hEB = acts("hEB", [P, HEADS, T], 28)
        hQ = acts("hQ", [P, HEADS, T], 32)
        hQE = acts("hQE", [P, HEADS, T], 36)
        hQO = acts("hQO", [P, HEADS, T], 40)
        hI = acts("hI", [P, NT, 512], 44)
        hKL = acts("hKL", [P, NT, HEADS, P], 48)
        hSC = acts("hSC", [P, NT, HEADS, P], 52)
        hS = acts("hS", [P, N_CHUNKS - 1, HEADS, P], 56)
        hG = acts("hG", [P, HEADS, T], 62)
        mU = acts("mU", [P, HEADS, T], 66)
        mV = acts("mV", [P, NT, 512], 70)
        mSQ = acts("mSQ", [P, NT, 512], 74)
        hON = acts("hON", [P, NT, 512], 16)
        w_sT = acts("w_sT", [P, HEADS, P], 78)
        lbd = keep("lbd", [P, HEADS])
        lb = keep("lb", [P, HEADS])
        omlb = keep("omlb", [P, HEADS])
        vss = keep("vss", [P, NT * HEADS])
        vrs = keep("vrs", [P, NT * HEADS])
        oss = keep("oss", [P, NT * HEADS])
        ors = keep("ors", [P, NT * HEADS])

        pick_slot = acts("pick_slot", [P, NT, SLOTS], 8)
        pick_wt = acts("pick_wt", [P, NT, SLOTS], 12)
        pick_tmp = acts("pick_tmp", [P, NT, SLOTS], 16)
        xs = acts("xs", [P, KD, SLOTS_PAD], 20)
        x_blk = [acts(f"x_blk{j}", [P, KD, BLOCK], 4 + 2 * j) for j in range(2)]
        x_two = [acts(f"x_two{j}", [P, KD, 2 * BLOCK], (16, 0)[j], F32R) for j in range(2)]
        w_lead = [acts(f"w_lead{b}", [P, 4, 512], 52 + 8 * b, F32R) for b in range(2)]
        hid = [acts(f"hid{j}", [BLOCK, D_EXPERT], 44 + 2 * j) for j in range(2)]
        upv = [acts(f"upv{j}", [BLOCK, D_EXPERT], 68 + 2 * j) for j in range(2)]
        hT = [acts(f"hT{j}", [P, 4, BLOCK], 48 + j) for j in range(2)]
        y_blk = [acts(f"y_blk{j}", [BLOCK, D], 8 + 4 * j) for j in range(2)]
        slot_wt = acts("slot_wt", [P, SLOTS // P, T], 72)
        y_rows = acts("y_rows", [P, SLOTS // P, D], 20)
        gain_row = acts("gain_row", [P, D], 76)
        NE = N_GROUPS + N_EXPERTS
        lg = keep("lg", [P, NT, NE])
        g8 = keep("g8", [P, NT, 8])
        gm8 = keep("gm8", [P, NT, 8])
        gi8 = keep("gi8", [P, NT, 8], U32)
        gneg = keep("gneg", [P, NT])
        gex = keep("gex", [P, NT, N_GROUPS])
        gsum = keep("gsum", [P, NT])
        gid = keep("gid", [P, NT])
        emask = keep("emask", [P, NT, N_EXPERTS], U32)
        em = keep("em", [P, NT, N_EXPERTS])
        ev8 = keep("ev8", [P, NT, 8])
        ei8 = keep("ei8", [P, NT, 8], U32)
        eneg = keep("eneg", [P, NT])
        e21 = keep("e21", [P, NT])
        wt = keep("wt", [P, 2, NT])
        eid = keep("eid", [P, NT, 2])
        chosen = keep("chosen", [P, 2, NT, N_EXPERTS])
        assigned = keep("assigned", [P, NT, N_EXPERTS])
        counts = keep("counts", [P, N_EXPERTS])
        starts = keep("starts", [P, N_EXPERTS])
        slot_of = keep("slot_of", [P, NT, N_EXPERTS])
        slot = keep("slot", [P, 2, NT])
        most = keep("most", [P, 1])
        starts_i = keep("starts_i", [1, N_EXPERTS], I32)
        most_i = keep("most_i", [1, 1], I32)

        y_sorted = nc.dram_tensor("y_sorted", (SLOTS_PAD, D), F32, kind="Internal").ap()

        QK = N_QK * DH
        sga = acts("sga", [P, KD, T], 0)
        qaT = acts("qaT", [P, NA_HEADS // 2, T], 8)
        kaT = acts("kaT", [P, NA_HEADS // 2, T], 12)
        va = acts("va", [P, NT, NA_HEADS * DH], 16)
        qk = acts("qk", [P, NT, QK], 20)
        vb = acts("vb", [P, NT, KV_HEADS * DH], 25)
        qk_sq = acts("qk_sq", [P, NT, QK], 26)
        qk_rot = acts("qk_rot", [P, NT, QK], 31)
        yaT = acts("yaT", [P, NA_HEADS // 2, T], 26)
        ybT = acts("ybT", [P, GQA_HEADS // 2, T], 30)
        qbT = acts("qbT", [P, GQA_HEADS // 2, T], 36)
        kk = acts("kk", [P, NT, KV_HEADS, 2, DH], 40)
        kbT = acts("kbT", [P, KV_HEADS, T], 42)
        sgb = acts("sgb", [P, KD, T], 44)
        rel_bias = acts("rel_bias", [P, NT, NA_HEADS, T], 52)
        prob_a = acts("prob_a", [P, NT, T], 68)
        prob_b = acts("prob_b", [P, NT, T], 70)
        prob_aT = acts("prob_aT", [P, NT, T], 72)
        prob_bT = acts("prob_bT", [P, NT, T], 74)
        rpb_wide = nc.dram_tensor("rpb_wide", (GRID_W, NA_HEADS, RPB_ROWS, GRID_W), F32, kind="Internal").ap()
        cos_gain = acts("cos_gain", [P, 2, NT, DH], 76)
        sin_gain = acts("sin_gain", [P, 2, NT, DH], 77)
        qk_ss = keep("qk_ss", [P, NT * N_QK])
        qk_rs = keep("qk_rs", [P, NT * N_QK])
        top_a = keep("top_a", [P, NT])
        top_b = keep("top_b", [P, NT])
        sum_a = keep("sum_a", [P, NT])
        sum_b = keep("sum_b", [P, NT])

        qT = acts("qT", [P, HP, T], 16)
        keysT = acts("keysT", [P, HP, NKEYS], 52)
        sc = acts("sc", [P, NT, HP, NKEYS], 60)
        cand = acts("cand", [P, NT, PEER_HEADS, TOPK, TOPK], 32)
        ts = acts("ts", [P, NT, HP, TOPK], 48)
        ti = acts("ti", [P, NT, HP, TOPK], 50, U32)
        match = acts("match", [P, HK, TOPK], 16)
        tif = acts("tif", [P, NT, HP, TOPK], 24)
        bpos = acts("bpos", [P, NT, HK], 26, U32)
        bdig = acts("bdig", [P, 2, NT, HK], 27, U32)
        bdigf = acts("bdigf", [P, 2, NT, HK], 29)
        raw = [at(f"raw{s}", [P, CJ * KD * NKEYS], ARENA + 8192 * s) for s in range(RAW_SLOTS)]
        rest = [at(f"rest{s}", [P, CJ * KD * NKEYS], ARENA + 8192 * s, F32R) for s in range(RAW_SLOTS)]
        lead = [at(f"lead{b}", [P, CJ * KD * NKEYS], ARENA + 24576 + 8192 * b, F32R) for b in range(2)]
        WORK = ARENA + 40960
        best = at("best", [P, NT, HK], WORK)
        ij = at("ij", [P, 2, NT, HK], WORK + 1024)
        bestT = at("bestT", [P, T], WORK + 3072)
        ijT = at("ijT", [P, 2, T], WORK + 4096)
        hot = [at(f"hot{b}", [P, 2, GT, NKEYS], ARENA + 32768 + 4096 * b) for b in range(2)]
        hid_hi = [at(f"hid_hi{b}", [P, CJ, T], WORK + 2048 * b, F32R) for b in range(2)]
        hid_lo = [at(f"hid_lo{b}", [P, CJ, T], WORK + 4096 + 2048 * b, F32R) for b in range(2)]
        gain_f = at("gain_f", [P, D], NT_AT)
        A = at("A", [P, NKEYS, T], ARENA + 3 * 16384)
        nT_lo = at("nT_lo", [P, KD, T], NT_AT, F32R)
        nT_hi = at("nT_hi", [P, KD, T], DEAD_AT, F32R)
        assert DEAD_AT + 4 * KD * T <= place[0]
        best_sum = keep("best_sum", [P, NT * PEER_HEADS])
        cur_g = keep("cur_g", [P, 2, GT])
        assert place[0] <= ARENA

        bank = [ctx.enter_context(nc.psum_tensor(f"bank{i}", [P, 512], F32)) for i in range(8)]

        def sem(name):
            return ctx.enter_context(nc.semaphore(name))

        x_in = sem("x_in")
        const_in = sem("const_in")
        rows_in = sem("rows_in")
        wr_in = sem("wr_in")
        ws_in = sem("ws_in")
        ring_full = [sem(f"ring_full{s}") for s in range(RING)]
        h_ready = sem("h_ready")
        stat_sum = sem("stat_sum")
        stat_mean = sem("stat_mean")
        stat_root = sem("stat_root")
        xhat_ready = sem("xhat_ready")
        xhat_turned = sem("xhat_turned")
        nT_act = sem("nT_act")
        nT_dve = sem("nT_dve")
        dve_step = sem("dve_step")
        act_step = sem("act_step")
        lb_diff = sem("lb_diff")
        lb_sig = sem("lb_sig")
        proj_done = sem("proj_done")
        proj_act = sem("proj_act")
        proj_dve = sem("proj_dve")
        f_ready = sem("f_ready")
        lf_ready = sem("lf_ready")
        d_ready = sem("d_ready")
        exp_ready = sem("exp_ready")
        qk_zero = sem("qk_zero")
        qk_ready = sem("qk_ready")
        sc_done = sem("sc_done")
        sc_masked = sem("sc_masked")
        kl_turned = sem("kl_turned")
        kl_ready = sem("kl_ready")
        state_done = sem("state_done")
        state_ready = sem("state_ready")
        o_done = sem("o_done")
        o_sq = sem("o_sq")
        o_ms = sem("o_ms")
        o_sd = sem("o_sd")
        on_ready = sem("on_ready")
        on_turned = sem("on_turned")
        v_ms = sem("v_ms")
        v_sd = sem("v_sd")
        vh_ready = sem("vh_ready")
        ws_masked = sem("ws_masked")
        mixed_done = sem("mixed_done")
        mix_g = sem("mix_g")
        mix_h = sem("mix_h")
        out1_done = sem("out1_done")
        stored = sem("stored")

        gain_in = sem("gain_in")
        xs_zero = sem("xs_zero")
        router_done = sem("router_done")
        gneg_ready = sem("gneg_ready")
        gsum_ready = sem("gsum_ready")
        eneg_ready = sem("eneg_ready")
        e21_ready = sem("e21_ready")
        assign_ready = sem("assign_ready")
        rank_done = sem("rank_done")
        starts_ready = sem("starts_ready")
        pick_ready = sem("pick_ready")
        gather_done = sem("gather_done")
        xs_act = sem("xs_act")
        xs_dve = sem("xs_dve")
        wt_turned = sem("wt_turned")
        slot_wt_ready = sem("slot_wt_ready")
        w_lead_ready = sem("w_lead_ready")
        w_rest_ready = sem("w_rest_ready")
        w_lead_used = sem("w_lead_used")
        w_used = sem("w_used")
        gate_low = sem("gate_low")
        up_low = sem("up_low")
        gate_sum = sem("gate_sum")
        up_sum = sem("up_sum")
        down_done = sem("down_done")
        x_ready = sem("x_ready")
        x_hi_ready = sem("x_hi_ready")
        x_lo_ready = sem("x_lo_ready")
        sil_ready = sem("sil_ready")
        hid_ready = sem("hid_ready")
        hid_turned = sem("hid_turned")
        hT_ready = sem("hT_ready")
        y_act = sem("y_act")
        y_dve = sem("y_dve")
        y_stored = sem("y_stored")
        many_gate = sem("many_gate")
        many_up = sem("many_up")
        many_down = sem("many_down")
        many_stored = sem("many_stored")
        y_rows_in = sem("y_rows_in")
        moe_done = sem("moe_done")

        rpb_spread = sem("rpb_spread")
        bias_in = sem("bias_in")
        bias_ready = sem("bias_ready")
        p2_done = sem("p2_done")
        p2_act = sem("p2_act")
        p2_dve = sem("p2_dve")
        qk_ms = sem("qk_ms")
        qk_sd = sem("qk_sd")
        qk_roped = sem("qk_roped")
        qk_turned = sem("qk_turned")
        qbT_ready = sem("qbT_ready")
        kbT_ready = sem("kbT_ready")
        gate2_done = sem("gate2_done")
        gate2_act = sem("gate2_act")
        sg_ready = sem("sg_ready")
        sa_done = sem("sa_done")
        ta_ready = sem("ta_ready")
        ea_ready = sem("ea_ready")
        pa_ready = sem("pa_ready")
        pa_turned = sem("pa_turned")
        paT_ready = sem("paT_ready")
        ya_done = sem("ya_done")
        ya_ready = sem("ya_ready")
        sb_done = sem("sb_done")
        tb_ready = sem("tb_ready")
        eb_ready = sem("eb_ready")
        pb_ready = sem("pb_ready")
        pb_turned = sem("pb_turned")
        pbT_ready = sem("pbT_ready")
        yb_done = sem("yb_done")
        yb_ready = sem("yb_ready")
        branch_done = sem("branch_done")
        merged_ready = sem("merged_ready")
        out2_done = sem("out2_done")

        keys_in = sem("keys_in")
        query_done = sem("query_done")
        query_act = sem("query_act")
        query_dve = sem("query_dve")
        score_done = sem("score_done")
        score_ready = sem("score_ready")
        routed = sem("routed")
        best_exp = sem("best_exp")
        gates_ready = sem("gates_ready")
        route_turned = sem("route_turned")
        route_ready = sem("route_ready")
        raw_full = [sem(f"raw_full{s}") for s in range(RAW_SLOTS)]
        chunk_used = sem("chunk_used")
        act_ready = sem("act_ready")
        nT_masked = sem("nT_masked")
        nT_split = sem("nT_split")
        lead_ready = sem("lead_ready")
        rest_ready = sem("rest_ready")
        hid_hi_ready = sem("hid_hi_ready")
        hid_lo_ready = sem("hid_lo_ready")
        hot_ready = sem("hot_ready")
        cur_ready = sem("cur_ready")
        hot_j_ready = sem("hot_j_ready")
        gates_done = sem("gates_done")
        gated = sem("gated")
        gain_f_in = sem("gain_f_in")
        out_ready = sem("out_ready")

        def chain(eng, s):
            n = [0]

            def link(ins):
                n[0] += 1
                ins.then_inc(s, 1)
                eng.wait_ge(s, n[0])

            return link

        def ring_wait(pe, n):
            pe.wait_ge(ring_full[n % RING], 16 * (n // RING + 1))

        def chunk_read(n):
            if n < CH_OUT1:
                return proj_done, 2 * (n + 1)
            if n < CH_MOE:
                return out1_done, 2 * (n - CH_OUT1 + 1)
            if n < CH_IN2:
                pair, i = divmod(n - CH_MOE, RING)
                j, kind = PAIR[i]
                if kind == 2:
                    return down_done, 2 * (2 * pair + j + 1)
                return w_used, 2 * (2 * pair + j) + kind + 1
            if n < CH_PROJ:
                i = n - CH_IN2
                return (p2_done, (2, 3, 5, 7, 9)[i]) if i < 5 else (gate2_done, 2 * (i - 4))
            if n < CH_OUT2:
                return branch_done, 7 + n - CH_PROJ
            if n < CH_WQ:
                return out2_done, 2 * (n - CH_OUT2 + 1)
            return query_done, 2 * (n - CH_WQ + 1)

        def quad(t):
            return t[:, :].rearrange("p (m n) -> p m n", m=4)

        def spread(ap, shape):
            return ap.broadcast_to(shape)

        H_COUNT = [0, 4, 8, 10, 14, 18]

        def act_stats(act, n):
            if n == 0:
                act.wait_ge(x_in, 16)
            else:
                act.wait_ge(h_ready, H_COUNT[n])
            for t in range(NT):
                act.activation(xhat[:, t, :], h[:, t, :], ACT.Square,
                               accum_out=stat_ss[:, t:t + 1]).then_inc(stat_sum, 1)
            act.wait_ge(stat_mean, n + 1)
            act.activation(stat_sd[:, :], stat_ms[:, :], ACT.Sqrt).then_inc(stat_root, 1)

        def dve_stats(dve, link, n):
            dve.wait_ge(stat_sum, NT * (n + 1))
            dve.tensor_scalar(stat_ms[:, :], stat_ss[:, :], 1.0 / D, EPS, ALU.mult, ALU.add).then_inc(stat_mean, 1)
            dve.wait_ge(stat_root, n + 1)
            link(dve.reciprocal(stat_rs[:, :], stat_sd[:, :]))

        def dve_xhat(dve):
            for t in range(NT):
                dve.tensor_scalar(xhat[:, t, :], h[:, t, :], stat_rs[:, t:t + 1], None,
                                  ALU.mult).then_inc(xhat_ready, 1)

        def pe_turn(pe, m):
            pe.wait_ge(xhat_ready, NT * (m + 1))
            for b in range(4):
                for k in (2 * b, 2 * b + 1):
                    for t in range(NT):
                        last = pe.transpose(bank[b][:, (k % 2) * T + t * P:(k % 2) * T + (t + 1) * P],
                                            xhat[:, t, k * P:(k + 1) * P], ident)
                last.then_inc(xhat_turned, 1)

        def act_nT(act, m, gain):
            for b in (0, 2):
                act.wait_ge(xhat_turned, 4 * m + b + 1)
                for k in (2 * b, 2 * b + 1):
                    last = act.activation(nT[:, k, :], bank[b][:, (k % 2) * T:(k % 2 + 1) * T], ACT.Copy,
                                          scale=pr(gain, k))
                last.then_inc(nT_act, 1)

        def dve_nT(dve, m, gain):
            for b in (1, 3):
                dve.wait_ge(xhat_turned, 4 * m + b + 1)
                for k in (2 * b, 2 * b + 1):
                    last = dve.tensor_scalar(nT[:, k, :], bank[b][:, (k % 2) * T:(k % 2 + 1) * T], pr(gain, k),
                                             None, ALU.mult)
                last.then_inc(nT_dve, 1)

        def wait_nT(eng, m):
            eng.wait_ge(nT_act, 2 * (m + 1))
            eng.wait_ge(nT_dve, 2 * (m + 1))

        def pe_columns(pe, dst, s, m):
            for k in range(KD):
                last = pe.matmul(dst, ring8(s)[:, k, m * P:(m + 1) * P], nT[:, k, :],
                                 start=(k == 0), stop=(k == KD - 1))
            return last

        def pe_rows(pe, dst, s, t, width=512):
            w = ring[s][:, 0:KD * width].rearrange("p (k f) -> p k f", k=KD)
            for k in range(KD):
                last = pe.matmul(dst, nT[:, k, t * P:(t + 1) * P], w[:, k, :],
                                 start=(k == 0), stop=(k == KD - 1))
            return last

        def pair_fill(pair, i):
            return 16 * (pair + (CH_MOE + i) // RING + 1)

        W_SLOT = [(CH_MOE + i) % RING for i in range(RING)]
        GATHER_BANK = [0, 1, 2, 3, 6, 7, 0, 1]

        IN1_BANK = [4, 5, 6, 7, 0, 1, 2, 3, 4, 5, 6, 7]
        OUT1_BANK = [5, 6, 7, 0]

        QUERY_BANK = [4, 5, 6, 7, 0, 1, 2, 3]
        def fill(i, at_n):
            return 16 * (at_n // RAW_SLOTS + 1) + 16 * (UNROLL // RAW_SLOTS) * i

        BRANCH_BANK = [(0, 1, 2, 3), (5, 6, 7, 4)]

        block = ctx.enter_context(nc.Block())

        @block.sync
        def _(sp):
            def load(n, src, cols=CHUNK_COLS, k=8):
                if n >= RING:
                    sp.wait_ge(*chunk_read(n - RING))
                dst = ring[n % RING][:, 0:cols].rearrange("p (k f) -> p k f", k=k)
                sp.dma_start(dst, src).then_inc(ring_full[n % RING], 16)

            sp.dma_start(h[:, :, :], dram["x"].rearrange("(t p) d -> p t d", p=P)).then_inc(x_in, 16)
            sp.dma_start(const[:, :], dram["const"]).then_inc(const_in, 16)
            sp.dma_start(param[:, :], dram["param"]).then_inc(const_in, 16)
            w_in = dram["w_in"]
            for n in range(2):
                f = IN1_ORDER[n] * 512
                load(n, w_in[:, f:f + 512].rearrange("(k p) f -> p k f", p=P))
            sp.dma_start(rows[:, :], dram["rows"].broadcast_to([P, ROW_N])).then_inc(rows_in, 16)
            sp.dma_start(w_sT[:, :, :], dram["w_sT"].rearrange("j (g i) -> j g i", g=HEADS)).then_inc(ws_in, 16)
            sp.dma_start(w_router[:, :, 0:N_GROUPS],
                         dram["w_group_router"].rearrange("(k p) f -> p k f", p=P)).then_inc(wr_in, 16)
            sp.dma_start(w_router[:, :, N_GROUPS:],
                         dram["w_expert_router"].rearrange("(k p) f -> p k f", p=P)).then_inc(wr_in, 16)
            for n in range(2, 6):
                f = IN1_ORDER[n] * 512
                load(n, w_in[:, f:f + 512].rearrange("(k p) f -> p k f", p=P))
            for n in range(2):
                load(CH_OUT1 + n, dram["w_out"][:, n * 512:n * 512 + 512].rearrange("(k p) f -> p k f", p=P))
            rpb = dram["rpb"]
            for i in range(RPB_ROWS):
                first = (RPB_H // 2 - (KROWS - 1) + i) * RPB_W + RPB_W // 2
                src = bass.AP(rpb.tensor, first, [[RPB_H * RPB_W, NA_HEADS], [-1, GRID_W], [1, GRID_W]])
                sp.dma_start(rpb_wide[:, :, i, :].rearrange("c a d -> a c d"), src).then_inc(rpb_spread, 16)
            sp.wait_ge(h_ready, 4)
            sp.dma_start(gain_row[:, :], dram["final_gain"].broadcast_to([P, D])).then_inc(gain_in, 16)

            def expert_source(i, pair):
                j, kind = PAIR[i]
                e = 2 * pair + j
                if kind == 2:
                    return dram["w_down"][bass.ds(e, 1)].rearrange("e (k p) f -> p (e k) f", p=P), 4
                w = dram["w_gate"] if kind == 0 else dram["w_up"]
                return w[bass.ds(e, 1)].rearrange("e (k p) f -> p (e k) f", p=P), 8

            for i in range(RING):
                src, k = expert_source(i, 0)
                load(CH_MOE + i, src, k=k)
            with sp.Fori(1, PAIRS) as pair:
                for i, (j, kind) in enumerate(PAIR):
                    s = (CH_MOE + i) % RING
                    if kind == 2:
                        sp.wait_ge(down_done, 4 * pair + 2 * j - 2)
                    else:
                        sp.wait_ge(w_used, 4 * pair + 2 * j + kind - 3)
                    src, k = expert_source(i, pair)
                    dst = ring[s][:, :].rearrange("p (k f) -> p k f", k=k)
                    sp.dma_start(dst, src).then_inc(ring_full[s], 16)
            for i, (first, width) in enumerate(IN2_COLS):
                if i == 2:
                    sp.wait_ge(y_rows_in, 16)
                load(CH_IN2 + i, dram["w_in_2"][:, first:first + width].rearrange("(k p) f -> p k f", p=P), KD * width)
                if i == RING - 1:
                    sp.wait_ge(w_used, 2 * N_EXPERTS)
                    sp.wait_ge(rpb_spread, 16 * RPB_ROWS)
                    for r in range(KROWS):
                        t, lo = r // 2, (r % 2) * GRID_W
                        first = KROWS - 1 - r
                        sp.dma_start(rel_bias[lo:lo + GRID_W, t, :, :],
                                     rpb_wide[:, :, first:first + KROWS, :].rearrange("c a k d -> c a (k d)")).then_inc(bias_in, 16)
            for i, name in enumerate(("w_proj_a", "w_proj_b")):
                load(CH_PROJ + i, dram[name].rearrange("(k p) f -> p k f", p=P), k=4)
            for i in range(2):
                load(CH_OUT2 + i, dram["w_out_2"][:, i * 512:i * 512 + 512].rearrange("(k p) f -> p k f", p=P))
            for i in range(4):
                load(CH_WQ + i, dram["w_q"][:, i * 512:i * 512 + 512].rearrange("(k p) f -> p k f", p=P))
            sp.wait_ge(h_ready, H_COUNT[4])
            sp.dma_start(keysT[:, :, :], dram["keysT"].rearrange("c (a n) -> c a n", n=NKEYS)).then_inc(keys_in, 16)

            def stream(slot, table, chunk):
                sp.dma_start(raw[slot][:, :], dram[table][bass.ds(chunk, 1)].rearrange("e p f -> p (e f)")).then_inc(raw_full[slot], 16)

            sp.wait_ge(*chunk_read(CH_END - 1))
            for n in range(RAW_SLOTS):
                stream(n, "u", n)

            def stream_next(n, slot, table):
                sp.wait_ge(chunk_used, n - RAW_SLOTS + 1)
                stream(slot, table, n if table == "u" else n - PEER_CHUNKS)

            turns = PEER_CHUNKS // RAW_SLOTS
            with sp.Fori(1, turns) as i:
                for slot in range(RAW_SLOTS):
                    stream_next(i * RAW_SLOTS + slot, slot, "u")
            for n in range(turns * RAW_SLOTS, (turns + 1) * RAW_SLOTS):
                stream_next(n, n % RAW_SLOTS, "u" if n < PEER_CHUNKS else "v")
            with sp.Fori(turns + 1, 2 * PEER_CHUNKS // RAW_SLOTS) as i:
                for slot in range(RAW_SLOTS):
                    stream_next(i * RAW_SLOTS + slot, slot, "v")
            for n in range(2 * PEER_CHUNKS // RAW_SLOTS * RAW_SLOTS, 2 * PEER_CHUNKS):
                stream_next(n, n % RAW_SLOTS, "v")
            sp.dma_start(gain_f[:, :], dram["norm_f_g"].broadcast_to([P, D])).then_inc(gain_f_in, 16)
            for t in range(NT):
                sp.wait_ge(out_ready, t + 1)
                sp.dma_start(out[t * P:(t + 1) * P, :], h[:, t, :]).then_inc(stored, 16)
            sp.wait_ge(stored, 16 * NT)

        @block.gpsimd
        def _(pool):
            pool.memset(hQE[:, :, :], 0.0).then_inc(qk_zero, 1)
            pool.memset(hQO[:, :, :], 0.0).then_inc(qk_zero, 1)
            pool.memset(hSC[:, :, :, :], 0.0).then_inc(qk_zero, 1)
            pool.wait_ge(ws_in, 16)
            pool.wait_ge(qk_zero, 3)
            pool.memset(w_sT[CHUNK:P, :, 0:CHUNK], 0.0).then_inc(ws_masked, 1)
            pool.wait_ge(h_ready, 4)
            pool.memset(xs[:, :, SLOTS:], 0.0).then_inc(xs_zero, 1)
            pool.wait_ge(xs_act, KD // 2)
            pool.wait_ge(xs_dve, KD // 2)
            pool.wait_ge(xs_zero, 1)
            pool.wait_ge(starts_ready, 1)
            load_most = pool.value_load(most_i[0:1, 0:1], min_val=0, max_val=T)
            with pool.If(load_most > BLOCK):
                def many_copies(e, peeled):
                    first = pool.value_load(starts_i[0:1, bass.ds(e, 1)], min_val=0, max_val=SLOTS)
                    for b in range(BLOCKS_MAX):
                        if b or not peeled:
                            pool.wait_ge(many_up, e * BLOCKS_MAX + b)
                        pool.tensor_copy(x_blk[0][:, :, :], xs[:, :, bass.ds(first + b * BLOCK, BLOCK)]).then_inc(x_ready, 1)

                many_copies(0, True)
                with pool.Fori(1, N_EXPERTS) as e:
                    many_copies(e, False)
            with pool.Else():
                def expert_input(e, j, peeled):
                    first = pool.value_load(starts_i[0:1, bass.ds(e, 1)], min_val=0, max_val=SLOTS)
                    pool.tensor_copy(x_blk[j][:, :, :], xs[:, :, bass.ds(first, BLOCK)]).then_inc(x_ready, 1)
                    if not peeled:
                        pool.wait_ge(w_used, 2 * e - 2)
                    pool.wait_ge(x_hi_ready, e + 1)
                    pool.tensor_tensor(x_two[j][:, :, BLOCK:], x_blk[j][:, :, :], x_two[j][:, :, 0:BLOCK].bitcast(F32),
                                       ALU.subtract).then_inc(x_lo_ready, 1)

                for j in range(2):
                    expert_input(j, j, True)
                with pool.Fori(1, PAIRS) as pair:
                    for j in range(2):
                        expert_input(2 * pair + j, j, False)
            pool.wait_ge(bias_in, 16 * KROWS)
            pool.wait_ge(const_in, 32)
            for t in range(NT):
                view = rel_bias[:, t, :, :].rearrange("p a (k c) -> p (a k) c", k=KROWS)
                pool.tensor_tensor(view, view, spread(c("window").unsqueeze(1), [P, NA_HEADS * KROWS, GRID_W]),
                                   ALU.add).then_inc(bias_ready, 1)
            pool.wait_ge(route_ready, 1)

            def weigh_hot(g, b):
                pool.tensor_copy(cur_g[:, b, :], bestT[:, bass.ds(g * GT, GT)]).then_inc(cur_ready, 1)
                pool.wait_ge(cur_ready, g + 1)
                pool.wait_ge(hot_ready, g + 1)
                pool.tensor_tensor(hot[b][:, 1, :, :], hot[b][:, 1, :, :],
                                   spread(cur_g[:, b, :].unsqueeze(2), [P, GT, NKEYS]), ALU.mult).then_inc(hot_j_ready, 1)

            with pool.Fori(0, GROUPS // 2) as g2:
                for b in range(2):
                    weigh_hot(2 * g2 + b, b)

        @block.scalar
        def _(act):
            link = chain(act, act_step)
            act_stats(act, 0)
            act.wait_ge(lb_diff, 1)
            act.activation(lb[:, :], lbd[:, :], ACT.Sigmoid).then_inc(lb_sig, 1)
            act.wait_ge(const_in, 32)
            act_nT(act, 0, "gain1")
            for use, dst in enumerate((hF, hF, hQ, hQ, hG, hG)):
                act.wait_ge(proj_done, use + 1)
                half = use % 2
                act.activation(dst[:, 2 * half:2 * half + 2, :].rearrange("p a t -> p (a t)"),
                               bank[IN1_BANK[use]][:, :], ACT.Sigmoid).then_inc(proj_act, 1)
            for t in range(NT):
                act.wait_ge(proj_done, 7 + t)
                act.activation(hI[:, t, :], bank[IN1_BANK[6 + t]][:, :], ACT.Copy).then_inc(proj_act, 1)
            act.wait_ge(f_ready, 1)
            act.activation(hF[:, :, :], hF[:, :, :], ACT.Ln).then_inc(lf_ready, 1)
            act.wait_ge(d_ready, 1)
            act.activation(hF[:, :, :], hD1[:, :, :], ACT.Exp).then_inc(exp_ready, 1)
            act.activation(hD1[:, :, :], hD1[:, :, :], ACT.Exp, scale=-1.0).then_inc(exp_ready, 1)
            act.wait_ge(d_ready, 2)
            act.activation(hD2[:, :, :], hD2[:, :, :], ACT.Exp).then_inc(exp_ready, 1)
            act.activation(hEB[:, :, :], hB[:, :, :], ACT.Exp).then_inc(exp_ready, 1)
            for t in range(NT):
                act.wait_ge(proj_done, 9 + t)
                act.activation(mV[:, t, :], bank[IN1_BANK[8 + t]][:, :], ACT.Gelu).then_inc(proj_act, 1)
            for half in range(2):
                act.wait_ge(proj_done, 11 + half)
                act.activation(mU[:, 2 * half:2 * half + 2, :].rearrange("p a t -> p (a t)"),
                               bank[IN1_BANK[10 + half]][:, :], ACT.Gelu).then_inc(proj_act, 1)
            for t in range(NT):
                act.wait_ge(kl_turned, t + 1)
                act.activation(hKL[:, t, :, :], quad(bank[2 + t]), ACT.Copy).then_inc(kl_ready, 1)
            act.wait_ge(v_ms, 1)
            act.activation(vrs[:, :], vss[:, :], ACT.Sqrt).then_inc(v_sd, 1)
            act.wait_ge(vh_ready, 1)
            for t in range(NT):
                act.wait_ge(o_done, t + 1)
                act.activation(mSQ[:, t, :], bank[t][:, :], ACT.Square).then_inc(o_sq, 1)
            act.wait_ge(o_ms, 1)
            act.activation(ors[:, :], oss[:, :], ACT.Sqrt).then_inc(o_sd, 1)
            act_stats(act, 1)
            act_nT(act, 1, "gain2")
            act.wait_ge(gneg_ready, 1)
            for t in range(NT):
                act.activation(gex[:, t, :], lg[:, t, 0:N_GROUPS], ACT.Exp, bias=gneg[:, t:t + 1],
                               accum_out=gsum[:, t:t + 1]).then_inc(gsum_ready, 1)
            act.wait_ge(eneg_ready, 1)
            for t in range(NT):
                act.activation(e21[:, t:t + 1], ev8[:, t, 1:2], ACT.Exp,
                               bias=eneg[:, t:t + 1]).then_inc(e21_ready, 1)
            for k in range(0, KD, 2):
                act.wait_ge(gather_done, k + 1)
                act.activation(xs[:, k, 0:SLOTS], bank[GATHER_BANK[k]][:, :], ACT.Copy,
                               scale=pr("gain2", k)).then_inc(xs_act, 1)
            for half in range(2):
                act.wait_ge(wt_turned, half + 1)
                act.activation(slot_wt[:, 2 * half:2 * half + 2, :].rearrange("p s t -> p (s t)"),
                               bank[4 + half][:, :], ACT.Copy).then_inc(slot_wt_ready, 1)
            act.wait_ge(starts_ready, 1)
            load_most = act.value_load(most_i[0:1, 0:1], min_val=0, max_val=T)
            with act.If(load_most > BLOCK):
                def many_scalar(e, peeled):
                    first = act.value_load(starts_i[0:1, bass.ds(e, 1)], min_val=0, max_val=SLOTS)
                    for b in range(BLOCKS_MAX):
                        n = e * BLOCKS_MAX + b
                        act.wait_ge(many_gate, n + 1)
                        act.activation(hid[0][:, :], bank[0][0:BLOCK, :], ACT.Silu).then_inc(sil_ready, 1)
                        act.wait_ge(hid_turned, n + 1)
                        act.activation(hT[0][:, :, :].rearrange("p f s -> p (f s)"), bank[4][:, 0:4 * BLOCK],
                                       ACT.Copy).then_inc(hT_ready, 1)
                        act.wait_ge(many_down, 2 * n + 1)
                        if b or not peeled:
                            act.wait_ge(many_stored, 16 * n)
                        act.activation(y_blk[0][:, 0:512], bank[6][0:BLOCK, :], ACT.Copy).then_inc(y_act, 1)
                        act.wait_ge(y_act, n + 1)
                        act.wait_ge(y_dve, n + 1)
                        act.dma_start(y_sorted[bass.ds(first + b * BLOCK, BLOCK)], y_blk[0][:, :]).then_inc(many_stored, 16)

                many_scalar(0, True)
                with act.Fori(1, N_EXPERTS) as e:
                    many_scalar(e, False)
                act.wait_ge(many_stored, 16 * N_EXPERTS * BLOCKS_MAX)
                act.nop().then_inc(y_stored, 16 * N_EXPERTS)
            with act.Else():
                def split_lead(e, pair, j, kind, peeled):
                    slot = W_SLOT[3 * j + kind]
                    act.wait_ge(ring_full[slot], pair_fill(pair, 3 * j + kind))
                    for half in range(2):
                        n = 4 * e + 2 * kind + half
                        if kind or not peeled:
                            act.wait_ge(w_lead_used, n - 1)
                            act.wait_ge(w_rest_ready, n - 1)
                        act.activation(w_lead[half][:, :, :], ring8(slot)[:, 4 * half:4 * half + 4, :],
                                       ACT.Copy).then_inc(w_lead_ready, 1)

                def low(e, j, kind):
                    act.wait_ge(w_used, 2 * e + kind + 1)
                    act.activation((hid, upv)[kind][j][:, :], bank[2 * kind + j][BLOCK:P, :],
                                   ACT.Copy).then_inc((gate_low, up_low)[kind], 1)

                def silu(e, j):
                    act.wait_ge(gate_sum, e + 1)
                    act.activation(hid[j][:, :], hid[j][:, :], ACT.Silu).then_inc(sil_ready, 1)

                def turned(e, j):
                    act.wait_ge(hid_turned, e + 1)
                    act.activation(hT[j][:, :, :].rearrange("p f s -> p (f s)"), bank[4 + j][:, 0:4 * BLOCK],
                                   ACT.Copy).then_inc(hT_ready, 1)

                def copy_store(e, pair, j, peeled):
                    act.wait_ge(down_done, 2 * e + 1)
                    if not peeled:
                        act.wait_ge(y_stored, 16 * e - 16)
                    act.activation(y_blk[j][:, 0:512], bank[6][0:BLOCK, :], ACT.Copy).then_inc(y_act, 1)
                    first = act.value_load(starts_i[0:1, bass.ds(e, 1)], min_val=0, max_val=SLOTS)
                    act.wait_ge(y_act, e + 1)
                    act.wait_ge(y_dve, e + 1)
                    if j or not peeled:
                        act.wait_ge(y_stored, 16 * e)
                    act.dma_start(y_sorted[bass.ds(first, BLOCK)], y_blk[j][:, :]).then_inc(y_stored, 16)

                def expert_scalar(e, pair, j, peeled, former_peeled):
                    act.wait_ge(x_ready, e + 1)
                    act.activation(x_two[j][:, :, 0:BLOCK], x_blk[j][:, :, :], ACT.Copy).then_inc(x_hi_ready, 1)
                    split_lead(e, pair, j, 0, peeled and j == 0)
                    if not peeled:
                        copy_store(e - 2, pair - 1, j, former_peeled)
                    split_lead(e, pair, j, 1, False)
                    if j or not peeled:
                        turned(e - 1, 1 - j)
                    low(e, j, 0)
                    silu(e, j)
                    low(e, j, 1)

                for j in range(2):
                    expert_scalar(j, 0, j, True, True)
                for j in range(2):
                    expert_scalar(2 + j, 1, j, False, True)
                with act.Fori(2, PAIRS) as pair:
                    for j in range(2):
                        expert_scalar(2 * pair + j, pair, j, False, False)
                copy_store(N_EXPERTS - 2, PAIRS - 1, 0, False)
                turned(N_EXPERTS - 1, 1)
                copy_store(N_EXPERTS - 1, PAIRS - 1, 1, False)
            act.wait_ge(y_stored, 16 * N_EXPERTS)
            act.dma_start(y_rows[:, :, :],
                          y_sorted[0:SLOTS].rearrange("(s p) d -> p s d", p=P)).then_inc(y_rows_in, 16)
            act_stats(act, 2)
            act_stats(act, 3)
            act_nT(act, 2, "gain12")
            for t in range(NT):
                act.wait_ge(p2_done, t + 1)
                act.activation(qk_sq[:, t, 0:512], bank[4 + t][:, :], ACT.Square)
                act.activation(qk[:, t, 0:512], bank[4 + t][:, :], ACT.Copy).then_inc(p2_act, 1)
            act.wait_ge(p2_done, 3)
            kv = bank[6][:, :].rearrange("p (t f) -> p t f", t=NT)
            act.activation(qk_sq[:, :, 512:], kv[:, :, 0:KV_HEADS * DH], ACT.Square)
            act.activation(qk[:, :, 512:], kv[:, :, 0:KV_HEADS * DH], ACT.Copy)
            act.activation(vb[:, :, :], kv[:, :, KV_HEADS * DH:], ACT.Copy).then_inc(p2_act, 1)
            act.wait_ge(qk_ms, 1)
            act.activation(qk_rs[:, :], qk_ss[:, :], ACT.Sqrt).then_inc(qk_sd, 1)
            for i in range(2):
                act.wait_ge(p2_done, 6 + i)
                act.activation(kaT[:, 2 * i:2 * i + 2, :].rearrange("p a t -> p (a t)"), bank[1 + i][:, :],
                               ACT.Copy).then_inc(p2_act, 1)
            for i in range(2):
                act.wait_ge(qk_turned, i + 1)
                act.activation(qbT[:, 2 * i:2 * i + 2, :].rearrange("p a t -> p (a t)"), bank[5 + i][:, :],
                               ACT.Copy).then_inc(qbT_ready, 1)
            for i in range(NA_HEADS):
                act.wait_ge(ta_ready, i + 1)
                for t in range(NT):
                    act.activation(prob_a[:, t, :], prob_a[:, t, :], ACT.Exp, bias=top_a[:, t:t + 1],
                                   accum_out=sum_a[:, t:t + 1]).then_inc(ea_ready, 1)
                act.wait_ge(tb_ready, i + 1)
                if i:
                    act.wait_ge(pb_turned, i)
                for t in range(NT):
                    act.activation(prob_b[:, t, :], bank[1][:, t * T:(t + 1) * T], ACT.Exp, bias=top_b[:, t:t + 1],
                                   scale=SCALE, accum_out=sum_b[:, t:t + 1]).then_inc(eb_ready, 1)
                act.wait_ge(gate2_done, i + 1)
                dst, half = (sga, i) if i < 4 else (sgb, i - 4)
                act.activation(dst[:, 2 * half:2 * half + 2, :].rearrange("p a t -> p (a t)"), bank[5 + i % 3][:, :],
                               ACT.Copy).then_inc(gate2_act, 1)
                act.wait_ge(pa_turned, i + 1)
                act.activation(prob_aT[:, :, :].rearrange("p k q -> p (k q)"), bank[2][:, :], ACT.Copy).then_inc(paT_ready, 1)
                part = slice((i % 2) * DH, (i % 2) * DH + DH)
                act.wait_ge(ya_done, i + 1)
                act.activation(yaT[part, i // 2, :], bank[4][0:DH, 0:T], ACT.Copy).then_inc(ya_ready, 1)
                act.wait_ge(yb_done, i + 1)
                act.activation(ybT[part, i // 2, :], bank[4][DH:P, 0:T], ACT.Copy).then_inc(yb_ready, 1)
            act.wait_ge(gate2_act, 8)
            for dst in (sga, sgb):
                act.activation(dst[:, :, :], dst[:, :, :], ACT.Sigmoid).then_inc(sg_ready, 1)
            act_stats(act, 4)
            act_nT(act, 3, "gain22")
            for use in range(0, 8, 2):
                act.wait_ge(query_done, use + 1)
                act.activation(qT[:, 2 * use:2 * use + 2, :].rearrange("p a t -> p (a t)"), bank[QUERY_BANK[use]][:, :],
                               ACT.Copy).then_inc(query_act, 1)
            for use in range(8):
                t, part = divmod(use, 4)
                act.wait_ge(score_done, use + 1)
                act.activation(sc[:, t, 4 * part:4 * part + 4, :].rearrange("p a n -> p (a n)"), bank[QUERY_BANK[use]][:, :],
                               ACT.Copy).then_inc(score_ready, 1)

            def act_columns(n):
                for b in range(2):
                    act.wait_ge(chunk_used, n + b + 1)
                    dst = A[:, bass.ds((n + b) * CJ, CJ), :].rearrange("p j t -> p (j t)")
                    act.activation(dst, bank[4 + b][:, :], ACT.Gelu).then_inc(act_ready, 1)

            with act.Fori(0, PLAIN // 2) as n2:
                act_columns(2 * n2)
            act.wait_ge(routed, 1)
            act.activation(best[:, :, :], best[:, :, :], ACT.Exp).then_inc(best_exp, 1)
            with act.Fori(PLAIN // 2, PEER_CHUNKS // 2) as n2:
                act_columns(2 * n2)
            act_stats(act, 5)

        @block.tensor
        def _(pe):
            pe.wait_ge(const_in, 32)
            pe_turn(pe, 0)
            wait_nT(pe, 0)
            for n, part in enumerate(IN1_ORDER):
                ring_wait(pe, n)
                for use in (2 * n, 2 * n + 1):
                    dst = bank[IN1_BANK[use]]
                    if use == 8:
                        pe.wait_ge(proj_act, 2)
                    if use == 10:
                        pe.wait_ge(proj_dve, 2)
                    if part in (4, 1):
                        last = pe_rows(pe, dst[:, :], n, use % 2)
                    else:
                        for m in range(2):
                            last = pe_columns(pe, dst[:, m * T:(m + 1) * T], n, 2 * (use % 2) + m)
                    last.then_inc(proj_done, 1)
            pe.wait_ge(proj_dve, 4)
            pe.wait_ge(qk_ready, 2)
            for t in range(NT):
                for hd in range(HEADS):
                    last = pe.matmul(bank[t][:, hd * P:(hd + 1) * P], hD1[:, hd, t * P:(t + 1) * P],
                                     hF[:, hd, t * P:(t + 1) * P], start=True, stop=True)
                last.then_inc(sc_done, 1)
            pe.wait_ge(qk_ready, 3)
            pe.wait_ge(proj_act, 8)
            for t in range(NT):
                for hd in range(HEADS):
                    last = pe.transpose(bank[2 + t][:, hd * P:(hd + 1) * P], hD2[:, hd, t * P:(t + 1) * P], ident)
                last.then_inc(kl_turned, 1)
            pe.wait_ge(proj_act, 12)
            for n in range(N_CHUNKS - 1):
                t, lo = n // 2, (n % 2) * CHUNK
                pe.wait_ge(kl_ready, t + 1)
                for hd in range(HEADS):
                    last = pe.matmul(bank[4 + n][:, hd * P:(hd + 1) * P], hKL[lo:lo + CHUNK, t, hd, :],
                                     hI[lo:lo + CHUNK, t, hd * P:(hd + 1) * P], start=True, stop=True)
                last.then_inc(state_done, 1)
            pe.wait_ge(ws_masked, 1)
            pe.wait_ge(vh_ready, 1)
            for pair in range(2):
                if pair:
                    pe.wait_ge(state_ready, 1)
                dst = bank[7 if pair == 0 else 4]
                for g in (2 * pair, 2 * pair + 1):
                    for t in range(NT):
                        o = (g % 2) * T + t * P
                        last = pe.matmul(dst[:, o:o + P], mV[:, t, g * P:(g + 1) * P], w_sT[:, g, :],
                                         start=True, stop=True)
                last.then_inc(mixed_done, 1)
            for t in range(NT):
                pe.wait_ge(sc_masked, t + 1)
                pe.wait_ge(qk_ready, 5)
                pe.wait_ge(state_ready, 1 if t == 0 else 3)
                for hd in range(HEADS):
                    dst = bank[t][:, hd * P:(hd + 1) * P]
                    tok = slice(t * P, (t + 1) * P)
                    pe.matmul(dst, hSC[:, t, hd, :], hI[:, t, hd * P:(hd + 1) * P], start=True, stop=False)
                    if t:
                        pe.matmul(dst, hQE[:, hd, tok], hS[:, 2 * t - 1, hd, :], start=False, stop=False)
                    last = pe.matmul(dst, hQO[:, hd, tok], hS[:, 2 * t, hd, :], start=False, stop=True)
                last.then_inc(o_done, 1)
            pe.wait_ge(on_ready, 1)
            for hd in range(HEADS):
                for t in range(NT):
                    o = (hd % 2) * T + t * P
                    last = pe.transpose(bank[2 + hd // 2][:, o:o + P], hON[:, t, hd * P:(hd + 1) * P], ident)
                if hd % 2:
                    last.then_inc(on_turned, 1)
            pe.wait_ge(mix_g, HEADS)
            pe.wait_ge(mix_h, HEADS)
            for half in range(2):
                n = CH_OUT1 + half
                ring_wait(pe, n)
                for t in range(NT):
                    for k in range(8):
                        last = pe.matmul(bank[OUT1_BANK[2 * half + t]][:, :], mixT[:, k, t * P:(t + 1) * P],
                                         ring8(n % RING)[:, k, :], start=(k == 0), stop=(k == 7))
                    last.then_inc(out1_done, 1)
            pe_turn(pe, 1)
            wait_nT(pe, 1)
            pe.wait_ge(wr_in, 32)
            for t in range(NT):
                for k in range(KD):
                    last = pe.matmul(bank[4][:, t * 64:t * 64 + NE], nT[:, k, t * P:(t + 1) * P], w_router[:, k, :],
                                     start=(k == 0), stop=(k == KD - 1))
            last.then_inc(router_done, 1)
            pe.wait_ge(assign_ready, 1)
            pe.matmul(bank[5][:, 0:32], c("before"), assigned[:, 0, :], start=True, stop=True)
            pe.matmul(bank[5][:, 32:64], c("before"), assigned[:, 1, :], start=True, stop=False)
            pe.matmul(bank[5][:, 32:64], c("ones"), assigned[:, 0, :], start=False, stop=True)
            pe.matmul(bank[5][:, 64:96], c("ones"), assigned[:, 0, :], start=True, stop=False)
            pe.matmul(bank[5][:, 64:96], c("ones"), assigned[:, 1, :], start=False, stop=True).then_inc(rank_done, 1)
            pe.wait_ge(pick_ready, NT)
            for k in range(KD):
                if k == 6:
                    pe.wait_ge(xs_act, 1)
                if k == 7:
                    pe.wait_ge(xs_dve, 1)
                for t in range(NT):
                    last = pe.matmul(bank[GATHER_BANK[k]][:, :], xhat[:, t, k * P:(k + 1) * P], pick_slot[:, t, :],
                                     start=(t == 0), stop=(t == NT - 1))
                last.then_inc(gather_done, 1)
            pe.wait_ge(pick_ready, 2 * NT)
            for s in range(SLOTS // P):
                for t in range(NT):
                    o = (s % 2) * T + t * P
                    last = pe.transpose(bank[4 + s // 2][:, o:o + P], pick_wt[:, t, s * P:(s + 1) * P], ident)
                if s % 2:
                    last.then_inc(wt_turned, 1)
            pe.wait_ge(starts_ready, 1)

            def expert_in(dst, w, block_in):
                for k in range(KD):
                    last = pe.matmul(dst[0:BLOCK, :], block_in[:, k, :], ring8(w)[:, k, :],
                                     start=(k == 0), stop=(k == KD - 1))
                return last

            def expert_turn(dst, hidden):
                for f in range(4):
                    last = pe.matmul(dst[:, f * BLOCK:(f + 1) * BLOCK], hidden[:, f * P:(f + 1) * P],
                                     ident[0:BLOCK, 0:BLOCK], start=True, stop=True)
                return last

            def expert_out(half, w, hidden_t):
                for f in range(4):
                    last = pe.matmul(bank[6 + half][0:BLOCK, :], hidden_t[:, f, :],
                                     ring4(w)[:, f, half * 512:(half + 1) * 512], start=(f == 0), stop=(f == 3))
                return last

            load_most = pe.value_load(most_i[0:1, 0:1], min_val=0, max_val=T)
            with pe.If(load_most > BLOCK):
                def many_products(pair, peeled):
                    for i in range(RING):
                        pe.wait_ge(ring_full[W_SLOT[i]], pair_fill(pair, i))
                    for j in range(2):
                        w_g, w_u, w_d = W_SLOT[3 * j:3 * j + 3]
                        for b in range(BLOCKS_MAX):
                            n = (2 * pair + j) * BLOCKS_MAX + b
                            pe.wait_ge(x_ready, n + 1)
                            expert_in(bank[0], w_g, x_blk[0]).then_inc(many_gate, 1)
                            expert_in(bank[2], w_u, x_blk[0]).then_inc(many_up, 1)
                            pe.wait_ge(hid_ready, n + 1)
                            expert_turn(bank[4], hid[0]).then_inc(hid_turned, 1)
                            pe.wait_ge(hT_ready, n + 1)
                            if b or j or not peeled:
                                pe.wait_ge(y_act, n)
                                pe.wait_ge(y_dve, n)
                            for half in range(2):
                                expert_out(half, w_d, hT[0]).then_inc(many_down, 1)
                    pe.wait_ge(many_down, 2 * (2 * pair + 2) * BLOCKS_MAX)
                    pe.nop().then_inc(w_used, 4)
                    pe.nop().then_inc(down_done, 4)

                many_products(0, True)
                with pe.Fori(1, PAIRS) as pair:
                    many_products(pair, False)
            with pe.Else():
                def product(e, j, kind, peeled):
                    if not peeled:
                        pe.wait_ge((gate_sum, up_sum)[kind], e - 1)
                    if kind == 0:
                        pe.wait_ge(x_lo_ready, e + 1)
                    for ready, used in ((w_lead_ready, w_lead_used), (w_rest_ready, w_used)):
                        for half in range(2):
                            pe.wait_ge(ready, 4 * e + 2 * kind + half + 1)
                            rows = slice(4 * half, 4 * half + 4)
                            part = w_lead[half] if ready is w_lead_ready else ring_rest8(W_SLOT[3 * j + kind])[:, rows, :]
                            for k in range(4):
                                last = pe.matmul(bank[2 * kind + j][:, :], x_two[j][:, 4 * half + k, :], part[:, k, :],
                                                 start=(ready is w_lead_ready and half == 0 and k == 0),
                                                 stop=(ready is w_rest_ready and half == 1 and k == 3))
                            if ready is w_lead_ready or half == 1:
                                last.then_inc(used, 1)

                def turn(e, j, peeled):
                    pe.wait_ge(hid_ready, e + 1)
                    if not peeled:
                        pe.wait_ge(hT_ready, e - 1)
                    expert_turn(bank[4 + j], hid[j]).then_inc(hid_turned, 1)

                def down(e, pair, j, first):
                    pe.wait_ge(ring_full[W_SLOT[3 * j + 2]], pair_fill(pair, 3 * j + 2))
                    pe.wait_ge(hT_ready, e + 1)
                    for half in range(2):
                        if not first:
                            pe.wait_ge((y_act, y_dve)[half], e)
                        expert_out(half, W_SLOT[3 * j + 2], hT[j]).then_inc(down_done, 1)

                for kind in range(2):
                    product(0, 0, kind, True)
                product(1, 1, 0, True)
                turn(0, 0, True)
                product(1, 1, 1, True)
                down(0, 0, 0, True)
                product(2, 0, 0, False)
                turn(1, 1, True)
                product(2, 0, 1, False)
                down(1, 0, 1, False)
                product(3, 1, 0, False)
                turn(2, 0, False)
                product(3, 1, 1, False)
                down(2, 1, 0, False)
                with pe.Fori(2, PAIRS) as pair:
                    for j in range(2):
                        e = 2 * pair + j
                        product(e, j, 0, False)
                        turn(e - 1, 1 - j, False)
                        product(e, j, 1, False)
                        down(e - 1, pair - 1 + j, 1 - j, False)
                turn(N_EXPERTS - 1, 1, False)
                down(N_EXPERTS - 1, PAIRS - 1, 1, False)
            pe.wait_ge(y_rows_in, 16)
            pe.wait_ge(slot_wt_ready, 2)
            for use in range(4):
                half, t = divmod(use, NT)
                for s in range(SLOTS // P):
                    last = pe.matmul(bank[use][:, :], slot_wt[:, s, t * P:(t + 1) * P],
                                     y_rows[:, s, half * 512:(half + 1) * 512],
                                     start=(s == 0), stop=(s == SLOTS // P - 1))
                last.then_inc(moe_done, 1)
            pe_turn(pe, 2)
            wait_nT(pe, 2)
            n = CH_IN2
            ring_wait(pe, n)
            for t in range(NT):
                pe_rows(pe, bank[4 + t][:, :], n % RING, t).then_inc(p2_done, 1)
            ring_wait(pe, n + 1)
            for t in range(NT):
                last = pe_rows(pe, bank[6][:, t * 256:(t + 1) * 256], (n + 1) % RING, t, 256)
            last.then_inc(p2_done, 1)
            for i, banks in ((2, (7, 0)), (3, (1, 2))):
                ring_wait(pe, n + i)
                for half in range(2):
                    for m in range(2):
                        last = pe_columns(pe, bank[banks[half]][:, m * T:(m + 1) * T], (n + i) % RING, 2 * half + m)
                    last.then_inc(p2_done, 1)
            ring_wait(pe, n + 4)
            for t in range(NT):
                if t:
                    pe.wait_ge(p2_act, 1)
                pe_rows(pe, bank[3 + t][:, :], (n + 4) % RING, t).then_inc(p2_done, 1)
            pe.wait_ge(qk_roped, 1)
            pe.wait_ge(p2_act, 3)
            for i in range(2):
                for a in (2 * i, 2 * i + 1):
                    for t in range(NT):
                        o = (a % 2) * T + t * P
                        last = pe.transpose(bank[5 + i][:, o:o + P], qk[:, t, a * P:(a + 1) * P], ident)
                last.then_inc(qk_turned, 1)
            pe.wait_ge(p2_dve, 1)
            for a in range(KV_HEADS):
                for t in range(NT):
                    last = pe.transpose(bank[7][:, a * T + t * P:a * T + (t + 1) * P],
                                        kk[:, t, a, :, :].rearrange("p r d -> p (r d)"), ident)
            last.then_inc(qk_turned, 1)

            def scores(dst, qT, kT, key_pair, i):
                part = slice((i % 2) * DH, (i % 2) * DH + DH)
                for t in range(NT):
                    last = pe.matmul(dst[:, t * T:(t + 1) * T], qT[part, i // 2, t * P:(t + 1) * P], kT[part, key_pair, :],
                                     start=True, stop=True)
                return last

            def turn_probs(dst, prob):
                for k in range(NT):
                    for t in range(NT):
                        last = pe.transpose(dst[:, k * T + t * P:k * T + (t + 1) * P], prob[:, t, k * P:(k + 1) * P], ident)
                return last

            def weigh(dst, v, first, prob_t):
                for k in range(NT):
                    last = pe.matmul(dst, v[:, k, first:first + DH], prob_t[:, k, :], start=(k == 0), stop=(k == NT - 1))
                return last

            def both_scores(i):
                scores(bank[0], qaT, kaT, i // 2, i).then_inc(sa_done, 1)
                scores(bank[1], qbT, kbT, i // 4, i).then_inc(sb_done, 1)

            pe.wait_ge(p2_act, 5)
            pe.wait_ge(p2_dve, 4)
            pe.wait_ge(qbT_ready, 2)
            pe.wait_ge(kbT_ready, 1)
            both_scores(0)
            for i in range(NA_HEADS):
                if i % 2 == 0:
                    ring_wait(pe, CH_IN2 + 5 + i // 2)
                if i >= 3:
                    pe.wait_ge(gate2_act, i - 2)
                for m in range(2):
                    last = pe_columns(pe, bank[5 + i % 3][:, m * T:(m + 1) * T], (CH_IN2 + 5 + i // 2) % RING, 2 * (i % 2) + m)
                last.then_inc(gate2_done, 1)
                pe.wait_ge(pa_ready, i + 1)
                turn_probs(bank[2], prob_a).then_inc(pa_turned, 1)
                pe.wait_ge(pb_ready, i + 1)
                turn_probs(bank[3], prob_b).then_inc(pb_turned, 1)
                if i + 1 < NA_HEADS:
                    both_scores(i + 1)
                pe.wait_ge(paT_ready, i + 1)
                if i:
                    pe.wait_ge(ya_ready, i)
                    pe.wait_ge(yb_ready, i)
                weigh(bank[4][0:DH, 0:T], va, i * DH, prob_aT).then_inc(ya_done, 1)
                pe.wait_ge(pbT_ready, i + 1)
                weigh(bank[4][DH:P, 0:T], vb, (i // 4) * DH, prob_bT).then_inc(yb_done, 1)
            pe.wait_ge(ya_ready, NA_HEADS)
            pe.wait_ge(yb_ready, GQA_HEADS)
            pe.wait_ge(gate2_act, 8)
            ring_wait(pe, CH_PROJ)
            ring_wait(pe, CH_PROJ + 1)
            for i in range(4):
                for b, y in enumerate((yaT, ybT)):
                    for m in range(2):
                        for k in range(4):
                            mt = 2 * i + m
                            last = pe.matmul(bank[BRANCH_BANK[b][i]][:, m * T:(m + 1) * T],
                                             ring4((CH_PROJ + b) % RING)[:, k, mt * P:(mt + 1) * P], y[:, k, :],
                                             start=(k == 0), stop=(k == 3))
                    last.then_inc(branch_done, 1)
            pe.wait_ge(merged_ready, 4)
            for half in range(2):
                ring_wait(pe, CH_OUT2 + half)
                for t in range(NT):
                    for k in range(KD):
                        last = pe.matmul(bank[2 * half + t][:, :], sga[:, k, t * P:(t + 1) * P],
                                         ring8((CH_OUT2 + half) % RING)[:, k, :], start=(k == 0), stop=(k == KD - 1))
                    last.then_inc(out2_done, 1)
            pe_turn(pe, 3)
            wait_nT(pe, 3)
            for use in range(8):
                n = CH_WQ + use // 2
                if use % 2 == 0:
                    ring_wait(pe, n)
                for m in range(2):
                    last = pe_columns(pe, bank[QUERY_BANK[use]][:, m * T:(m + 1) * T], n % RING, 2 * (use % 2) + m)
                last.then_inc(query_done, 1)
            pe.wait_ge(query_act, 4)
            pe.wait_ge(query_dve, 4)
            pe.wait_ge(keys_in, 16)
            for use in range(8):
                t, part = divmod(use, 4)
                for a in range(4):
                    hp = 4 * part + a
                    last = pe.matmul(bank[QUERY_BANK[use]][:, a * NKEYS:(a + 1) * NKEYS], qT[:, hp, t * P:(t + 1) * P],
                                     keysT[:, hp, :], start=True, stop=True)
                last.then_inc(score_done, 1)

            def bank_free(n, peeled):
                if not peeled or n >= 2:
                    pe.wait_ge(act_ready, n - 1)

            def columns_of(tile, table):
                if table == "u":
                    return tile[:, :].rearrange("p (k j i) -> p k j i", k=KD, j=CJ)
                return tile[:, :].rearrange("p (j d) -> p j d", j=CJ)

            def act_plain(i, at_n, peeled):
                n = at_n + UNROLL * i
                slot, b = at_n % RAW_SLOTS, at_n % 2
                bank_free(n, peeled)
                pe.wait_ge(raw_full[slot], fill(i, at_n))
                u = columns_of(raw[slot], "u")
                for j in range(CJ):
                    for k in range(KD):
                        last = pe.matmul(bank[4 + b][:, j * T:(j + 1) * T], u[:, k, j, :], nT[:, k, :],
                                         start=(k == 0), stop=(k == KD - 1))
                last.then_inc(chunk_used, 1)

            def act_split(n, at_n):
                slot, b = at_n % RAW_SLOTS, at_n % 2
                bank_free(n, False)
                hi = columns_of(lead[b], "u")
                lo = columns_of(rest[slot], "u")
                pe.wait_ge(lead_ready, n - PLAIN + 1)
                for j in range(CJ):
                    dst = bank[4 + b][:, j * T:(j + 1) * T]
                    for k in range(KD):
                        pe.matmul(dst, hi[:, k, j, :], nT_hi[:, k, :], start=(k == 0), stop=False)
                    if j == 0:
                        pe.wait_ge(nT_split, 1)
                    for k in range(KD):
                        pe.matmul(dst, hi[:, k, j, :], nT_lo[:, k, :], start=False, stop=False)
                    if j == 0:
                        pe.wait_ge(rest_ready, n - PLAIN + 1)
                    for k in range(KD):
                        last = pe.matmul(dst, lo[:, k, j, :], nT_hi[:, k, :], start=False, stop=(k == KD - 1))
                last.then_inc(chunk_used, 1)

            pe.wait_ge(score_ready, 8)
            head = PLAIN % UNROLL
            for n in range(head):
                act_plain(0, n, True)
            with pe.Fori(0, PLAIN // UNROLL) as i:
                for s in range(UNROLL):
                    act_plain(i, head + s, False)
            pe.wait_ge(gates_ready, 1)
            for i, src in enumerate((best, ij[:, 0], ij[:, 1])):
                for t in range(NT):
                    last = pe.transpose(bank[6 + i // 2][:, (i % 2) * T + t * P:(i % 2) * T + (t + 1) * P], src[:, t, :], ident)
            last.then_inc(route_turned, 1)
            with pe.Fori(0, (PEER_CHUNKS - PLAIN) // UNROLL) as i:
                for s in range(UNROLL):
                    act_split(PLAIN + UNROLL * i + s, PLAIN + s)

            def gate_products(g, b, peeled):
                pe.wait_ge(hot_j_ready, g + 1)
                if not peeled:
                    pe.wait_ge(gated, g - 1)
                for t in range(GT):
                    last = pe.matmul(bank[6 + b][:, t * NKEYS:(t + 1) * NKEYS], hot[b][:, 0, t, :], hot[b][:, 1, t, :],
                                     start=True, stop=True)
                last.then_inc(gates_done, 1)

            pe.wait_ge(route_ready, 1)
            for b in range(2):
                gate_products(b, b, True)
            with pe.Fori(1, GROUPS // 2) as g2:
                for b in range(2):
                    gate_products(2 * g2 + b, b, False)

            def out_products(n, at_n, first, last):
                slot, b = at_n % RAW_SLOTS, at_n % 2
                v_hi = columns_of(lead[b], "v")
                v_lo = columns_of(rest[slot], "v")
                c = n - PEER_CHUNKS
                pe.wait_ge(lead_ready, n - PLAIN + 1)
                pe.wait_ge(rest_ready, n - PLAIN + 1)
                pe.wait_ge(hid_hi_ready, c + 1)
                pe.wait_ge(hid_lo_ready, c + 1)
                for j in range(CJ):
                    for t in range(NT):
                        tok = slice(t * P, (t + 1) * P)
                        for i, (x, v) in enumerate(((hid_hi, v_hi), (hid_hi, v_lo), (hid_lo, v_hi))):
                            for half in range(2):
                                ins = pe.matmul(bank[2 * half + t][:, :], x[b][:, j, tok], v[:, j, half * 512:(half + 1) * 512],
                                                start=(first and j == 0 and i == 0), stop=(last and j == CJ - 1 and i == 2))
                ins.then_inc(chunk_used, 1)

            v_head = 2
            out_products(PEER_CHUNKS, PEER_CHUNKS, True, False)
            out_products(PEER_CHUNKS + 1, PEER_CHUNKS + 1, False, False)
            with pe.Fori(0, PEER_CHUNKS // UNROLL) as i:
                for s in range(UNROLL):
                    out_products(PEER_CHUNKS + v_head + UNROLL * i + s, PEER_CHUNKS + v_head + s, False, False)
            out_products(2 * PEER_CHUNKS - 2, 2 * PEER_CHUNKS - 2, False, False)
            out_products(2 * PEER_CHUNKS - 1, 2 * PEER_CHUNKS - 1, False, True)

        @block.vector
        def _(dve):
            link = chain(dve, dve_step)
            dve_stats(dve, link, 0)
            dve_xhat(dve)
            dve.wait_ge(const_in, 32)
            dve.tensor_tensor(lbd[:, :], prs("lb0"), prs("lb1"), ALU.subtract).then_inc(lb_diff, 1)
            dve_nT(dve, 0, "gain1")
            dve.wait_ge(lb_sig, 1)
            link(dve.tensor_scalar(omlb[:, :], lb[:, :], -1.0, 1.0, ALU.mult, ALU.add))
            dve.wait_ge(proj_act, 2)
            for hd in range(HEADS):
                last = dve.tensor_scalar(hF[:, hd, :], hF[:, hd, :], omlb[:, hd:hd + 1], lb[:, hd:hd + 1],
                                         ALU.mult, ALU.add)
            link(last)
            dve.tensor_scalar(hK[:, :, :], hF[:, :, :], -1.0, 1.0, ALU.mult, ALU.add).then_inc(f_ready, 1)
            for use, dst in ((2, hQ), (3, hQ), (4, hG), (5, hG)):
                dve.wait_ge(proj_act, use + 1)
                half = use % 2
                view = dst[:, 2 * half:2 * half + 2, :].rearrange("p a t -> p (a t)")
                dve.tensor_tensor(view, bank[IN1_BANK[use]][:, :], view, ALU.mult).then_inc(proj_dve, 1)
            dve.wait_ge(lf_ready, 1)
            for hd in range(HEADS):
                last = dve.tensor_tensor_scan(hB[:, hd, :], c("scanmask"), hF[:, hd, :], 0.0, ALU.mult, ALU.add)
            link(last)

            def chunks(tile):
                return tile[:, :, :].rearrange("p a (n s) -> p (a n) s", s=CHUNK)

            b_all = chunks(hB)
            shape = [P, HEADS * N_CHUNKS, CHUNK]
            mid = spread(b_all[:, :, CHUNK // 2 - 1:CHUNK // 2], shape)
            end = spread(b_all[:, :, CHUNK - 1:CHUNK], shape)
            dve.tensor_tensor(chunks(hD1), b_all, mid, ALU.subtract).then_inc(d_ready, 1)
            dve.tensor_tensor(chunks(hD2), end, b_all, ALU.subtract).then_inc(d_ready, 1)
            dve.wait_ge(exp_ready, 1)
            dve.wait_ge(proj_dve, 4)
            dve.tensor_tensor(hF[:, :, :], hQ[:, :, :], hF[:, :, :], ALU.mult).then_inc(qk_ready, 1)
            dve.wait_ge(exp_ready, 2)
            dve.tensor_tensor(hD1[:, :, :], hK[:, :, :], hD1[:, :, :], ALU.mult).then_inc(qk_ready, 1)
            dve.wait_ge(exp_ready, 3)
            dve.tensor_tensor(hD2[:, :, :], hK[:, :, :], hD2[:, :, :], ALU.mult).then_inc(qk_ready, 1)
            dve.wait_ge(exp_ready, 4)
            dve.wait_ge(qk_zero, 2)
            for odd, dst in enumerate((hQE, hQO)):
                def pick(tile):
                    return tile[:, :, :].rearrange("p a (n e s) -> p (a n) e s", e=2, s=CHUNK)[:, :, odd, :]
                dve.tensor_tensor(pick(dst), pick(hQ), pick(hEB), ALU.mult).then_inc(qk_ready, 1)
            dve.wait_ge(qk_zero, 3)
            mask = spread(c("causal").bitcast(U32).unsqueeze(1), [P, HEADS, P])
            for t in range(NT):
                dve.wait_ge(sc_done, t + 1)
                dve.copy_predicated(hSC[:, t, :, :], mask, quad(bank[t])).then_inc(sc_masked, 1)
            dve.wait_ge(proj_act, 10)
            link(dve.tensor_tensor(mSQ[:, :, :], mV[:, :, :], mV[:, :, :], ALU.mult))
            link(dve.tensor_reduce(vss[:, :], mSQ[:, :, :].rearrange("p t (g c) -> p (t g) c", g=HEADS), AX_X, ALU.add))
            dve.tensor_scalar(vss[:, :], vss[:, :], 1.0 / P, EPS, ALU.mult, ALU.add).then_inc(v_ms, 1)
            dve.wait_ge(v_sd, 1)
            link(dve.reciprocal(vrs[:, :], vrs[:, :]))
            v8 = mV[:, :, :].rearrange("p t (g c) -> p (t g) c", g=HEADS)
            dve.tensor_tensor(v8, v8, spread(vrs[:, :].unsqueeze(2), [P, NT * HEADS, P]), ALU.mult).then_inc(vh_ready, 1)
            dve.wait_ge(state_done, 1)
            dve.tensor_copy(hS[:, 0, :, :], quad(bank[4])).then_inc(state_ready, 1)
            eb = hEB[:, :, :].rearrange("p a (n s) -> p a n s", s=CHUNK)
            for n in (1, 2):
                dve.wait_ge(state_ready, n)
                decay = spread(eb[:, :, n, CHUNK - 1:CHUNK], [P, HEADS, P])
                link(dve.tensor_tensor(hS[:, n, :, :], hS[:, n - 1, :, :], decay, ALU.mult))
                dve.wait_ge(state_done, n + 1)
                dve.tensor_tensor(hS[:, n, :, :], quad(bank[4 + n]), hS[:, n, :, :], ALU.add).then_inc(state_ready, 1)
            dve.wait_ge(rows_in, 16)
            dve.wait_ge(proj_act, 12)
            for g in range(HEADS):
                dve.wait_ge(mixed_done, g // 2 + 1)
                src = bank[7 if g < 2 else 4][:, (g % 2) * T:(g % 2 + 1) * T].rearrange("p (t i) -> p t i", t=NT)
                bias = spread(row("b_s")[:, g * P:(g + 1) * P].unsqueeze(1), [P, NT, P])
                dst = mixT[:, g, :].rearrange("p (t i) -> p t i", t=NT)
                link(dve.scalar_tensor_tensor(dst, src, pr("vgain", g), bias, ALU.mult, ALU.add))
                dve.tensor_tensor(mixT[:, g, :], mixT[:, g, :], mU[:, g, :], ALU.mult).then_inc(mix_g, 1)
            dve.wait_ge(o_sq, NT)
            link(dve.tensor_reduce(oss[:, :], mSQ[:, :, :].rearrange("p t (g c) -> p (t g) c", g=HEADS), AX_X, ALU.add))
            dve.tensor_scalar(oss[:, :], oss[:, :], 1.0 / P, EPS, ALU.mult, ALU.add).then_inc(o_ms, 1)
            dve.wait_ge(o_sd, 1)
            link(dve.reciprocal(ors[:, :], ors[:, :]))
            for t in range(NT):
                last = dve.tensor_tensor(hON[:, t, :].rearrange("p (g c) -> p g c", g=HEADS), quad(bank[t]),
                                         spread(ors[:, t * HEADS:(t + 1) * HEADS].unsqueeze(2), [P, HEADS, P]), ALU.mult)
            last.then_inc(on_ready, 1)
            for hd in range(HEADS):
                dve.wait_ge(on_turned, hd // 2 + 1)
                dve.scalar_tensor_tensor(mixT[:, HEADS + hd, :], bank[2 + hd // 2][:, (hd % 2) * T:(hd % 2 + 1) * T],
                                         pr("ogain", hd), hG[:, hd, :], ALU.mult, ALU.mult).then_inc(mix_h, 1)
            for half in range(2):
                for t in range(NT):
                    dve.wait_ge(out1_done, 2 * half + t + 1)
                    dst = h[:, t, half * 512:(half + 1) * 512]
                    dve.tensor_tensor(dst, bank[OUT1_BANK[2 * half + t]][:, :], dst, ALU.add).then_inc(h_ready, 1)
            dve_stats(dve, link, 1)
            dve_xhat(dve)
            dve_nT(dve, 1, "gain2")
            dve.memset(g8[:, :, :], BIG)
            dve.memset(em[:, :, :], BIG)
            dve.wait_ge(router_done, 1)
            link(dve.tensor_tensor(lg[:, :, :], bank[4][:, 0:2 * 64].rearrange("p (t e) -> p t e", t=NT)[:, :, 0:NE],
                                   spread(row("b_router").unsqueeze(1), [P, NT, NE]), ALU.add))
            link(dve.tensor_copy(g8[:, :, 0:N_GROUPS], lg[:, :, 0:N_GROUPS]))
            for t in range(NT):
                last = dve.max(gm8[:, t, :], g8[:, t, :])
            link(last)
            for t in range(NT):
                last = dve.max_index(gi8[:, t, :], gm8[:, t, :], g8[:, t, :])
            link(last)
            dve.tensor_scalar(gneg[:, :].unsqueeze(2), gm8[:, :, 0:1], -1.0, None, ALU.mult).then_inc(gneg_ready, 1)
            link(dve.tensor_copy(gid[:, :].unsqueeze(2), gi8[:, :, 0:1]))
            for t in range(NT):
                last = dve.tensor_scalar(emask[:, t, :], c("group"), gid[:, t:t + 1], None, ALU.is_equal)
            link(last)
            link(dve.copy_predicated(em[:, :, :], emask[:, :, :], lg[:, :, N_GROUPS:]))
            for t in range(NT):
                last = dve.max(ev8[:, t, :], em[:, t, :])
            link(last)
            for t in range(NT):
                last = dve.max_index(ei8[:, t, :], ev8[:, t, :], em[:, t, :])
            link(last)
            dve.tensor_scalar(eneg[:, :].unsqueeze(2), ev8[:, :, 0:1], -1.0, None, ALU.mult).then_inc(eneg_ready, 1)
            link(dve.tensor_copy(eid[:, :, :], ei8[:, :, 0:2]))
            for k in range(2):
                for t in range(NT):
                    last = dve.tensor_scalar(chosen[:, k, t, :], c("iota")[:, 0:N_EXPERTS], eid[:, t, k:k + 1], None,
                                             ALU.is_equal)
            link(last)
            dve.tensor_tensor(assigned[:, :, :], chosen[:, 0, :, :], chosen[:, 1, :, :], ALU.add).then_inc(assign_ready, 1)
            dve.wait_ge(gsum_ready, NT)
            dve.wait_ge(e21_ready, NT)
            link(dve.scalar_tensor_tensor(wt[:, 0, :], e21[:, :], 1.0, gsum[:, :], ALU.add, ALU.mult))
            link(dve.reciprocal(wt[:, 0, :], wt[:, 0, :]))
            link(dve.tensor_tensor(wt[:, 1, :], wt[:, 0, :], e21[:, :], ALU.mult))
            dve.wait_ge(rank_done, 1)
            link(dve.tensor_copy(counts[:, :], bank[5][:, 64:96]))
            link(dve.tensor_tensor_scan(starts[:, :], c("ones")[:, 0:N_EXPERTS], counts[:, :], 0.0, ALU.mult, ALU.add))
            dve.tensor_reduce(most[:, :], counts[:, :], AX_X, ALU.max)
            link(dve.tensor_tensor(starts[:, :], starts[:, :], counts[:, :], ALU.subtract))
            dve.tensor_copy(most_i[:, :], most[0:1, :])
            dve.tensor_copy(starts_i[:, :], starts[0:1, :]).then_inc(starts_ready, 1)
            link(dve.tensor_tensor(slot_of[:, :, :], bank[5][:, 0:64].rearrange("p (t e) -> p t e", t=NT),
                                   spread(starts[:, :].unsqueeze(1), [P, NT, N_EXPERTS]), ALU.add))
            for k in range(2):
                last = dve.tensor_tensor(chosen[:, k, :, :], chosen[:, k, :, :], slot_of[:, :, :], ALU.mult)
            link(last)
            link(dve.tensor_reduce(slot[:, :, :], chosen[:, :, :, :], AX_X, ALU.add))
            for t in range(NT):
                link(dve.tensor_scalar(pick_slot[:, t, :], c("iota"), slot[:, 0, t:t + 1], None, ALU.is_equal))
                dve.scalar_tensor_tensor(pick_slot[:, t, :], c("iota"), slot[:, 1, t:t + 1], pick_slot[:, t, :],
                                         ALU.is_equal, ALU.add).then_inc(pick_ready, 1)
            for t in range(NT):
                dve.tensor_scalar(pick_wt[:, t, :], c("iota"), slot[:, 0, t:t + 1], wt[:, 0, t:t + 1],
                                  ALU.is_equal, ALU.mult)
                link(dve.tensor_scalar(pick_tmp[:, t, :], c("iota"), slot[:, 1, t:t + 1], wt[:, 1, t:t + 1],
                                       ALU.is_equal, ALU.mult))
                dve.tensor_tensor(pick_wt[:, t, :], pick_wt[:, t, :], pick_tmp[:, t, :], ALU.add).then_inc(pick_ready, 1)
            for k in range(1, KD, 2):
                dve.wait_ge(gather_done, k + 1)
                dve.tensor_scalar(xs[:, k, 0:SLOTS], bank[GATHER_BANK[k]][:, :], pr("gain2", k), None,
                                  ALU.mult).then_inc(xs_dve, 1)

            dve.wait_ge(starts_ready, 1)
            load_most = dve.value_load(most_i[0:1, 0:1], min_val=0, max_val=T)
            with dve.If(load_most > BLOCK):
                def many_vector(e, peeled):
                    for b in range(BLOCKS_MAX):
                        n = e * BLOCKS_MAX + b
                        dve.wait_ge(many_up, n + 1)
                        dve.wait_ge(sil_ready, n + 1)
                        dve.tensor_tensor(hid[0][:, :], bank[2][0:BLOCK, :], hid[0][:, :], ALU.mult).then_inc(hid_ready, 1)
                        dve.wait_ge(many_down, 2 * n + 2)
                        if b or not peeled:
                            dve.wait_ge(many_stored, 16 * n)
                        dve.tensor_copy(y_blk[0][:, 512:], bank[7][0:BLOCK, :]).then_inc(y_dve, 1)

                many_vector(0, True)
                with dve.Fori(1, N_EXPERTS) as e:
                    many_vector(e, False)
            with dve.Else():
                def split_rest(e, j, kind):
                    slot = W_SLOT[3 * j + kind]
                    for half in range(2):
                        part = slice(4 * half, 4 * half + 4)
                        dve.wait_ge(w_lead_ready, 4 * e + 2 * kind + half + 1)
                        dve.tensor_tensor(ring_rest8(slot)[:, part, :], ring8(slot)[:, part, :],
                                          w_lead[half][:, :, :].bitcast(F32), ALU.subtract).then_inc(w_rest_ready, 1)

                def total(e, j, kind):
                    dve.wait_ge((gate_low, up_low)[kind], e + 1)
                    dst = (hid, upv)[kind][j]
                    return dve.tensor_tensor(dst[:, :], bank[2 * kind + j][0:BLOCK, :], dst[:, :],
                                             ALU.add).then_inc((gate_sum, up_sum)[kind], 1)

                def copy(e, j, peeled):
                    dve.wait_ge(down_done, 2 * e + 2)
                    if not peeled:
                        dve.wait_ge(y_stored, 16 * e - 16)
                    dve.tensor_copy(y_blk[j][:, 512:], bank[7][0:BLOCK, :]).then_inc(y_dve, 1)

                def expert_vector(e, j, peeled, former_peeled):
                    split_rest(e, j, 0)
                    if not peeled:
                        copy(e - 2, j, former_peeled)
                    split_rest(e, j, 1)
                    total(e, j, 0)
                    total(e, j, 1)
                    dve.wait_ge(up_sum, e + 1)
                    dve.wait_ge(sil_ready, e + 1)
                    dve.tensor_tensor(hid[j][:, :], hid[j][:, :], upv[j][:, :], ALU.mult).then_inc(hid_ready, 1)

                for j in range(2):
                    expert_vector(j, j, True, True)
                for j in range(2):
                    expert_vector(2 + j, j, False, True)
                with dve.Fori(2, PAIRS) as pair:
                    for j in range(2):
                        expert_vector(2 * pair + j, j, False, False)
                for j in range(2):
                    copy(N_EXPERTS - 2 + j, j, False)
            for use in range(4):
                half, t = divmod(use, NT)
                dve.wait_ge(moe_done, use + 1)
                dst = h[:, t, half * 512:(half + 1) * 512]
                dve.tensor_tensor(dst, bank[use][:, :], dst, ALU.add).then_inc(h_ready, 1)
            dve_stats(dve, link, 2)
            dve.wait_ge(gain_in, 16)
            for t in range(NT):
                dve.scalar_tensor_tensor(h[:, t, :], h[:, t, :], stat_rs[:, t:t + 1], gain_row[:, :],
                                         ALU.mult, ALU.mult).then_inc(h_ready, 1)
            dve_stats(dve, link, 3)
            dve_xhat(dve)
            dve_nT(dve, 2, "gain12")
            def halves(ap, half):
                return ap.rearrange("p (s e f) -> p s e f", s=2, e=2)[:, :, half, :]

            dve.wait_ge(h_ready, H_COUNT[3])
            for i, gain in enumerate(("qgain", "kgain")):
                for t in range(NT):
                    cs = c("cos")[:, t * DH:(t + 1) * DH]
                    sn = c("sin")[:, t * DH:(t + 1) * DH]
                    dve.tensor_tensor(cos_gain[:, i, t, :], cs, row(gain), ALU.mult)
                    for half in range(2):
                        last = dve.tensor_tensor(halves(sin_gain[:, i, t, :], half), halves(sn, half),
                                                 halves(row(gain), 1 - half), ALU.mult)
            link(last)
            dve.wait_ge(p2_act, 3)
            link(dve.tensor_reduce(qk_ss[:, :], qk_sq[:, :, :].rearrange("p t (a d) -> p (t a) d", d=DH), AX_X, ALU.add))
            dve.tensor_scalar(qk_ss[:, :], qk_ss[:, :], 1.0 / DH, EPS, ALU.mult, ALU.add).then_inc(qk_ms, 1)
            dve.wait_ge(qk_sd, 1)
            link(dve.reciprocal(qk_rs[:, :], qk_rs[:, :]))
            heads = qk[:, :, :].rearrange("p t (a d) -> p (t a) d", d=DH)
            link(dve.tensor_tensor(heads, heads, spread(qk_rs[:, :].unsqueeze(2), [P, NT * N_QK, DH]), ALU.mult))
            for t in range(NT):
                for i, (a, b) in enumerate(((0, GQA_HEADS), (GQA_HEADS, N_QK))):
                    src = qk[:, t, a * DH:b * DH].rearrange("p (a s e f) -> p (a s) e f", s=2, e=2, f=DH // 4)
                    dst = qk_rot[:, t, a * DH:b * DH].rearrange("p (a s e f) -> p (a s) e f", s=2, e=2, f=DH // 4)
                    for half in range(2):
                        table = spread(halves(sin_gain[:, i, t, :], half).unsqueeze(1), [P, b - a, 2, DH // 4])
                        last = dve.tensor_tensor(dst[:, :, half, :].rearrange("p (a s) f -> p a s f", s=2),
                                                 src[:, :, 1 - half, :].rearrange("p (a s) f -> p a s f", s=2), table, ALU.mult)
            link(last)
            for t in range(NT):
                for i, (a, b) in enumerate(((0, GQA_HEADS), (GQA_HEADS, N_QK))):
                    view = qk[:, t, a * DH:b * DH].rearrange("p (a d) -> p a d", d=DH)
                    last = dve.tensor_tensor(view, view, spread(cos_gain[:, i, t, :].unsqueeze(1), [P, b - a, DH]), ALU.mult)
            link(last)
            nq = GQA_HEADS * DH
            for copy in range(2):
                dve.tensor_tensor(kk[:, :, :, copy, :], qk[:, :, nq:].rearrange("p t (a d) -> p t a d", d=DH),
                                  qk_rot[:, :, nq:].rearrange("p t (a d) -> p t a d", d=DH), ALU.add)
            dve.tensor_tensor(qk[:, :, 0:nq], qk[:, :, 0:nq], qk_rot[:, :, 0:nq], ALU.add).then_inc(qk_roped, 1)
            for i, dst in enumerate((qaT[:, 0:2, :].rearrange("p a t -> p (a t)"),
                                     qaT[:, 2:4, :].rearrange("p a t -> p (a t)"), va[:, 0, :], va[:, 1, :])):
                dve.wait_ge(p2_done, (4, 5, 8, 9)[i])
                dve.tensor_copy(dst, bank[(7, 0, 3, 4)[i]][:, :]).then_inc(p2_dve, 1)
            dve.wait_ge(qk_turned, 3)
            dve.tensor_copy(kbT[:, :, :].rearrange("p a t -> p (a t)"), bank[7][:, :]).then_inc(kbT_ready, 1)
            dve.wait_ge(bias_ready, NT)
            sa = bank[0][:, :].rearrange("p (t k) -> p t k", t=NT)
            sb = bank[1][:, :].rearrange("p (t k) -> p t k", t=NT)
            for i in range(NA_HEADS):
                dve.wait_ge(sa_done, i + 1)
                if i:
                    dve.wait_ge(pa_turned, i)
                link(dve.scalar_tensor_tensor(prob_a[:, :, :], sa, SCALE, rel_bias[:, :, i, :], ALU.mult, ALU.add))
                link(dve.tensor_reduce(top_a[:, :], prob_a[:, :, :], AX_X, ALU.max))
                dve.tensor_scalar(top_a[:, :], top_a[:, :], -1.0, None, ALU.mult).then_inc(ta_ready, 1)
                dve.wait_ge(sb_done, i + 1)
                link(dve.tensor_reduce(top_b[:, :], sb, AX_X, ALU.max))
                dve.tensor_scalar(top_b[:, :], top_b[:, :], -SCALE, None, ALU.mult).then_inc(tb_ready, 1)
                dve.wait_ge(ea_ready, 2 * (i + 1))
                link(dve.reciprocal(sum_a[:, :], sum_a[:, :]))
                dve.tensor_tensor(prob_a[:, :, :], prob_a[:, :, :], spread(sum_a[:, :].unsqueeze(2), [P, NT, T]),
                                  ALU.mult).then_inc(pa_ready, 1)
                dve.wait_ge(eb_ready, 2 * (i + 1))
                link(dve.reciprocal(sum_b[:, :], sum_b[:, :]))
                dve.tensor_tensor(prob_b[:, :, :], prob_b[:, :, :], spread(sum_b[:, :].unsqueeze(2), [P, NT, T]),
                                  ALU.mult).then_inc(pb_ready, 1)
                dve.wait_ge(pb_turned, i + 1)
                if i:
                    dve.wait_ge(yb_done, i)
                dve.tensor_copy(prob_bT[:, :, :].rearrange("p k q -> p (k q)"), bank[3][:, :]).then_inc(pbT_ready, 1)
            dve.wait_ge(sg_ready, 2)
            for i in range(4):
                part = slice(2 * i, 2 * i + 2)
                for b, gate in enumerate((sga, sgb)):
                    dve.wait_ge(branch_done, 2 * i + b + 1)
                    view = gate[:, part, :].rearrange("p a t -> p (a t)")
                    last = dve.tensor_tensor(view, bank[BRANCH_BANK[b][i]][:, :], view, ALU.mult)
                link(last)
                dve.tensor_tensor(sga[:, part, :], sga[:, part, :], sgb[:, part, :], ALU.add).then_inc(merged_ready, 1)
            for half in range(2):
                for t in range(NT):
                    dve.wait_ge(out2_done, 2 * half + t + 1)
                    dst = h[:, t, half * 512:(half + 1) * 512]
                    dve.tensor_tensor(dst, bank[2 * half + t][:, :], dst, ALU.add).then_inc(h_ready, 1)
            dve_stats(dve, link, 4)
            dve_xhat(dve)
            dve_nT(dve, 3, "gain22")
            for use in range(1, 8, 2):
                dve.wait_ge(query_done, use + 1)
                dve.tensor_copy(qT[:, 2 * use:2 * use + 2, :].rearrange("p a t -> p (a t)"),
                                bank[QUERY_BANK[use]][:, :]).then_inc(query_dve, 1)

            def best_of(views):
                for lo in (0, 8):
                    for score, value, _ in views:
                        last = dve.max(value[:, lo:lo + 8], score)
                    link(last)
                    for score, value, place in views:
                        last = dve.max_index(place[:, lo:lo + 8], value[:, lo:lo + 8], score)
                    link(last)
                    if lo == 0:
                        for score, value, _ in views:
                            last = dve.match_replace(score, value[:, 0:8], score, BIG)
                        link(last)

            for use in range(8):
                t, part = divmod(use, 4)
                dve.wait_ge(score_ready, use + 1)
                best_of([(sc[:, t, hp, :], ts[:, t, hp, :], ti[:, t, hp, :]) for hp in range(4 * part, 4 * part + 4)])
            link(dve.tensor_copy(tif[:, :, :, :], ti[:, :, :, :]))
            wide = [P, PEER_HEADS, TOPK, TOPK]

            def half_of(tile, t, half):
                return tile[:, t, :, :].rearrange("p (a e) k -> p a e k", e=2)[:, :, half, :]

            for t in range(NT):
                last = dve.tensor_tensor(cand[:, t, :, :, :], spread(half_of(ts, t, 0).unsqueeze(3), wide),
                                         spread(half_of(ts, t, 1).unsqueeze(2), wide), ALU.add)
            link(last)
            for t in range(NT):
                best_of([(cand[:, t, a, :, :].rearrange("p x y -> p (x y)"), best[:, t, a * TOPK:(a + 1) * TOPK],
                          bpos[:, t, a * TOPK:(a + 1) * TOPK]) for a in range(PEER_HEADS)])
            dve.tensor_scalar(bdig[:, 0, :, :], bpos[:, :, :], 4, None, ALU.logical_shift_right)
            link(dve.tensor_scalar(bdig[:, 1, :, :], bpos[:, :, :], TOPK - 1, None, ALU.bitwise_and))
            link(dve.tensor_copy(bdigf[:, :, :, :], bdig[:, :, :, :]))
            for half in range(2):
                for t in range(NT):
                    link(dve.tensor_tensor(match[:, :, :], spread(c("iota")[:, 0:TOPK].unsqueeze(1), [P, HK, TOPK]),
                                           spread(bdigf[:, half, t, :].unsqueeze(2), [P, HK, TOPK]), ALU.is_equal))
                    by_head = match[:, :, :].rearrange("p (a k) x -> p a k x", a=PEER_HEADS)
                    link(dve.tensor_tensor(by_head, by_head, spread(half_of(tif, t, half).unsqueeze(2), wide), ALU.mult))
                    link(dve.tensor_reduce(ij[:, half, t, :], match[:, :, :], AX_X, ALU.add))
            by_head = best[:, :, :].rearrange("p t (a k) -> p (t a) k", k=TOPK)
            flat = [P, NT * PEER_HEADS, TOPK]
            link(dve.tensor_copy(best_sum[:, :].unsqueeze(2), by_head[:, :, 0:1]))
            dve.tensor_tensor(by_head, by_head, spread(best_sum[:, :].unsqueeze(2), flat), ALU.subtract).then_inc(routed, 1)
            dve.wait_ge(best_exp, 1)
            link(dve.tensor_reduce(best_sum[:, :], by_head, AX_X, ALU.add))
            link(dve.reciprocal(best_sum[:, :], best_sum[:, :]))
            dve.tensor_tensor(by_head, by_head, spread(best_sum[:, :].unsqueeze(2), flat), ALU.mult).then_inc(gates_ready, 1)

            def lead_of(dst, src):
                return dve.tensor_copy(dst, src)

            def split_chunk(n, at_n, loaded):
                slot, b = at_n % RAW_SLOTS, at_n % 2
                dve.wait_ge(raw_full[slot], loaded)
                dve.wait_ge(chunk_used, n - 1)
                lead_of(lead[b][:, :], raw[slot][:, :]).then_inc(lead_ready, 1)
                dve.wait_ge(lead_ready, n - PLAIN + 1)
                dve.tensor_tensor(rest[slot][:, :], raw[slot][:, :], lead[b][:, :].bitcast(F32), ALU.subtract).then_inc(rest_ready, 1)

            lead_of(nT_hi[:, :, :], nT[:, :, :]).then_inc(nT_masked, 1)
            dve.wait_ge(route_turned, 1)
            dve.wait_ge(nT_masked, 1)
            dve.tensor_tensor(nT_lo[:, :, :], nT[:, :, :], nT_hi[:, :, :].bitcast(F32), ALU.subtract).then_inc(nT_split, 1)
            dve.tensor_copy(bestT[:, :], bank[6][:, 0:T])
            dve.tensor_copy(ijT[:, 0, :], bank[6][:, T:])
            dve.tensor_copy(ijT[:, 1, :], bank[7][:, 0:T]).then_inc(route_ready, 1)

            def one_hots(g, b):
                whole = [P, 2, GT, NKEYS]
                dve.tensor_tensor(hot[b][:, :, :, :], spread(c("iota")[:, 0:NKEYS].unsqueeze(1).unsqueeze(1), whole),
                                  spread(ijT[:, :, bass.ds(g * GT, GT)].unsqueeze(3), whole),
                                  ALU.is_equal).then_inc(hot_ready, 1)

            def gate_columns(g, b):
                dve.wait_ge(gates_done, g + 1)
                view = A[:, :, bass.ds(g * GT, GT)]
                dve.tensor_tensor(view, bank[6 + b][:, :].rearrange("p (t j) -> p j t", t=GT), view, ALU.mult).then_inc(gated, 1)

            with dve.Fori(0, (PEER_CHUNKS - PLAIN) // UNROLL) as i:
                for s in range(UNROLL):
                    n = PLAIN + UNROLL * i + s
                    split_chunk(n, PLAIN + s, fill(i, PLAIN + s))
            dve.wait_ge(route_ready, 1)
            dve.wait_ge(chunk_used, PEER_CHUNKS)
            for b in range(2):
                one_hots(b, b)
            dve.wait_ge(act_ready, PEER_CHUNKS)
            with dve.Fori(0, GROUPS // 2 - 1) as g2:
                for b in range(2):
                    gate_columns(2 * g2 + b, b)
                    one_hots(2 * g2 + b + 2, b)
            for b in range(2):
                gate_columns(GROUPS - 2 + b, b)
            def split_hidden(n, at_n):
                c, b = n - PEER_CHUNKS, at_n % 2
                src = A[:, bass.ds(c * CJ, CJ), :]
                lead_of(hid_hi[b][:, :, :], src).then_inc(hid_hi_ready, 1)
                dve.wait_ge(hid_hi_ready, c + 1)
                dve.tensor_tensor(hid_lo[b][:, :, :], src, hid_hi[b][:, :, :].bitcast(F32), ALU.subtract).then_inc(hid_lo_ready, 1)

            def split_both(n, at_n, loaded):
                split_chunk(n, at_n, loaded)
                split_hidden(n, at_n)

            dve.wait_ge(gated, GROUPS)
            dve.wait_ge(gates_done, GROUPS)
            dve.wait_ge(hot_j_ready, GROUPS)
            v_head = 2
            for n in range(PEER_CHUNKS, PEER_CHUNKS + v_head):
                split_both(n, n, fill(0, n))
            with dve.Fori(0, PEER_CHUNKS // UNROLL) as i:
                for s in range(UNROLL):
                    at_n = PEER_CHUNKS + v_head + s
                    n = at_n + UNROLL * i
                    split_both(n, at_n, fill(i, at_n))
            for n in range(2 * PEER_CHUNKS - 2, 2 * PEER_CHUNKS):
                split_both(n, n, fill(0, n))
            for use in range(4):
                half, t = divmod(use, NT)
                dve.wait_ge(chunk_used, 2 * PEER_CHUNKS)
                dst = h[:, t, half * 512:(half + 1) * 512]
                dve.tensor_tensor(dst, bank[2 * half + t][:, :], dst, ALU.add).then_inc(h_ready, 1)
            dve_stats(dve, link, 5)
            dve.wait_ge(gain_f_in, 16)
            for t in range(NT):
                dve.scalar_tensor_tensor(h[:, t, :], h[:, t, :], stat_rs[:, t:t + 1], gain_f[:, :],
                                         ALU.mult, ALU.mult).then_inc(out_ready, 1)

        return locals()


def layouts(inputs):
    g = {k: np.asarray(v) for k, v in inputs.items()}

    def across(a):
        return a.reshape(-1, P).T

    out = {
        "x": g["x"][0],
        "const": constants(),
        "param": np.concatenate([
            across(g["norm1_gain"][0]), across(g["gmlp_v_gain"][0]), across(g["hgrn_lower_bounds"][0]),
            across(g["hgrn_lower_bounds"][1]), across(g["hgrn_out_gain"][0]), across(g["norm2_gain"][0]),
            across(g["norm1_g_2"][0]), across(g["norm2_g_2"][0])], axis=1),
        "rows": np.concatenate([g["gmlp_b_s"][0].reshape(-1), g["b_group_router"][0], g["b_expert_router"][0],
                                g["gqa_q_norm_g_2"][0], g["gqa_k_norm_g_2"][0]])[None],
        "w_in": g["w_in"][0],
        "w_sT": g["gmlp_w_s"][0].transpose(2, 0, 1).reshape(P, HEADS * P),
        "w_out": g["w_out"][0],
        "w_group_router": g["w_group_router"][0],
        "w_expert_router": g["w_expert_router"][0],
        "w_gate": g["w_gate"][0],
        "w_up": g["w_up"][0],
        "w_down": g["w_down"][0],
        "final_gain": g["final_gain"][None],
        "w_in_2": g["w_in_2"][0],
        "rpb": g["na_rpb_2"][0].reshape(-1),
        "w_proj_a": g["w_proj_a_2"][0],
        "w_proj_b": g["w_proj_b_2"][0],
        "w_out_2": g["w_out_2"][0],
        "w_q": g["peer_w_q_2"][0],
        "keysT": g["peer_sub_keys_2"][0].transpose(3, 0, 1, 2).reshape(P, HP * NKEYS),
        "u": g["peer_u_2"][0].reshape(NKEYS, PEER_CHUNKS, CJ, KD, P).transpose(1, 4, 3, 2, 0).reshape(PEER_CHUNKS, P, -1),
        "v": g["peer_v_2"][0].reshape(NKEYS, PEER_CHUNKS, CJ * D).transpose(1, 0, 2),
        "norm_f_g": g["norm_f_g_2"][None],
    }
    return {k: np.ascontiguousarray(v) for k, v in out.items()}


def kernel(**inputs):
    import concourse.bacc as bacc
    from concourse.bass_utils import run_bass_kernel_spmd

    arrays = layouts(inputs)
    nc = bacc.Bacc("TRN2", target_bir_lowering=False, num_devices=1)
    dram = {k: nc.dram_tensor(f"in_{k}", v.shape, mybir.dt.from_np(v.dtype), kind="ExternalInput").ap()
            for k, v in arrays.items()}
    out = nc.dram_tensor("out", (T, D), F32, kind="ExternalOutput").ap()
    build(nc, dram, out)
    r = run_bass_kernel_spmd(nc, [{f"in_{k}": v for k, v in arrays.items()}], core_ids=[0])
    return r.results[0]["out"].reshape(1, T, D)
```

```python
from contextlib import ExitStack

import numpy as np

import concourse.bass as bass
from concourse import mybir

F32 = mybir.dt.float32
F32R = mybir.dt.float32r
U32 = mybir.dt.uint32
I32 = mybir.dt.int32
ALU = mybir.AluOpType
ACT = mybir.ActivationFunctionType
AX_X = mybir.AxisListType.X

P = 128
T = 256
NT = T // P
D = 1024
KD = D // P
EPS = 1e-6
BIG = -3.0e38

HEADS = 4
CHUNK = 64
N_CHUNKS = T // CHUNK
N_GROUPS = 4
N_EXPERTS = 32
PER_GROUP = N_EXPERTS // N_GROUPS
D_EXPERT = 512
SLOTS = 2 * T
BLOCK = 64
BLOCKS_MAX = T // BLOCK
SLOTS_PAD = SLOTS + T

NA_HEADS = 8
DH = 64
GRID_W = 64
KROWS = T // GRID_W
WIN_W = 16
RPB_H, RPB_W = 15, 31
RPB_ROWS = 2 * KROWS - 1
GQA_HEADS = 8
KV_HEADS = 2
N_QK = GQA_HEADS + KV_HEADS
SCALE = DH ** -0.5
PEER_HEADS = 8
NKEYS = 128
TOPK = 16
HP = 2 * PEER_HEADS

RING = 6
CHUNK_COLS = 4096
IN1_ORDER = (3, 2, 5, 4, 1, 0)
CH_OUT1 = 6
CH_MOE = CH_OUT1 + 2
CH_IN2 = CH_MOE + 3 * N_EXPERTS
IN2_COLS = [(1536, 512), (2048, 256), (0, 512), (512, 512), (1024, 512),
            (2304, 512), (2816, 512), (3328, 512), (3840, 512)]
CH_PROJ = CH_IN2 + len(IN2_COLS)
CH_OUT2 = CH_PROJ + 2
CH_WQ = CH_OUT2 + 2
CH_END = CH_WQ + 4
LEAD_SLOT = 1
BLOCK2_SLOTS = (2, 3, 4, 5, 0)
IN1_SLOTS = 4
SPLIT = ([(n, 512) for n in range(6)] + [(CH_IN2 + i, IN2_COLS[i][1]) for i in range(len(IN2_COLS))]
         + [(CH_WQ + i, 512) for i in range(4)])
SPLIT_IN2 = 6
SPLIT_WQ = SPLIT_IN2 + len(IN2_COLS)

CJ = 2
RAW_SLOTS = 3
UNROLL = 6
ROUTING = 16
PEER_CHUNKS = NKEYS // CJ
HK = PEER_HEADS * TOPK
GT = 4
GROUPS = T // GT
HOTS = 4
VECTOR_HOTS = 1
SCALAR_HOTS = HOTS - VECTOR_HOTS

PAIR = [(0, 0), (0, 1), (0, 2), (1, 0), (1, 1), (1, 2)]
PAIRS = N_EXPERTS // 2

CONST_PARTS = [("ident", P), ("iota", SLOTS), ("window", GRID_W), ("cos", NT * DH), ("sin", NT * DH),
               ("causal", P), ("scanmask", T), ("before", P), ("ones", P), ("group", N_EXPERTS)]
PARAM_PARTS = [("gain1", KD), ("vgain", HEADS), ("lb0", HEADS), ("lb1", HEADS), ("ogain", HEADS),
               ("gain2", KD), ("gain12", KD), ("gain22", KD)]
ROW_PARTS = [("qgain", DH), ("kgain", DH), ("b_s", HEADS * P), ("b_router", N_GROUPS + N_EXPERTS)]


def columns(parts):
    at, out = 0, {}
    for name, n in parts:
        out[name] = (at, at + n)
        at += n
    return out, at


CONST_AT, CONST_N = columns(CONST_PARTS)
PARAM_AT, PARAM_N = columns(PARAM_PARTS)
ROW_AT, ROW_N = columns(ROW_PARTS)


def constants():
    c = np.zeros((P, CONST_N), np.float32)

    def put(name, value):
        a, b = CONST_AT[name]
        c[:, a:b] = value

    p = np.arange(P)
    put("ident", np.eye(P))
    put("causal", (p[:, None] <= p[None, :]) & (p[:, None] // CHUNK == p[None, :] // CHUNK))
    put("scanmask", np.broadcast_to(np.arange(T) % CHUNK != 0, (P, T)))
    put("iota", np.broadcast_to(np.arange(SLOTS), (P, SLOTS)))
    put("before", p[:, None] < p[None, :])
    put("ones", 1.0)
    col = p % GRID_W
    start = np.clip(col - WIN_W // 2, 0, GRID_W - WIN_W)
    key = np.arange(GRID_W)
    inside = (key[None, :] >= start[:, None]) & (key[None, :] < start[:, None] + WIN_W)
    put("window", np.where(inside, 0.0, BIG))
    sec, nf = DH // 2, DH // 4
    t = np.arange(T)
    inv = np.float32(10000.0) ** (-np.arange(nf, dtype=np.float32) / np.float32(nf))
    ang_r = (t // GRID_W).astype(np.float32)[:, None] * inv[None, :]
    ang_c = (t % GRID_W).astype(np.float32)[:, None] * inv[None, :]
    cos = np.concatenate([np.cos(ang_r), np.cos(ang_r), np.cos(ang_c), np.cos(ang_c)], 1)
    sin = np.concatenate([-np.sin(ang_r), np.sin(ang_r), -np.sin(ang_c), np.sin(ang_c)], 1)
    put("cos", cos.reshape(NT, P, DH).transpose(1, 0, 2).reshape(P, NT * DH))
    put("sin", sin.reshape(NT, P, DH).transpose(1, 0, 2).reshape(P, NT * DH))
    put("group", np.broadcast_to(np.arange(N_EXPERTS) // PER_GROUP, (P, N_EXPERTS)))
    return c


def build(nc, dram, out):
    with ExitStack() as ctx:
        place = [16512]

        def keep(name, shape, dt=F32):
            n = 4
            for s in shape[1:]:
                n *= s
            t = nc.alloc_sbuf_tensor_at(name, shape, dt, offset=place[0])
            place[0] += (n + 31) // 32 * 32
            return t

        ARENA = 229344 - 176 * 1024
        ACTS = ARENA + RING * 16384

        def at(name, shape, offset, dt=F32):
            return nc.alloc_sbuf_tensor_at(name, shape, dt, offset=offset)

        def acts(name, shape, kib, dt=F32):
            return at(name, shape, ACTS + int(kib * 1024), dt)

        h = keep("h", [P, NT, D])
        NT_AT = place[0]
        nT = keep("nT", [P, KD, T])
        param = keep("param", [P, PARAM_N])
        rows_qk = keep("rows_qk", [P, ROW_AT["b_s"][0]])
        stat_ss = keep("stat_ss", [P, NT])
        stat_ms = keep("stat_ms", [P, NT])
        stat_sd = keep("stat_sd", [P, NT])
        stat_warm = keep("stat_warm", [P, NT])
        stat_rs = keep("stat_rs", [P, NT])
        const = keep("const", [P, CONST_N])
        DEAD_AT = place[0] - 4 * (CONST_N - CONST_AT["causal"][0])
        rows = keep("rows", [P, ROW_N - ROW_AT["b_s"][0]])
        w_router = keep("w_router", [P, KD, N_GROUPS + N_EXPERTS])

        def c(name):
            a, b = CONST_AT[name]
            return const[:, a:b]

        def pr(name, i):
            a = PARAM_AT[name][0]
            return param[:, a + i:a + i + 1]

        def prs(name):
            a, b = PARAM_AT[name]
            return param[:, a:b]

        def row(name):
            a, b = ROW_AT[name]
            first = ROW_AT["b_s"][0]
            return rows_qk[:, a:b] if b <= first else rows[:, a - first:b - first]

        ident = c("ident")

        ring = [at(f"ring{s}", [P, CHUNK_COLS], ARENA + 16384 * s) for s in range(RING)]

        def ring8(s):
            return ring[s][:, :].rearrange("p (k f) -> p k f", k=8)

        ring_rest = [at(f"ring_rest{s}", [P, CHUNK_COLS], ARENA + 16384 * s, F32R) for s in range(RING)]

        def ring_rest8(s):
            return ring_rest[s][:, :].rearrange("p (k f) -> p k f", k=8)

        def ring4(s):
            return ring[s][:, :].rearrange("p (k f) -> p k f", k=4)

        half_lead1 = [at(f"half_lead1{b}", [P, CHUNK_COLS // 2], ARENA + 16384 * IN1_SLOTS + 8192 * b, F32R) for b in range(2)]
        half_lead2 = [at(f"half_lead2{b}", [P, CHUNK_COLS // 2], ARENA + 16384 * LEAD_SLOT + 8192 * b, F32R) for b in range(2)]
        nT_hi1 = at("nT_hi1", [P, KD, T], ARENA + 16384 * (IN1_SLOTS + 1), F32R)
        nT_hi = at("nT_hi", [P, KD, T], DEAD_AT, F32R)
        nT_lo = at("nT_lo", [P, KD, T], NT_AT, F32R)
        xhat = acts("xhat", [P, NT, D], 0)
        mixT = acts("mixT", [P, 8, T], 0)
        hF = acts("hF", [P, HEADS, T], 8)
        hK = acts("hK", [P, HEADS, T], 12)
        hB = acts("hB", [P, HEADS, T], 16)
        hD1 = acts("hD1", [P, HEADS, T], 20)
        hD2 = acts("hD2", [P, HEADS, T], 24)
        hEB = acts("hEB", [P, HEADS, T], 28)
        hQ = acts("hQ", [P, HEADS, T], 32)
        hQE = acts("hQE", [P, HEADS, T], 36)
        hQO = acts("hQO", [P, HEADS, T], 40)
        hI = acts("hI", [P, NT, 512], 44)
        hKL = acts("hKL", [P, NT, HEADS, P], 48)
        hSC = acts("hSC", [P, NT, HEADS, P], 52)
        hS = acts("hS", [P, N_CHUNKS - 1, HEADS, P], 56)
        hG = acts("hG", [P, HEADS, T], 62)
        mU = acts("mU", [P, HEADS, T], 66)
        mV = acts("mV", [P, NT, 512], 70)
        mSQ = acts("mSQ", [P, NT, 512], 74)
        hON = acts("hON", [P, NT, 512], 16)
        w_sT = acts("w_sT", [P, HEADS, P], 78)
        lbd = keep("lbd", [P, HEADS])
        lb = keep("lb", [P, HEADS])
        omlb = keep("omlb", [P, HEADS])
        vss = keep("vss", [P, NT * HEADS])
        vrs = keep("vrs", [P, NT * HEADS])
        oss = keep("oss", [P, NT * HEADS])
        ors = keep("ors", [P, NT * HEADS])

        pick_slot = acts("pick_slot", [P, NT, SLOTS], 8, F32R)
        xhat_lead = acts("xhat_lead", [P, NT, D], 52, F32R)
        xhat_rest = acts("xhat_rest", [P, NT, D], 60, F32R)
        pick_wt = acts("pick_wt", [P, NT, SLOTS], 12)
        pick_tmp = acts("pick_tmp", [P, NT, SLOTS], 16)
        xs = acts("xs", [P, KD, SLOTS_PAD], 20)
        x_blk = [acts(f"x_blk{j}", [P, KD, BLOCK], 4 + 2 * j) for j in range(2)]
        x_two = [acts(f"x_two{j}", [P, KD, 2 * BLOCK], (16, 0)[j], F32R) for j in range(2)]
        w_lead = [acts(f"w_lead{b}", [P, 4, 512], 52 + 8 * b, F32R) for b in range(2)]
        hid = [acts(f"hid{j}", [BLOCK, D_EXPERT], 44 + 2 * j) for j in range(2)]
        upv = [acts(f"upv{j}", [BLOCK, D_EXPERT], 68 + 2 * j) for j in range(2)]
        hT = [acts(f"hT{j}", [P, 4, BLOCK], 48 + j) for j in range(2)]
        y_blk = [acts(f"y_blk{j}", [BLOCK, D], 8 + 4 * j) for j in range(2)]
        slot_wt = acts("slot_wt", [P, SLOTS // P, T], 72)
        y_rows = acts("y_rows", [P, SLOTS // P, D], 20)
        gain_row = acts("gain_row", [P, D], 76)
        NE = N_GROUPS + N_EXPERTS
        lg = keep("lg", [P, NT, NE])
        g8 = keep("g8", [P, NT, 8])
        gm8 = keep("gm8", [P, NT, 8])
        gi8 = keep("gi8", [P, NT, 8], U32)
        gneg = keep("gneg", [P, NT])
        gex = keep("gex", [P, NT, N_GROUPS])
        gsum = keep("gsum", [P, NT])
        gid = keep("gid", [P, NT])
        emask = keep("emask", [P, NT, N_EXPERTS], U32)
        em = keep("em", [P, NT, N_EXPERTS])
        ev8 = keep("ev8", [P, NT, 8])
        ei8 = keep("ei8", [P, NT, 8], U32)
        eneg = keep("eneg", [P, NT])
        e21 = keep("e21", [P, NT])
        wt = keep("wt", [P, 2, NT])
        eid = keep("eid", [P, NT, 2])
        chosen = keep("chosen", [P, 2, NT, N_EXPERTS])
        assigned = keep("assigned", [P, NT, N_EXPERTS])
        counts = keep("counts", [P, N_EXPERTS])
        starts = keep("starts", [P, N_EXPERTS])
        place_of = keep("place_of", [P, NT, N_EXPERTS])
        slot = keep("slot", [P, 2, NT])
        most = keep("most", [P, 1])
        starts_i = keep("starts_i", [1, N_EXPERTS], I32)
        most_i = keep("most_i", [1, 1], I32)

        y_sorted = nc.dram_tensor("y_sorted", (SLOTS_PAD, D), F32, kind="Internal").ap()

        QK = N_QK * DH
        sga = acts("sga", [P, KD, T], 0)
        qaT = acts("qaT", [P, NA_HEADS // 2, T], 8)
        kaT = acts("kaT", [P, NA_HEADS // 2, T], 12)
        va = acts("va", [P, NT, NA_HEADS * DH], 16)
        qk = acts("qk", [P, NT, QK], 20)
        vb = acts("vb", [P, NT, KV_HEADS * DH], 25)
        qk_sq = acts("qk_sq", [P, NT, QK], 26)
        qk_rot = acts("qk_rot", [P, NT, QK], 31)
        yaT = acts("yaT", [P, NA_HEADS // 2, T], 26)
        ybT = acts("ybT", [P, GQA_HEADS // 2, T], 30)
        qbT = acts("qbT", [P, GQA_HEADS // 2, T], 36)
        kk = acts("kk", [P, NT, KV_HEADS, 2, DH], 40)
        kbT = acts("kbT", [P, KV_HEADS, T], 42)
        sgb = acts("sgb", [P, KD, T], 44)
        rel_bias = acts("rel_bias", [P, NT, NA_HEADS, T], 52)
        prob_a = acts("prob_a", [P, NT, T], 68)
        prob_b = acts("prob_b", [P, NT, T], 70)
        prob_aT = acts("prob_aT", [P, NT, T], 72)
        prob_bT = acts("prob_bT", [P, NT, T], 74)
        rpb_wide = nc.dram_tensor("rpb_wide", (GRID_W, NA_HEADS, RPB_ROWS, GRID_W), F32, kind="Internal").ap()
        cos_gain = acts("cos_gain", [P, 2, NT, DH], 76)
        sin_gain = acts("sin_gain", [P, 2, NT, DH], 77)
        qk_ss_at = place[0]
        qk_ss = keep("qk_ss", [P, NT * N_QK])
        qk_rs = keep("qk_rs", [P, NT * N_QK])
        top_a = keep("top_a", [P, NT])
        top_b = keep("top_b", [P, NT])
        sum_a = keep("sum_a", [P, NT])
        sum_b = keep("sum_b", [P, NT])

        qT = acts("qT", [P, HP, T], 16)
        keysT = acts("keysT", [P, HP, NKEYS], 52)
        sc = acts("sc", [P, NT, HP, NKEYS], 60)
        cand = acts("cand", [P, NT, PEER_HEADS, TOPK, TOPK], 32)
        ts = acts("ts", [P, NT, HP, TOPK], 48)
        ti = acts("ti", [P, NT, HP, TOPK], 50, U32)
        match = acts("match", [P, HK, TOPK], 16)
        tif = acts("tif", [P, NT, HP, TOPK], 24)
        bpos = acts("bpos", [P, NT, HK], 26, U32)
        bdig = acts("bdig", [P, 2, NT, HK], 27, U32)
        bdigf = acts("bdigf", [P, 2, NT, HK], 29)
        raw = [at(f"raw{s}", [P, CJ * KD * NKEYS], ARENA + 8192 * s) for s in range(RAW_SLOTS)]
        rest = [at(f"rest{s}", [P, CJ * KD * NKEYS], ARENA + 8192 * s, F32R) for s in range(RAW_SLOTS)]
        lead = [at(f"lead{b}", [P, CJ * KD * NKEYS], ARENA + 24576 + 8192 * b, F32R) for b in range(2)]
        WORK = ARENA + 40960
        best = at("best", [P, NT, HK], WORK)
        ij = at("ij", [P, 2, NT, HK], WORK + 1024)
        bestT = at("bestT", [P, T], WORK + 3072)
        ijT = at("ijT", [P, 2, T], WORK + 4096)
        hot = [at(f"hot{b}", [P, 2, GT, NKEYS], ARENA + 24576 + 4096 * b) for b in range(HOTS)]
        hid_hi = [at(f"hid_hi{b}", [P, CJ, T], WORK + 2048 * b, F32R) for b in range(2)]
        hid_lo = [at(f"hid_lo{b}", [P, CJ, T], WORK + 4096 + 2048 * b, F32R) for b in range(2)]
        gain_f = at("gain_f", [P, D], NT_AT)
        A = at("A", [P, NKEYS, T], ARENA + 3 * 16384)
        nT_lo = at("nT_lo", [P, KD, T], NT_AT, F32R)
        assert DEAD_AT + 4 * KD * T <= qk_ss_at
        best_sum = keep("best_sum", [P, NT * PEER_HEADS])
        cur_g = keep("cur_g", [P, HOTS, GT])
        assert place[0] <= ARENA

        bank = [ctx.enter_context(nc.psum_tensor(f"bank{i}", [P, 512], F32)) for i in range(8)]

        def sem(name):
            return ctx.enter_context(nc.semaphore(name))

        x_in = sem("x_in")
        const_in = sem("const_in")
        rows_in = sem("rows_in")
        ws_in = sem("ws_in")
        ring_full = [sem(f"ring_full{s}") for s in range(RING)]
        h_ready = sem("h_ready")
        stat_sum = sem("stat_sum")
        stat_mean = sem("stat_mean")
        stat_root = sem("stat_root")
        xhat_ready = sem("xhat_ready")
        xhat_turned = sem("xhat_turned")
        nT_act = sem("nT_act")
        nT_dve = sem("nT_dve")
        half_hi = sem("half_hi")
        half_rest = sem("half_rest")
        half_hi_used = sem("half_hi_used")
        dve_step = sem("dve_step")
        act_step = sem("act_step")
        lb_diff = sem("lb_diff")
        lb_sig = sem("lb_sig")
        proj_done = sem("proj_done")
        proj_act = sem("proj_act")
        proj_dve = sem("proj_dve")
        f_ready = sem("f_ready")
        lf_ready = sem("lf_ready")
        d_ready = sem("d_ready")
        exp_ready = sem("exp_ready")
        qk_zero = sem("qk_zero")
        qk_ready = sem("qk_ready")
        sc_done = sem("sc_done")
        sc_masked = sem("sc_masked")
        kl_turned = sem("kl_turned")
        kl_ready = sem("kl_ready")
        state_done = sem("state_done")
        state_ready = sem("state_ready")
        o_done = sem("o_done")
        o_sq = sem("o_sq")
        o_ms = sem("o_ms")
        o_sd = sem("o_sd")
        on_ready = sem("on_ready")
        on_turned = sem("on_turned")
        v_ms = sem("v_ms")
        v_sd = sem("v_sd")
        vh_ready = sem("vh_ready")
        ws_masked = sem("ws_masked")
        mixed_done = sem("mixed_done")
        mix_g = sem("mix_g")
        mix_h = sem("mix_h")
        out1_done = sem("out1_done")
        stored = sem("stored")

        gain_in = sem("gain_in")
        xs_zero = sem("xs_zero")
        router_done = sem("router_done")
        gneg_ready = sem("gneg_ready")
        gsum_ready = sem("gsum_ready")
        eneg_ready = sem("eneg_ready")
        e21_ready = sem("e21_ready")
        assign_ready = sem("assign_ready")
        rank_done = sem("rank_done")
        starts_ready = sem("starts_ready")
        pick_ready = sem("pick_ready")
        xhat_lead_ready = sem("xhat_lead_ready")
        xhat_rest_ready = sem("xhat_rest_ready")
        gather_done = sem("gather_done")
        xs_act = sem("xs_act")
        xs_dve = sem("xs_dve")
        wt_turned = sem("wt_turned")
        slot_wt_ready = sem("slot_wt_ready")
        w_lead_ready = sem("w_lead_ready")
        w_rest_ready = sem("w_rest_ready")
        w_lead_used = sem("w_lead_used")
        w_used = sem("w_used")
        gate_low = sem("gate_low")
        up_low = sem("up_low")
        gate_sum = sem("gate_sum")
        up_sum = sem("up_sum")
        down_done = sem("down_done")
        x_ready = sem("x_ready")
        x_hi_ready = sem("x_hi_ready")
        x_lo_ready = sem("x_lo_ready")
        sil_ready = sem("sil_ready")
        hid_ready = sem("hid_ready")
        hid_turned = sem("hid_turned")
        hT_ready = sem("hT_ready")
        y_act = sem("y_act")
        y_dve = sem("y_dve")
        y_stored = sem("y_stored")
        many_gate, many_up, many_down = gate_low, up_low, gate_sum
        many_stored = sem("many_stored")
        y_rows_in = [sem(f"y_rows_in{b}") for b in range(2)]
        moe_done = sem("moe_done")

        rpb_spread = sem("rpb_spread")
        bias_in = sem("bias_in")
        p2_done = sem("p2_done")
        p2_act = sem("p2_act")
        p2_dve = sem("p2_dve")
        qk_ms = sem("qk_ms")
        qk_sd = sem("qk_sd")
        qk_roped = sem("qk_roped")
        qk_turned = sem("qk_turned")
        qbT_ready = sem("qbT_ready")
        kbT_ready = sem("kbT_ready")
        gate2_done = sem("gate2_done")
        gate2_act = sem("gate2_act")
        sg_ready = sem("sg_ready")
        sa_done = sem("sa_done")
        ta_ready = sem("ta_ready")
        ea_ready = sem("ea_ready")
        pa_ready = sem("pa_ready")
        pa_turned = sem("pa_turned")
        paT_ready = sem("paT_ready")
        ya_done = sem("ya_done")
        ya_ready = sem("ya_ready")
        sb_done = sem("sb_done")
        tb_ready = sem("tb_ready")
        eb_ready = sem("eb_ready")
        pb_ready = sem("pb_ready")
        pb_turned = sem("pb_turned")
        pbT_ready = sem("pbT_ready")
        yb_done = sem("yb_done")
        yb_ready = sem("yb_ready")
        branch_done = sem("branch_done")
        merged_ready = sem("merged_ready")
        out2_done = sem("out2_done")

        keys_in = sem("keys_in")
        query_done = sem("query_done")
        query_act = sem("query_act")
        query_dve = sem("query_dve")
        score_done = sem("score_done")
        score_ready = sem("score_ready")
        routed = sem("routed")
        best_exp = sem("best_exp")
        gates_ready = sem("gates_ready")
        route_turned = sem("route_turned")
        route_ready = sem("route_ready")
        raw_full = [sem(f"raw_full{s}") for s in range(RAW_SLOTS)]
        chunk_used = sem("chunk_used")
        act_ready = sem("act_ready")
        lead_ready = sem("lead_ready")
        rest_ready = sem("rest_ready")
        hid_hi_ready = sem("hid_hi_ready")
        hid_lo_ready = sem("hid_lo_ready")
        hot_ready = sem("hot_ready")
        cur_ready = sem("cur_ready")
        hot_j_ready = sem("hot_j_ready")
        hot_i_step = sem("hot_i_step")
        gates_done = sem("gates_done")
        gated = sem("gated")
        gain_f_in = sem("gain_f_in")
        out_ready = sem("out_ready")

        def chain(eng, s):
            n = [0]

            def link(ins):
                n[0] += 1
                ins.then_inc(s, 1)
                eng.wait_ge(s, n[0])

            return link

        def slot_of(n):
            if n < CH_MOE:
                return n % IN1_SLOTS
            return n % RING if n < CH_IN2 else BLOCK2_SLOTS[(n - CH_IN2) % len(BLOCK2_SLOTS)]

        def former(n):
            return max([i for i in range(n) if slot_of(i) == slot_of(n)], default=CH_OUT1 - 1)

        def landed(n):
            return 16 * sum(slot_of(i) == slot_of(n) for i in range(n + 1))

        def ring_wait(eng, n):
            eng.wait_ge(ring_full[slot_of(n)], landed(n))

        def chunk_read(n):
            if n < CH_OUT1:
                return proj_done, 2 * (n + 1)
            if n < CH_MOE:
                return out1_done, 2 * (n - CH_OUT1 + 1)
            if n < CH_IN2:
                pair, i = divmod(n - CH_MOE, RING)
                j, kind = PAIR[i]
                if kind == 2:
                    return down_done, 2 * (2 * pair + j + 1)
                return w_used, 2 * (2 * pair + j) + kind + 1
            if n < CH_PROJ:
                i = n - CH_IN2
                return (p2_done, (2, 3, 5, 7, 9)[i]) if i < 5 else (gate2_done, 2 * (i - 4))
            if n < CH_OUT2:
                return branch_done, 7 + n - CH_PROJ
            if n < CH_WQ:
                return out2_done, 2 * (n - CH_OUT2 + 1)
            return query_done, 2 * (n - CH_WQ + 1)

        def quad(t):
            return t[:, :].rearrange("p (m n) -> p m n", m=4)

        def spread(ap, shape):
            return ap.broadcast_to(shape)

        H_COUNT = [0, 4, 8, 10, 14, 18]
        H_COUNT_0 = [0, 4, 7, 9, 14, 17]
        OTHER_TABLES = (2, 4, 5)

        def act_stats(act, n):
            if n in OTHER_TABLES:
                act.wait_ge(stat_root, n)
                act.activation(stat_warm[:, :], stat_sd[:, :], ACT.Sqrt)
            if n == 0:
                act.wait_ge(x_in, 16)
            else:
                act.wait_ge(h_ready, H_COUNT_0[n])
            act.activation(xhat[:, 0, :], h[:, 0, :], ACT.Square, accum_out=stat_ss[:, 0:1]).then_inc(stat_sum, 1)
            act.wait_ge(stat_mean, n + 1)
            act.activation(stat_sd[:, :], stat_ms[:, :], ACT.Sqrt).then_inc(stat_root, 1)

        def dve_stats(dve, link, n):
            if n == 0:
                dve.wait_ge(x_in, 16)
            else:
                dve.wait_ge(h_ready, H_COUNT[n])
            dve.scalar_tensor_tensor(xhat[:, 1, :], h[:, 1, :], 1.0, h[:, 1, :], ALU.mult, ALU.mult,
                                     accum_out=stat_ss[:, 1:2]).then_inc(stat_sum, 1)
            dve.wait_ge(stat_sum, NT * (n + 1))
            dve.tensor_scalar(stat_ms[:, :], stat_ss[:, :], 1.0 / D, EPS, ALU.mult, ALU.add).then_inc(stat_mean, 1)
            dve.wait_ge(stat_root, n + 1)
            link(dve.reciprocal(stat_rs[:, :], stat_sd[:, :]))

        def dve_xhat(dve):
            for t in range(NT):
                dve.tensor_scalar(xhat[:, t, :], h[:, t, :], stat_rs[:, t:t + 1], None,
                                  ALU.mult).then_inc(xhat_ready, 1)

        def pe_turn(pe, m):
            pe.wait_ge(xhat_ready, NT * (m + 1))
            for b in range(4):
                for k in (2 * b, 2 * b + 1):
                    for t in range(NT):
                        last = pe.transpose(bank[b][:, (k % 2) * T + t * P:(k % 2) * T + (t + 1) * P],
                                            xhat[:, t, k * P:(k + 1) * P], ident)
                last.then_inc(xhat_turned, 1)

        def act_nT(act, m, gain):
            for b in (0, 2):
                act.wait_ge(xhat_turned, 4 * m + b + 1)
                for k in (2 * b, 2 * b + 1):
                    last = act.activation(nT[:, k, :], bank[b][:, (k % 2) * T:(k % 2 + 1) * T], ACT.Copy,
                                          scale=pr(gain, k))
                last.then_inc(nT_act, 1)

        def dve_nT(dve, m, gain):
            for b in (1, 3):
                dve.wait_ge(xhat_turned, 4 * m + b + 1)
                for k in (2 * b, 2 * b + 1):
                    last = dve.tensor_scalar(nT[:, k, :], bank[b][:, (k % 2) * T:(k % 2 + 1) * T], pr(gain, k),
                                             None, ALU.mult)
                last.then_inc(nT_dve, 1)

        def wait_nT(eng, m):
            eng.wait_ge(nT_act, 4 + 2 * m)
            eng.wait_ge(nT_dve, 4 + 2 * m)

        SPLIT_TURN = {0: 0, 2: 6, 3: 10}

        def act_nT_lead(act, m, gain, nT_hi):
            for b in range(4):
                act.wait_ge(xhat_turned, 4 * m + b + 1)
                for k in (2 * b, 2 * b + 1):
                    last = act.activation(nT_hi[:, k, :], bank[b][:, (k % 2) * T:(k % 2 + 1) * T], ACT.Copy,
                                          scale=pr(gain, k))
                last.then_inc(nT_act, 1)

        def dve_nT_rest(dve, m, gain, nT_hi):
            for b in range(4):
                dve.wait_ge(nT_act, SPLIT_TURN[m] + b + 1)
                for k in (2 * b, 2 * b + 1):
                    last = dve.scalar_tensor_tensor(nT_lo[:, k, :], bank[b][:, (k % 2) * T:(k % 2 + 1) * T], pr(gain, k),
                                                    nT_hi[:, k, :].bitcast(F32), ALU.mult, ALU.subtract)
                last.then_inc(nT_dve, 1)

        def wait_nT_split(pe, m):
            pe.wait_ge(nT_act, SPLIT_TURN[m] + 4)
            pe.wait_ge(nT_dve, SPLIT_TURN[m] + 4)

        def half_view(tile, i, half):
            width = SPLIT[i][1]
            first = 0 if half is None else 4 * half * width
            return tile[:, first:first + 4 * width].rearrange("p (k f) -> p k f", k=4)

        def half_lead(i, half):
            return half_view((half_lead1 if i < SPLIT_IN2 else half_lead2)[half], i, None)

        def act_half(act, i, half):
            n, chunk = 2 * i + half, SPLIT[i][0]
            ring_wait(act, chunk)
            if n >= 2:
                act.wait_ge(half_hi_used, n - 1)
                act.wait_ge(half_rest, n - 1)
            act.activation(half_lead(i, half), half_view(ring[slot_of(chunk)], i, half), ACT.Copy).then_inc(half_hi, 1)

        def pool_half(pool, i, half):
            slot = slot_of(SPLIT[i][0])
            pool.wait_ge(half_hi, 2 * i + half + 1)
            pool.tensor_tensor(half_view(ring_rest[slot], i, half), half_view(ring[slot], i, half),
                               half_lead(i, half).bitcast(F32), ALU.subtract).then_inc(half_rest, 1)

        def pe_half(pe, i, half, outs, done):
            rest_in = half_view(ring_rest[slot_of(SPLIT[i][0])], i, half)
            lead_in = half_lead(i, half)
            x_hi = nT_hi1 if i < SPLIT_IN2 else nT_hi

            def product(dst, by_channel, tile, w, x, k, start, stop):
                part = slice(tile * P, (tile + 1) * P)
                if by_channel:
                    return pe.matmul(dst, w[:, k, part], x[:, 4 * half + k, :], start=start, stop=stop)
                return pe.matmul(dst, x[:, 4 * half + k, part], w[:, k, :], start=start, stop=stop)

            pe.wait_ge(half_hi, 2 * i + half + 1)
            begins = True
            for dst, by_channel, tile, ends in outs:
                for x in (x_hi, nT_lo):
                    for k in range(4):
                        start = begins and half == 0 and x is x_hi and k == 0
                        last = product(dst, by_channel, tile, lead_in, x, k, start, False)
                begins = ends
            last.then_inc(half_hi_used, 1)
            pe.wait_ge(half_rest, 2 * i + half + 1)
            for dst, by_channel, tile, ends in outs:
                for k in range(4):
                    last = product(dst, by_channel, tile, rest_in, x_hi, k, False, half == 1 and k == 3 and ends)
                if half == 1 and ends:
                    last.then_inc(done, 1)

        def pe_columns(pe, dst, s, m):
            for k in range(KD):
                last = pe.matmul(dst, ring8(s)[:, k, m * P:(m + 1) * P], nT[:, k, :],
                                 start=(k == 0), stop=(k == KD - 1))
            return last

        def pe_rows(pe, dst, s, t, width=512):
            w = ring[s][:, 0:KD * width].rearrange("p (k f) -> p k f", k=KD)
            for k in range(KD):
                last = pe.matmul(dst, nT[:, k, t * P:(t + 1) * P], w[:, k, :],
                                 start=(k == 0), stop=(k == KD - 1))
            return last

        def pair_fill(pair, i):
            return 16 * pair + landed(CH_MOE + i)

        W_SLOT = [(CH_MOE + i) % RING for i in range(RING)]
        GATHER_BANK = [0, 1, 2, 3, 6, 7, 0, 1]

        IN1_BANK = [4, 5, 6, 7, 0, 1, 2, 3, 4, 5, 6, 7]
        OUT1_BANK = [5, 6, 7, 0]

        QUERY_BANK = [4, 5, 6, 7, 0, 1, 2, 3]
        def fill(i, at_n):
            return 16 * (at_n // RAW_SLOTS + 1) + 16 * (UNROLL // RAW_SLOTS) * i

        BRANCH_BANK = [(0, 1, 2, 3), (5, 6, 7, 4)]

        block = ctx.enter_context(nc.Block())

        @block.sync
        def _(sp):
            def load(n, src, cols=CHUNK_COLS, k=8):
                if n >= IN1_SLOTS:
                    sp.wait_ge(*chunk_read(former(n)))
                dst = ring[slot_of(n)][:, 0:cols].rearrange("p (k f) -> p k f", k=k)
                sp.dma_start(dst, src).then_inc(ring_full[slot_of(n)], 16)

            sp.dma_start(h[:, :, :], dram["x"].rearrange("(t p) d -> p t d", p=P)).then_inc(x_in, 16)
            w_in = dram["w_in"]
            for n in range(2):
                f = IN1_ORDER[n] * 512
                load(n, w_in[:, f:f + 512].rearrange("(k p) f -> p k f", p=P))
                if n == 0:
                    sp.dma_start(const[:, :], dram["const"]).then_inc(const_in, 16)
                    sp.dma_start(param[:, :], dram["param"]).then_inc(const_in, 16)
            first = ROW_AT["b_s"][0]
            sp.dma_start(rows_qk[:, :], dram["rows"][:, 0:first].broadcast_to([P, first])).then_inc(rows_in, 16)
            sp.dma_start(rows[:, :], dram["rows"][:, first:].broadcast_to([P, ROW_N - first])).then_inc(rows_in, 16)
            sp.dma_start(w_sT[:, :, :], dram["w_sT"].rearrange("j (g i) -> j g i", g=HEADS)).then_inc(ws_in, 16)
            sp.dma_start(w_router[:, :, 0:N_GROUPS],
                         dram["w_group_router"].rearrange("(k p) f -> p k f", p=P)).then_inc(rows_in, 16)
            sp.dma_start(w_router[:, :, N_GROUPS:],
                         dram["w_expert_router"].rearrange("(k p) f -> p k f", p=P)).then_inc(rows_in, 16)
            for n in range(2, 6):
                f = IN1_ORDER[n] * 512
                load(n, w_in[:, f:f + 512].rearrange("(k p) f -> p k f", p=P))
            for n in range(2):
                load(CH_OUT1 + n, dram["w_out"][:, n * 512:n * 512 + 512].rearrange("(k p) f -> p k f", p=P))
            rpb = dram["rpb"]
            for i in range(RPB_ROWS):
                first = (RPB_H // 2 - (KROWS - 1) + i) * RPB_W + RPB_W // 2
                src = bass.AP(rpb.tensor, first, [[RPB_H * RPB_W, NA_HEADS], [-1, GRID_W], [1, GRID_W]])
                sp.dma_start(rpb_wide[:, :, i, :].rearrange("c a d -> a c d"), src).then_inc(rpb_spread, 16)
            sp.wait_ge(h_ready, 4)
            sp.dma_start(gain_row[:, :], dram["final_gain"].broadcast_to([P, D])).then_inc(gain_in, 16)

            def expert_source(i, pair):
                j, kind = PAIR[i]
                e = 2 * pair + j
                if kind == 2:
                    return dram["w_down"][bass.ds(e, 1)].rearrange("e (k p) f -> p (e k) f", p=P), 4
                w = dram["w_gate"] if kind == 0 else dram["w_up"]
                return w[bass.ds(e, 1)].rearrange("e (k p) f -> p (e k) f", p=P), 8

            for i in range(RING):
                src, k = expert_source(i, 0)
                load(CH_MOE + i, src, k=k)
            with sp.Fori(1, PAIRS) as pair:
                for i, (j, kind) in enumerate(PAIR):
                    s = (CH_MOE + i) % RING
                    if kind == 2:
                        sp.wait_ge(down_done, 4 * pair + 2 * j - 2)
                    else:
                        sp.wait_ge(w_used, 4 * pair + 2 * j + kind - 3)
                    src, k = expert_source(i, pair)
                    dst = ring[s][:, :].rearrange("p (k f) -> p k f", k=k)
                    sp.dma_start(dst, src).then_inc(ring_full[s], 16)
            for i, (first, width) in enumerate(IN2_COLS):
                if i == 2:
                    for b in range(2):
                        sp.wait_ge(y_rows_in[b], 16)
                load(CH_IN2 + i, dram["w_in_2"][:, first:first + width].rearrange("(k p) f -> p k f", p=P), KD * width)
                if i == RING - 1:
                    sp.wait_ge(w_used, 2 * N_EXPERTS)
                    sp.wait_ge(rpb_spread, 16 * RPB_ROWS)
                    for r in range(KROWS):
                        t, lo = r // 2, (r % 2) * GRID_W
                        first = KROWS - 1 - r
                        sp.dma_start(rel_bias[lo:lo + GRID_W, t, :, :],
                                     rpb_wide[:, :, first:first + KROWS, :].rearrange("c a k d -> c a (k d)")).then_inc(bias_in, 16)
            for i, name in enumerate(("w_proj_a", "w_proj_b")):
                load(CH_PROJ + i, dram[name].rearrange("(k p) f -> p k f", p=P), k=4)
            for i in range(2):
                load(CH_OUT2 + i, dram["w_out_2"][:, i * 512:i * 512 + 512].rearrange("(k p) f -> p k f", p=P))
            for i in range(4):
                load(CH_WQ + i, dram["w_q"][:, i * 512:i * 512 + 512].rearrange("(k p) f -> p k f", p=P))
            sp.wait_ge(h_ready, H_COUNT[4])
            sp.dma_start(keysT[:, :, :], dram["keysT"].rearrange("c (a n) -> c a n", n=NKEYS)).then_inc(keys_in, 16)

            def stream(slot, table, chunk):
                sp.dma_start(raw[slot][:, :], dram[table][bass.ds(chunk, 1)].rearrange("e p f -> p (e f)")).then_inc(raw_full[slot], 16)

            sp.wait_ge(*chunk_read(CH_END - 1))
            for n in range(RAW_SLOTS):
                stream(n, "u", n)

            def stream_next(n, slot, table):
                sp.wait_ge(chunk_used, n - RAW_SLOTS + 1)
                stream(slot, table, n if table == "u" else n - PEER_CHUNKS)

            turns = PEER_CHUNKS // RAW_SLOTS
            with sp.Fori(1, turns) as i:
                for slot in range(RAW_SLOTS):
                    stream_next(i * RAW_SLOTS + slot, slot, "u")
            for n in range(turns * RAW_SLOTS, (turns + 1) * RAW_SLOTS):
                stream_next(n, n % RAW_SLOTS, "u" if n < PEER_CHUNKS else "v")
            with sp.Fori(turns + 1, 2 * PEER_CHUNKS // RAW_SLOTS) as i:
                for slot in range(RAW_SLOTS):
                    stream_next(i * RAW_SLOTS + slot, slot, "v")
            for n in range(2 * PEER_CHUNKS // RAW_SLOTS * RAW_SLOTS, 2 * PEER_CHUNKS):
                stream_next(n, n % RAW_SLOTS, "v")
            sp.dma_start(gain_f[:, :], dram["norm_f_g"].broadcast_to([P, D])).then_inc(gain_f_in, 16)
            for t in range(NT):
                sp.wait_ge(out_ready, t + 1)
                sp.dma_start(out[t * P:(t + 1) * P, :], h[:, t, :]).then_inc(stored, 16)
            sp.wait_ge(stored, 16 * NT)

        @block.gpsimd
        def _(pool):
            pool.memset(hQE[:, :, :], 0.0).then_inc(qk_zero, 1)
            pool.memset(hQO[:, :, :], 0.0).then_inc(qk_zero, 1)
            pool.memset(hSC[:, :, :, :], 0.0).then_inc(qk_zero, 1)
            pool.wait_ge(ws_in, 16)
            pool.wait_ge(qk_zero, 3)
            pool.memset(w_sT[CHUNK:P, :, 0:CHUNK], 0.0).then_inc(ws_masked, 1)
            pool.wait_ge(ws_masked, 1)
            for i in range(SPLIT_IN2):
                for half in range(2):
                    pool_half(pool, i, half)
            pool.wait_ge(h_ready, 4)
            pool.memset(xs[:, :, SLOTS:], 0.0).then_inc(xs_zero, 1)
            pool.wait_ge(xhat_lead_ready, 1)
            pool.tensor_tensor(xhat_rest[:, :, :], xhat[:, :, :], xhat_lead[:, :, :].bitcast(F32),
                               ALU.subtract).then_inc(xhat_rest_ready, 1)
            pool.wait_ge(xs_act, KD // 2)
            pool.wait_ge(xs_dve, KD // 2)
            pool.wait_ge(xs_zero, 1)
            pool.wait_ge(starts_ready, 1)
            load_most = pool.value_load(most_i[0:1, 0:1], min_val=0, max_val=T)
            with pool.If(load_most > BLOCK):
                def many_copies(e, peeled):
                    first = pool.value_load(starts_i[0:1, bass.ds(e, 1)], min_val=0, max_val=SLOTS)
                    for b in range(BLOCKS_MAX):
                        if b or not peeled:
                            pool.wait_ge(many_up, e * BLOCKS_MAX + b)
                        pool.tensor_copy(x_blk[0][:, :, :], xs[:, :, bass.ds(first + b * BLOCK, BLOCK)]).then_inc(x_ready, 1)

                many_copies(0, True)
                with pool.Fori(1, N_EXPERTS) as e:
                    many_copies(e, False)
            with pool.Else():
                def expert_input(e, j, peeled):
                    first = pool.value_load(starts_i[0:1, bass.ds(e, 1)], min_val=0, max_val=SLOTS)
                    pool.tensor_copy(x_blk[j][:, :, :], xs[:, :, bass.ds(first, BLOCK)]).then_inc(x_ready, 1)
                    if not peeled:
                        pool.wait_ge(w_used, 2 * e - 2)
                    pool.wait_ge(x_hi_ready, e + 1)
                    pool.tensor_tensor(x_two[j][:, :, BLOCK:], x_blk[j][:, :, :], x_two[j][:, :, 0:BLOCK].bitcast(F32),
                                       ALU.subtract).then_inc(x_lo_ready, 1)

                for j in range(2):
                    expert_input(j, j, True)
                with pool.Fori(1, PAIRS) as pair:
                    for j in range(2):
                        expert_input(2 * pair + j, j, False)
            for i in range(len(IN2_COLS)):
                for half in range(2):
                    pool_half(pool, SPLIT_IN2 + i, half)
            for i in range(SPLIT_WQ, len(SPLIT)):
                for half in range(2):
                    pool_half(pool, i, half)

            def pool_rest(n, at_n):
                slot, b = at_n % RAW_SLOTS, at_n % 2
                pool.wait_ge(lead_ready, n + 1)
                pool.tensor_tensor(rest[slot][:, :], raw[slot][:, :], lead[b][:, :].bitcast(F32),
                                   ALU.subtract).then_inc(rest_ready, 1)

            for n in range(ROUTING % UNROLL):
                pool_rest(n, n)
            with pool.Fori(0, ROUTING // UNROLL) as i:
                for s in range(UNROLL):
                    at_n = ROUTING % UNROLL + s
                    pool_rest(at_n + UNROLL * i, at_n)
            pool.wait_ge(route_ready, 1)

            def weigh_hot(g, b):
                pool.tensor_copy(cur_g[:, b, :], bestT[:, bass.ds(g * GT, GT)]).then_inc(cur_ready, 1)
                pool.wait_ge(cur_ready, g + 1)
                pool.wait_ge(hot_ready, g + 1)
                pool.tensor_tensor(hot[b][:, 1, :, :], hot[b][:, 1, :, :],
                                   spread(cur_g[:, b, :].unsqueeze(2), [P, GT, NKEYS]), ALU.mult).then_inc(hot_j_ready, 1)

            with pool.Fori(0, GROUPS // HOTS) as turn:
                for b in range(HOTS):
                    weigh_hot(HOTS * turn + b, b)

        @block.scalar
        def _(act):
            link = chain(act, act_step)
            act_stats(act, 0)
            for half in range(2):
                act_half(act, 0, half)
            act.wait_ge(const_in, 32)
            act_nT_lead(act, 0, "gain1", nT_hi1)
            act.wait_ge(lb_diff, 1)
            act.activation(lb[:, :], lbd[:, :], ACT.Sigmoid).then_inc(lb_sig, 1)
            for use, dst in enumerate((hF, hF, hQ, hQ, hG, hG)):
                if use % 2 == 0:
                    for half in range(2):
                        act_half(act, use // 2 + 1, half)
                act.wait_ge(proj_done, use + 1)
                half = use % 2
                act.activation(dst[:, 2 * half:2 * half + 2, :].rearrange("p a t -> p (a t)"),
                               bank[IN1_BANK[use]][:, :], ACT.Sigmoid).then_inc(proj_act, 1)
            for half in range(2):
                act_half(act, 4, half)
            for t in range(NT):
                act.wait_ge(proj_done, 7 + t)
                act.activation(hI[:, t, :], bank[IN1_BANK[6 + t]][:, :], ACT.Copy).then_inc(proj_act, 1)
            for half in range(2):
                act_half(act, 5, half)
            act.wait_ge(f_ready, 1)
            act.activation(hF[:, :, :], hF[:, :, :], ACT.Ln).then_inc(lf_ready, 1)
            act.wait_ge(d_ready, 1)
            act.activation(hF[:, :, :], hD1[:, :, :], ACT.Exp).then_inc(exp_ready, 1)
            act.activation(hD1[:, :, :], hD1[:, :, :], ACT.Exp, scale=-1.0).then_inc(exp_ready, 1)
            act.wait_ge(d_ready, 2)
            act.activation(hD2[:, :, :], hD2[:, :, :], ACT.Exp).then_inc(exp_ready, 1)
            act.activation(hEB[:, :, :], hB[:, :, :], ACT.Exp).then_inc(exp_ready, 1)
            for t in range(NT):
                act.wait_ge(proj_done, 9 + t)
                act.activation(mV[:, t, :], bank[IN1_BANK[8 + t]][:, :], ACT.Gelu).then_inc(proj_act, 1)
            for half in range(2):
                act.wait_ge(proj_done, 11 + half)
                act.activation(mU[:, 2 * half:2 * half + 2, :].rearrange("p a t -> p (a t)"),
                               bank[IN1_BANK[10 + half]][:, :], ACT.Gelu).then_inc(proj_act, 1)
            for t in range(NT):
                act.wait_ge(kl_turned, t + 1)
                act.activation(hKL[:, t, :, :], quad(bank[2 + t]), ACT.Copy).then_inc(kl_ready, 1)
            act.wait_ge(v_ms, 1)
            act.activation(vrs[:, :], vss[:, :], ACT.Sqrt).then_inc(v_sd, 1)
            act.wait_ge(vh_ready, 1)
            for t in range(NT):
                act.wait_ge(o_done, t + 1)
                act.activation(mSQ[:, t, :], bank[t][:, :], ACT.Square).then_inc(o_sq, 1)
            act.wait_ge(o_ms, 1)
            act.activation(ors[:, :], oss[:, :], ACT.Sqrt).then_inc(o_sd, 1)
            act_stats(act, 1)
            act_nT(act, 1, "gain2")
            act.activation(xhat_lead[:, :, :], xhat[:, :, :], ACT.Copy).then_inc(xhat_lead_ready, 1)
            act.wait_ge(gneg_ready, 1)
            for t in range(NT):
                act.activation(gex[:, t, :], lg[:, t, 0:N_GROUPS], ACT.Exp, bias=gneg[:, t:t + 1],
                               accum_out=gsum[:, t:t + 1]).then_inc(gsum_ready, 1)
            act.wait_ge(eneg_ready, 1)
            for t in range(NT):
                act.activation(e21[:, t:t + 1], ev8[:, t, 1:2], ACT.Exp,
                               bias=eneg[:, t:t + 1]).then_inc(e21_ready, 1)
            for k in range(0, KD, 2):
                act.wait_ge(gather_done, k + 1)
                act.activation(xs[:, k, 0:SLOTS], bank[GATHER_BANK[k]][:, :], ACT.Copy,
                               scale=pr("gain2", k)).then_inc(xs_act, 1)
            for half in range(2):
                act.wait_ge(wt_turned, half + 1)
                act.activation(slot_wt[:, 2 * half:2 * half + 2, :].rearrange("p s t -> p (s t)"),
                               bank[4 + half][:, :], ACT.Copy).then_inc(slot_wt_ready, 1)
            act.wait_ge(starts_ready, 1)
            load_most = act.value_load(most_i[0:1, 0:1], min_val=0, max_val=T)
            with act.If(load_most > BLOCK):
                def many_scalar(e, peeled):
                    first = act.value_load(starts_i[0:1, bass.ds(e, 1)], min_val=0, max_val=SLOTS)
                    for b in range(BLOCKS_MAX):
                        n = e * BLOCKS_MAX + b
                        act.wait_ge(many_gate, n + 1)
                        act.activation(hid[0][:, :], bank[0][0:BLOCK, :], ACT.Silu).then_inc(sil_ready, 1)
                        act.wait_ge(hid_turned, n + 1)
                        act.activation(hT[0][:, :, :].rearrange("p f s -> p (f s)"), bank[4][:, 0:4 * BLOCK],
                                       ACT.Copy).then_inc(hT_ready, 1)
                        act.wait_ge(many_down, 2 * n + 1)
                        if b or not peeled:
                            act.wait_ge(many_stored, 16 * n)
                        act.activation(y_blk[0][:, 0:512], bank[6][0:BLOCK, :], ACT.Copy).then_inc(y_act, 1)
                        act.wait_ge(y_act, n + 1)
                        act.wait_ge(y_dve, n + 1)
                        act.dma_start(y_sorted[bass.ds(first + b * BLOCK, BLOCK)], y_blk[0][:, :]).then_inc(many_stored, 16)

                many_scalar(0, True)
                with act.Fori(1, N_EXPERTS) as e:
                    many_scalar(e, False)
                act.wait_ge(many_stored, 16 * N_EXPERTS * BLOCKS_MAX)
                act.nop().then_inc(y_stored, 16 * N_EXPERTS)
            with act.Else():
                def split_lead(e, pair, j, kind, peeled, halves=range(2)):
                    slot = W_SLOT[3 * j + kind]
                    act.wait_ge(ring_full[slot], pair_fill(pair, 3 * j + kind))
                    for half in halves:
                        n = 4 * e + 2 * kind + half
                        if kind or not peeled:
                            act.wait_ge(w_lead_used, n - 1)
                            act.wait_ge(w_rest_ready, n - 1)
                        act.activation(w_lead[half][:, :, :], ring8(slot)[:, 4 * half:4 * half + 4, :],
                                       ACT.Copy).then_inc(w_lead_ready, 1)

                def low(e, j, kind):
                    act.wait_ge(w_used, 2 * e + kind + 1)
                    act.activation((hid, upv)[kind][j][:, :], bank[2 * kind + j][BLOCK:P, :],
                                   ACT.Copy).then_inc((gate_low, up_low)[kind], 1)

                def silu(e, j):
                    act.wait_ge(gate_sum, e + 1)
                    act.activation(hid[j][:, :], hid[j][:, :], ACT.Silu).then_inc(sil_ready, 1)

                def turned(e, j):
                    act.wait_ge(hid_turned, e + 1)
                    act.activation(hT[j][:, :, :].rearrange("p f s -> p (f s)"), bank[4 + j][:, 0:4 * BLOCK],
                                   ACT.Copy).then_inc(hT_ready, 1)

                def copy_store(e, pair, j, peeled):
                    act.wait_ge(down_done, 2 * e + 1)
                    if not peeled:
                        act.wait_ge(y_stored, 16 * e - 16)
                    act.activation(y_blk[j][:, 0:512], bank[6][0:BLOCK, :], ACT.Copy).then_inc(y_act, 1)
                    first = act.value_load(starts_i[0:1, bass.ds(e, 1)], min_val=0, max_val=SLOTS)
                    act.wait_ge(y_act, e + 1)
                    act.wait_ge(y_dve, e + 1)
                    if j or not peeled:
                        act.wait_ge(y_stored, 16 * e)
                    act.dma_start(y_sorted[bass.ds(first, BLOCK)], y_blk[j][:, :]).then_inc(y_stored, 16)

                def expert_scalar(e, pair, j, peeled, former_peeled):
                    first = peeled and j == 0
                    if first:
                        act.wait_ge(gather_done, KD)
                        split_lead(e, pair, j, 0, True, [0])
                    act.wait_ge(x_ready, e + 1)
                    act.activation(x_two[j][:, :, 0:BLOCK], x_blk[j][:, :, :], ACT.Copy).then_inc(x_hi_ready, 1)
                    split_lead(e, pair, j, 0, first, [1] if first else range(2))
                    if not peeled:
                        copy_store(e - 2, pair - 1, j, former_peeled)
                    split_lead(e, pair, j, 1, False)
                    if j or not peeled:
                        turned(e - 1, 1 - j)
                    low(e, j, 0)
                    silu(e, j)
                    low(e, j, 1)

                for j in range(2):
                    expert_scalar(j, 0, j, True, True)
                for j in range(2):
                    expert_scalar(2 + j, 1, j, False, True)
                with act.Fori(2, PAIRS) as pair:
                    for j in range(2):
                        expert_scalar(2 * pair + j, pair, j, False, False)
                copy_store(N_EXPERTS - 2, PAIRS - 1, 0, False)
                turned(N_EXPERTS - 1, 1)
                copy_store(N_EXPERTS - 1, PAIRS - 1, 1, False)
            act.wait_ge(y_stored, 16 * N_EXPERTS)
            for b in range(2):
                act.dma_start(y_rows[:, 2 * b:2 * b + 2, :],
                              y_sorted[b * T:(b + 1) * T].rearrange("(s p) d -> p s d", p=P)).then_inc(y_rows_in[b], 16)
            act_stats(act, 2)
            act_stats(act, 3)
            act_half(act, SPLIT_IN2 + 0, 0)
            act_half(act, SPLIT_IN2 + 0, 1)
            act_nT_lead(act, 2, "gain12", nT_hi)
            for i in (1, 2):
                for half in range(2):
                    act_half(act, SPLIT_IN2 + i, half)
            for t in range(NT):
                act.wait_ge(p2_done, t + 1)
                act.activation(qk_sq[:, t, 0:512], bank[4 + t][:, :], ACT.Square)
                act.activation(qk[:, t, 0:512], bank[4 + t][:, :], ACT.Copy).then_inc(p2_act, 1)
            act.wait_ge(p2_done, 3)
            kv = bank[6][:, :].rearrange("p (t f) -> p t f", t=NT)
            act.activation(qk_sq[:, :, 512:], kv[:, :, 0:KV_HEADS * DH], ACT.Square)
            act.activation(qk[:, :, 512:], kv[:, :, 0:KV_HEADS * DH], ACT.Copy)
            act.activation(vb[:, :, :], kv[:, :, KV_HEADS * DH:], ACT.Copy).then_inc(p2_act, 1)
            for half in range(2):
                act_half(act, SPLIT_IN2 + 3, half)
            act.wait_ge(qk_ms, 1)
            act.activation(qk_rs[:, :], qk_ss[:, :], ACT.Sqrt).then_inc(qk_sd, 1)
            for half in range(2):
                act_half(act, SPLIT_IN2 + 4, half)
            for i in range(2):
                act.wait_ge(p2_done, 6 + i)
                act.activation(kaT[:, 2 * i:2 * i + 2, :].rearrange("p a t -> p (a t)"), bank[1 + i][:, :],
                               ACT.Copy).then_inc(p2_act, 1)
            for half in range(2):
                act_half(act, SPLIT_IN2 + 5, half)
            for i in range(2):
                act.wait_ge(qk_turned, i + 1)
                act.activation(qbT[:, 2 * i:2 * i + 2, :].rearrange("p a t -> p (a t)"), bank[5 + i][:, :],
                               ACT.Copy).then_inc(qbT_ready, 1)
            for i in range(NA_HEADS):
                act.wait_ge(ta_ready, i + 1)
                for t in range(NT):
                    act.activation(prob_a[:, t, :], prob_a[:, t, :], ACT.Exp, bias=top_a[:, t:t + 1],
                                   accum_out=sum_a[:, t:t + 1]).then_inc(ea_ready, 1)
                act.wait_ge(tb_ready, i + 1)
                if i:
                    act.wait_ge(pb_turned, i)
                for t in range(NT):
                    act.activation(prob_b[:, t, :], bank[1][:, t * T:(t + 1) * T], ACT.Exp, bias=top_b[:, t:t + 1],
                                   scale=SCALE, accum_out=sum_b[:, t:t + 1]).then_inc(eb_ready, 1)
                if i % 2:
                    dst = sga if i < 4 else sgb
                    for b in range(2):
                        use = i - 1 + b
                        act.wait_ge(gate2_done, use + 1)
                        act.activation(dst[:, 2 * (use % 4):2 * (use % 4) + 2, :].rearrange("p a t -> p (a t)"),
                                       bank[5 + b][:, :], ACT.Copy).then_inc(gate2_act, 1)
                act.wait_ge(pa_turned, i + 1)
                act.activation(prob_aT[:, :, :].rearrange("p k q -> p (k q)"), bank[2][:, :], ACT.Copy).then_inc(paT_ready, 1)
                part = slice((i % 2) * DH, (i % 2) * DH + DH)
                act.wait_ge(ya_done, i + 1)
                act.activation(yaT[part, i // 2, :], bank[4][0:DH, 0:T], ACT.Copy).then_inc(ya_ready, 1)
                act.wait_ge(yb_done, i + 1)
                act.activation(ybT[part, i // 2, :], bank[4][DH:P, 0:T], ACT.Copy).then_inc(yb_ready, 1)
                if i + 2 < NA_HEADS:
                    act_half(act, SPLIT_IN2 + 5 + (i + 2) // 2, i % 2)
            act.wait_ge(gate2_act, 8)
            for dst in (sga, sgb):
                act.activation(dst[:, :, :], dst[:, :, :], ACT.Sigmoid).then_inc(sg_ready, 1)
            for half in range(2):
                act_half(act, SPLIT_WQ, half)
            act_stats(act, 4)
            act_nT_lead(act, 3, "gain22", nT_hi)
            for use in range(0, 8, 2):
                if use < 6:
                    for half in range(2):
                        act_half(act, SPLIT_WQ + use // 2 + 1, half)
                act.wait_ge(query_done, use + 1)
                act.activation(qT[:, 2 * use:2 * use + 2, :].rearrange("p a t -> p (a t)"), bank[QUERY_BANK[use]][:, :],
                               ACT.Copy).then_inc(query_act, 1)
            for use in range(8):
                t, part = divmod(use, 4)
                act.wait_ge(score_done, use + 1)
                act.activation(sc[:, t, 4 * part:4 * part + 4, :].rearrange("p a n -> p (a n)"), bank[QUERY_BANK[use]][:, :],
                               ACT.Copy).then_inc(score_ready, 1)

            def act_column(n, at_n):
                act.wait_ge(chunk_used, n + 1)
                dst = A[:, bass.ds(n * CJ, CJ), :].rearrange("p j t -> p (j t)")
                act.activation(dst, bank[4 + at_n % 2][:, :], ACT.Gelu).then_inc(act_ready, 1)

            def act_lead(n, at_n, loaded):
                slot, b = at_n % RAW_SLOTS, at_n % 2
                act.wait_ge(raw_full[slot], loaded)
                act.activation(lead[b][:, :], raw[slot][:, :], ACT.Copy).then_inc(lead_ready, 1)

            head = ROUTING % UNROLL
            for n in range(head):
                if n >= 2:
                    act_column(n - 2, n - 2)
                act_lead(n, n, fill(0, n))
            with act.Fori(0, ROUTING // UNROLL) as i:
                for s in range(UNROLL):
                    at_n = head + s
                    act_column(at_n + UNROLL * i - 2, at_n - 2)
                    act_lead(at_n + UNROLL * i, at_n, fill(i, at_n))
            act.wait_ge(routed, 1)
            act.activation(best[:, :, :], best[:, :, :], ACT.Exp).then_inc(best_exp, 1)
            with act.Fori(ROUTING // 2 - 1, PEER_CHUNKS // 2) as n2:
                for b in range(2):
                    act_column(2 * n2 + b, b)
            act.wait_ge(route_ready, 1)

            def scalar_hots(turn, b, peeled):
                k = SCALAR_HOTS * turn + b - VECTOR_HOTS
                if not peeled:
                    act.wait_ge(gates_done, HOTS * (turn - 1) + b + 1)
                for t in range(GT):
                    last = act.activation(hot[b][:, 0, t, :], c("iota")[:, 0:NKEYS], ACT.Square,
                                          bias=ijT[:, 0, bass.ds((HOTS * turn + b) * GT + t, 1)], scale=-1.0)
                last.then_inc(hot_i_step, 1)
                act.wait_ge(hot_i_step, 2 * k + 1)
                act.activation(hot[b][:, 0, :, :], hot[b][:, 0, :, :], ACT.Relu, bias=1.0,
                               scale=-1.0).then_inc(hot_i_step, 1)

            for b in range(VECTOR_HOTS, HOTS):
                scalar_hots(0, b, True)
            with act.Fori(1, GROUPS // HOTS) as turn:
                for b in range(VECTOR_HOTS, HOTS):
                    scalar_hots(turn, b, False)
            act_stats(act, 5)

        @block.tensor
        def _(pe):
            pe.wait_ge(const_in, 32)
            pe_turn(pe, 0)
            wait_nT_split(pe, 0)

            def whole(i, outs, done):
                for half in range(2):
                    pe_half(pe, i, half, outs, done)

            for n, part in enumerate(IN1_ORDER):
                if n == 4:
                    pe.wait_ge(proj_act, 2)
                if n == 5:
                    pe.wait_ge(proj_dve, 2)
                banks = IN1_BANK[2 * n:2 * n + 2]
                if part in (4, 1):
                    outs = [(bank[banks[t]][:, :], False, t, True) for t in range(NT)]
                else:
                    outs = [(bank[banks[m // 2]][:, (m % 2) * T:(m % 2 + 1) * T], True, m, m % 2 == 1) for m in range(4)]
                whole(n, outs, proj_done)
            pe.wait_ge(proj_dve, 4)
            pe.wait_ge(qk_ready, 2)
            for t in range(NT):
                for hd in range(HEADS):
                    last = pe.matmul(bank[t][:, hd * P:(hd + 1) * P], hD1[:, hd, t * P:(t + 1) * P],
                                     hF[:, hd, t * P:(t + 1) * P], start=True, stop=True)
                last.then_inc(sc_done, 1)
            pe.wait_ge(qk_ready, 3)
            pe.wait_ge(proj_act, 8)
            for t in range(NT):
                for hd in range(HEADS):
                    last = pe.transpose(bank[2 + t][:, hd * P:(hd + 1) * P], hD2[:, hd, t * P:(t + 1) * P], ident)
                last.then_inc(kl_turned, 1)
            pe.wait_ge(proj_act, 12)
            for n in range(N_CHUNKS - 1):
                t, lo = n // 2, (n % 2) * CHUNK
                pe.wait_ge(kl_ready, t + 1)
                for hd in range(HEADS):
                    last = pe.matmul(bank[4 + n][:, hd * P:(hd + 1) * P], hKL[lo:lo + CHUNK, t, hd, :],
                                     hI[lo:lo + CHUNK, t, hd * P:(hd + 1) * P], start=True, stop=True)
                last.then_inc(state_done, 1)
            pe.wait_ge(ws_masked, 1)
            pe.wait_ge(vh_ready, 1)
            for pair in range(2):
                if pair:
                    pe.wait_ge(state_ready, 1)
                dst = bank[7 if pair == 0 else 4]
                for g in (2 * pair, 2 * pair + 1):
                    for t in range(NT):
                        o = (g % 2) * T + t * P
                        last = pe.matmul(dst[:, o:o + P], mV[:, t, g * P:(g + 1) * P], w_sT[:, g, :],
                                         start=True, stop=True)
                last.then_inc(mixed_done, 1)
            for t in range(NT):
                pe.wait_ge(sc_masked, t + 1)
                pe.wait_ge(qk_ready, 5)
                pe.wait_ge(state_ready, 1 if t == 0 else 3)
                for hd in range(HEADS):
                    dst = bank[t][:, hd * P:(hd + 1) * P]
                    tok = slice(t * P, (t + 1) * P)
                    pe.matmul(dst, hSC[:, t, hd, :], hI[:, t, hd * P:(hd + 1) * P], start=True, stop=False)
                    if t:
                        pe.matmul(dst, hQE[:, hd, tok], hS[:, 2 * t - 1, hd, :], start=False, stop=False)
                    last = pe.matmul(dst, hQO[:, hd, tok], hS[:, 2 * t, hd, :], start=False, stop=True)
                last.then_inc(o_done, 1)
            def out1(half, t, mixer):
                n = CH_OUT1 + half
                for k in range(HEADS * mixer, HEADS * mixer + HEADS):
                    last = pe.matmul(bank[OUT1_BANK[2 * half + t]][:, :], mixT[:, k, t * P:(t + 1) * P],
                                     ring8(slot_of(n))[:, k, :], start=(k == 0), stop=(k == 2 * HEADS - 1))
                return last

            ring_wait(pe, CH_OUT1)
            pe.wait_ge(state_ready, 3)
            pe.wait_ge(mix_g, HEADS)
            out1(0, 0, 0)
            pe.wait_ge(on_ready, 1)
            for hd in range(HEADS):
                for t in range(NT):
                    o = (hd % 2) * T + t * P
                    last = pe.transpose(bank[2 + hd // 2][:, o:o + P], hON[:, t, hd * P:(hd + 1) * P], ident)
                if hd % 2:
                    last.then_inc(on_turned, 1)
            out1(0, 1, 0)
            pe.wait_ge(mix_h, HEADS)
            for t in range(NT):
                out1(0, t, 1).then_inc(out1_done, 1)
            ring_wait(pe, CH_OUT1 + 1)
            for t in range(NT):
                out1(1, t, 0)
                out1(1, t, 1).then_inc(out1_done, 1)
            pe_turn(pe, 1)
            wait_nT(pe, 1)
            pe.wait_ge(rows_in, 64)
            for t in range(NT):
                for k in range(KD):
                    last = pe.matmul(bank[4][:, t * 64:t * 64 + NE], nT[:, k, t * P:(t + 1) * P], w_router[:, k, :],
                                     start=(k == 0), stop=(k == KD - 1))
            last.then_inc(router_done, 1)
            pe.wait_ge(assign_ready, 1)
            pe.matmul(bank[5][:, 0:32], c("before"), assigned[:, 0, :], start=True, stop=True)
            pe.matmul(bank[5][:, 32:64], c("before"), assigned[:, 1, :], start=True, stop=False)
            pe.matmul(bank[5][:, 32:64], c("ones"), assigned[:, 0, :], start=False, stop=True)
            pe.matmul(bank[5][:, 64:96], c("ones"), assigned[:, 0, :], start=True, stop=False)
            pe.matmul(bank[5][:, 64:96], c("ones"), assigned[:, 1, :], start=False, stop=True).then_inc(rank_done, 1)
            pe.wait_ge(pick_ready, NT)
            pe.wait_ge(xhat_rest_ready, 1)
            for k in range(KD):
                if k == 6:
                    pe.wait_ge(xs_act, 1)
                if k == 7:
                    pe.wait_ge(xs_dve, 1)
                for part in (xhat_lead, xhat_rest):
                    for t in range(NT):
                        last = pe.matmul(bank[GATHER_BANK[k]][:, :], part[:, t, k * P:(k + 1) * P], pick_slot[:, t, :],
                                         start=(part is xhat_lead and t == 0), stop=(part is xhat_rest and t == NT - 1))
                last.then_inc(gather_done, 1)
            pe.wait_ge(pick_ready, 2 * NT)
            for s in range(SLOTS // P):
                for t in range(NT):
                    o = (s % 2) * T + t * P
                    last = pe.transpose(bank[4 + s // 2][:, o:o + P], pick_wt[:, t, s * P:(s + 1) * P], ident)
                if s % 2:
                    last.then_inc(wt_turned, 1)
            pe.wait_ge(starts_ready, 1)

            def expert_in(dst, w, block_in):
                for k in range(KD):
                    last = pe.matmul(dst[0:BLOCK, :], block_in[:, k, :], ring8(w)[:, k, :],
                                     start=(k == 0), stop=(k == KD - 1))
                return last

            def expert_turn(dst, hidden):
                for f in range(4):
                    last = pe.matmul(dst[:, f * BLOCK:(f + 1) * BLOCK], hidden[:, f * P:(f + 1) * P],
                                     ident[0:BLOCK, 0:BLOCK], start=True, stop=True)
                return last

            def expert_out(half, w, hidden_t):
                for f in range(4):
                    last = pe.matmul(bank[6 + half][0:BLOCK, :], hidden_t[:, f, :],
                                     ring4(w)[:, f, half * 512:(half + 1) * 512], start=(f == 0), stop=(f == 3))
                return last

            load_most = pe.value_load(most_i[0:1, 0:1], min_val=0, max_val=T)
            with pe.If(load_most > BLOCK):
                def many_products(pair, peeled):
                    for i in range(RING):
                        pe.wait_ge(ring_full[W_SLOT[i]], pair_fill(pair, i))
                    for j in range(2):
                        w_g, w_u, w_d = W_SLOT[3 * j:3 * j + 3]
                        for b in range(BLOCKS_MAX):
                            n = (2 * pair + j) * BLOCKS_MAX + b
                            pe.wait_ge(x_ready, n + 1)
                            expert_in(bank[0], w_g, x_blk[0]).then_inc(many_gate, 1)
                            expert_in(bank[2], w_u, x_blk[0]).then_inc(many_up, 1)
                            pe.wait_ge(hid_ready, n + 1)
                            expert_turn(bank[4], hid[0]).then_inc(hid_turned, 1)
                            pe.wait_ge(hT_ready, n + 1)
                            if b or j or not peeled:
                                pe.wait_ge(y_act, n)
                                pe.wait_ge(y_dve, n)
                            for half in range(2):
                                expert_out(half, w_d, hT[0]).then_inc(many_down, 1)
                    pe.wait_ge(many_down, 2 * (2 * pair + 2) * BLOCKS_MAX)
                    pe.nop().then_inc(w_used, 4)
                    pe.nop().then_inc(down_done, 4)

                many_products(0, True)
                with pe.Fori(1, PAIRS) as pair:
                    many_products(pair, False)
            with pe.Else():
                def product(e, j, kind, peeled):
                    if not peeled:
                        pe.wait_ge((gate_sum, up_sum)[kind], e - 1)
                    if kind == 0:
                        pe.wait_ge(x_lo_ready, e + 1)
                    for ready, used in ((w_lead_ready, w_lead_used), (w_rest_ready, w_used)):
                        for half in range(2):
                            pe.wait_ge(ready, 4 * e + 2 * kind + half + 1)
                            rows = slice(4 * half, 4 * half + 4)
                            part = w_lead[half] if ready is w_lead_ready else ring_rest8(W_SLOT[3 * j + kind])[:, rows, :]
                            for k in range(4):
                                last = pe.matmul(bank[2 * kind + j][:, :], x_two[j][:, 4 * half + k, :], part[:, k, :],
                                                 start=(ready is w_lead_ready and half == 0 and k == 0),
                                                 stop=(ready is w_rest_ready and half == 1 and k == 3))
                            if ready is w_lead_ready or half == 1:
                                last.then_inc(used, 1)

                def turn(e, j, peeled):
                    pe.wait_ge(hid_ready, e + 1)
                    if not peeled:
                        pe.wait_ge(hT_ready, e - 1)
                    expert_turn(bank[4 + j], hid[j]).then_inc(hid_turned, 1)

                def down(e, pair, j, first):
                    pe.wait_ge(ring_full[W_SLOT[3 * j + 2]], pair_fill(pair, 3 * j + 2))
                    pe.wait_ge(hT_ready, e + 1)
                    for half in range(2):
                        if not first:
                            pe.wait_ge((y_act, y_dve)[half], e)
                        expert_out(half, W_SLOT[3 * j + 2], hT[j]).then_inc(down_done, 1)

                for kind in range(2):
                    product(0, 0, kind, True)
                product(1, 1, 0, True)
                turn(0, 0, True)
                product(1, 1, 1, True)
                down(0, 0, 0, True)
                product(2, 0, 0, False)
                turn(1, 1, True)
                product(2, 0, 1, False)
                down(1, 0, 1, False)
                product(3, 1, 0, False)
                turn(2, 0, False)
                product(3, 1, 1, False)
                down(2, 1, 0, False)
                with pe.Fori(2, PAIRS) as pair:
                    for j in range(2):
                        e = 2 * pair + j
                        product(e, j, 0, False)
                        turn(e - 1, 1 - j, False)
                        product(e, j, 1, False)
                        down(e - 1, pair - 1 + j, 1 - j, False)
                turn(N_EXPERTS - 1, 1, False)
                down(N_EXPERTS - 1, PAIRS - 1, 1, False)
            pe.wait_ge(slot_wt_ready, 2)
            for b in range(2):
                pe.wait_ge(y_rows_in[b], 16)
                for use in range(4):
                    half, t = divmod(use, NT)
                    for s in (2 * b, 2 * b + 1):
                        last = pe.matmul(bank[use][:, :], slot_wt[:, s, t * P:(t + 1) * P],
                                         y_rows[:, s, half * 512:(half + 1) * 512],
                                         start=(s == 0), stop=(s == SLOTS // P - 1))
                    if b:
                        last.then_inc(moe_done, 1)
            pe_turn(pe, 2)
            wait_nT_split(pe, 2)

            whole(SPLIT_IN2 + 0, [(bank[4 + t][:, :], False, t, True) for t in range(NT)], p2_done)
            whole(SPLIT_IN2 + 1, [(bank[6][:, t * 256:(t + 1) * 256], False, t, t == NT - 1) for t in range(NT)], p2_done)
            for i, banks in ((2, (7, 0)), (3, (1, 2))):
                whole(SPLIT_IN2 + i, [(bank[banks[m // 2]][:, (m % 2) * T:(m % 2 + 1) * T], True, m, m % 2 == 1) for m in range(4)], p2_done)
            pe.wait_ge(p2_act, 1)
            whole(SPLIT_IN2 + 4, [(bank[3 + t][:, :], False, t, True) for t in range(NT)], p2_done)
            pe.wait_ge(qk_roped, 1)
            pe.wait_ge(p2_act, 3)
            for i in range(2):
                for a in (2 * i, 2 * i + 1):
                    for t in range(NT):
                        o = (a % 2) * T + t * P
                        last = pe.transpose(bank[5 + i][:, o:o + P], qk[:, t, a * P:(a + 1) * P], ident)
                last.then_inc(qk_turned, 1)
            pe.wait_ge(p2_dve, 1)
            for a in range(KV_HEADS):
                for t in range(NT):
                    last = pe.transpose(bank[7][:, a * T + t * P:a * T + (t + 1) * P],
                                        kk[:, t, a, :, :].rearrange("p r d -> p (r d)"), ident)
            last.then_inc(qk_turned, 1)

            def scores(dst, qT, kT, key_pair, i):
                part = slice((i % 2) * DH, (i % 2) * DH + DH)
                for t in range(NT):
                    last = pe.matmul(dst[:, t * T:(t + 1) * T], qT[part, i // 2, t * P:(t + 1) * P], kT[part, key_pair, :],
                                     start=True, stop=True)
                return last

            def turn_probs(dst, prob):
                for k in range(NT):
                    for t in range(NT):
                        last = pe.transpose(dst[:, k * T + t * P:k * T + (t + 1) * P], prob[:, t, k * P:(k + 1) * P], ident)
                return last

            def weigh(dst, v, first, prob_t):
                for k in range(NT):
                    last = pe.matmul(dst, v[:, k, first:first + DH], prob_t[:, k, :], start=(k == 0), stop=(k == NT - 1))
                return last

            def both_scores(i):
                scores(bank[0], qaT, kaT, i // 2, i).then_inc(sa_done, 1)
                scores(bank[1], qbT, kbT, i // 4, i).then_inc(sb_done, 1)

            pe.wait_ge(p2_act, 5)
            pe.wait_ge(p2_dve, 4)
            pe.wait_ge(qbT_ready, 2)
            pe.wait_ge(kbT_ready, 1)
            both_scores(0)
            for i in range(NA_HEADS):
                if i % 2 == 0 and i:
                    pe.wait_ge(gate2_act, i)
                pe_half(pe, SPLIT_IN2 + 5 + i // 2, i % 2,
                        [(bank[5 + m // 2][:, (m % 2) * T:(m % 2 + 1) * T], True, m, m % 2 == 1) for m in range(4)], gate2_done)
                pe.wait_ge(pa_ready, i + 1)
                turn_probs(bank[2], prob_a).then_inc(pa_turned, 1)
                pe.wait_ge(pb_ready, i + 1)
                turn_probs(bank[3], prob_b).then_inc(pb_turned, 1)
                if i + 1 < NA_HEADS:
                    both_scores(i + 1)
                pe.wait_ge(paT_ready, i + 1)
                if i:
                    pe.wait_ge(ya_ready, i)
                    pe.wait_ge(yb_ready, i)
                weigh(bank[4][0:DH, 0:T], va, i * DH, prob_aT).then_inc(ya_done, 1)
                pe.wait_ge(pbT_ready, i + 1)
                weigh(bank[4][DH:P, 0:T], vb, (i // 4) * DH, prob_bT).then_inc(yb_done, 1)
            pe.wait_ge(ya_ready, NA_HEADS)
            pe.wait_ge(yb_ready, GQA_HEADS)
            pe.wait_ge(gate2_act, 8)
            ring_wait(pe, CH_PROJ)
            ring_wait(pe, CH_PROJ + 1)
            for i in range(4):
                for b, y in enumerate((yaT, ybT)):
                    for m in range(2):
                        for k in range(4):
                            mt = 2 * i + m
                            last = pe.matmul(bank[BRANCH_BANK[b][i]][:, m * T:(m + 1) * T],
                                             ring4(slot_of(CH_PROJ + b))[:, k, mt * P:(mt + 1) * P], y[:, k, :],
                                             start=(k == 0), stop=(k == 3))
                    last.then_inc(branch_done, 1)
            pe.wait_ge(merged_ready, 3)
            for half in range(2):
                ring_wait(pe, CH_OUT2 + half)
                for t in range(NT):
                    for k in range(KD):
                        if (half, t, k) == (0, 0, KD - 2):
                            pe.wait_ge(merged_ready, 4)
                        last = pe.matmul(bank[2 * half + t][:, :], sga[:, k, t * P:(t + 1) * P],
                                         ring8(slot_of(CH_OUT2 + half))[:, k, :], start=(k == 0), stop=(k == KD - 1))
                    last.then_inc(out2_done, 1)
            pe_turn(pe, 3)
            wait_nT_split(pe, 3)
            for i in range(4):
                whole(SPLIT_WQ + i, [(bank[QUERY_BANK[2 * i + m // 2]][:, (m % 2) * T:(m % 2 + 1) * T], True, m, m % 2 == 1)
                                          for m in range(4)], query_done)
            pe.wait_ge(query_act, 4)
            pe.wait_ge(query_dve, 4)
            pe.wait_ge(keys_in, 16)
            for use in range(8):
                t, part = divmod(use, 4)
                for a in range(4):
                    hp = 4 * part + a
                    last = pe.matmul(bank[QUERY_BANK[use]][:, a * NKEYS:(a + 1) * NKEYS], qT[:, hp, t * P:(t + 1) * P],
                                     keysT[:, hp, :], start=True, stop=True)
                last.then_inc(score_done, 1)

            def bank_free(n, peeled):
                if not peeled or n >= 2:
                    pe.wait_ge(act_ready, n - 1)

            def columns_of(tile, table):
                if table == "u":
                    return tile[:, :].rearrange("p (k j i) -> p k j i", k=KD, j=CJ)
                return tile[:, :].rearrange("p (j d) -> p j d", j=CJ)

            def act_split(n, at_n, peeled=False):
                slot, b = at_n % RAW_SLOTS, at_n % 2
                bank_free(n, peeled)
                hi = columns_of(lead[b], "u")
                lo = columns_of(rest[slot], "u")
                pe.wait_ge(lead_ready, n + 1)
                for j in range(CJ):
                    dst = bank[4 + b][:, j * T:(j + 1) * T]
                    for x in (nT_hi, nT_lo):
                        for k in range(KD):
                            pe.matmul(dst, hi[:, k, j, :], x[:, k, :], start=(x is nT_hi and k == 0), stop=False)
                    if j == 0:
                        pe.wait_ge(rest_ready, n + 1)
                    for k in range(KD):
                        last = pe.matmul(dst, lo[:, k, j, :], nT_hi[:, k, :], start=False, stop=(k == KD - 1))
                last.then_inc(chunk_used, 1)

            pe.wait_ge(score_ready, 8)
            for n in range(ROUTING % UNROLL):
                act_split(n, n, True)
            with pe.Fori(0, ROUTING // UNROLL) as i:
                for s in range(UNROLL):
                    at_n = ROUTING % UNROLL + s
                    act_split(at_n + UNROLL * i, at_n)
            pe.wait_ge(gates_ready, 1)
            for i, src in enumerate((best, ij[:, 0], ij[:, 1])):
                for t in range(NT):
                    last = pe.transpose(bank[6 + i // 2][:, (i % 2) * T + t * P:(i % 2) * T + (t + 1) * P], src[:, t, :], ident)
            last.then_inc(route_turned, 1)
            with pe.Fori(0, (PEER_CHUNKS - ROUTING) // UNROLL) as i:
                for s in range(UNROLL):
                    act_split(ROUTING + UNROLL * i + s, ROUTING + s)

            def gate_products(turn, b, peeled):
                g = HOTS * turn + b
                pe.wait_ge(hot_j_ready, g + 1)
                if b >= VECTOR_HOTS:
                    pe.wait_ge(hot_i_step, 2 * (SCALAR_HOTS * turn + b - VECTOR_HOTS) + 2)
                if not peeled:
                    pe.wait_ge(gated, g - HOTS + 1)
                for t in range(GT):
                    last = pe.matmul(bank[4 + b][:, t * NKEYS:(t + 1) * NKEYS], hot[b][:, 0, t, :], hot[b][:, 1, t, :],
                                     start=True, stop=True)
                last.then_inc(gates_done, 1)

            pe.wait_ge(route_ready, 1)
            pe.wait_ge(act_ready, PEER_CHUNKS)
            for b in range(HOTS):
                gate_products(0, b, True)
            with pe.Fori(1, GROUPS // HOTS) as turn:
                for b in range(HOTS):
                    gate_products(turn, b, False)

            def out_products(n, at_n, first, last):
                slot, b = at_n % RAW_SLOTS, at_n % 2
                v_hi = columns_of(lead[b], "v")
                v_lo = columns_of(rest[slot], "v")
                c = n - PEER_CHUNKS
                pe.wait_ge(lead_ready, n + 1)
                pe.wait_ge(rest_ready, n + 1)
                pe.wait_ge(hid_hi_ready, c + 1)
                pe.wait_ge(hid_lo_ready, c + 1)
                for j in range(CJ):
                    for t in range(NT):
                        tok = slice(t * P, (t + 1) * P)
                        for i, (x, v) in enumerate(((hid_hi, v_hi), (hid_hi, v_lo), (hid_lo, v_hi))):
                            for half in range(2):
                                ins = pe.matmul(bank[2 * half + t][:, :], x[b][:, j, tok], v[:, j, half * 512:(half + 1) * 512],
                                                start=(first and j == 0 and i == 0), stop=(last and j == CJ - 1 and i == 2))
                ins.then_inc(chunk_used, 1)

            v_head = 2
            out_products(PEER_CHUNKS, PEER_CHUNKS, True, False)
            out_products(PEER_CHUNKS + 1, PEER_CHUNKS + 1, False, False)
            with pe.Fori(0, PEER_CHUNKS // UNROLL) as i:
                for s in range(UNROLL):
                    out_products(PEER_CHUNKS + v_head + UNROLL * i + s, PEER_CHUNKS + v_head + s, False, False)
            out_products(2 * PEER_CHUNKS - 2, 2 * PEER_CHUNKS - 2, False, False)
            out_products(2 * PEER_CHUNKS - 1, 2 * PEER_CHUNKS - 1, False, True)

        @block.vector
        def _(dve):
            link = chain(dve, dve_step)
            dve_stats(dve, link, 0)
            dve_xhat(dve)
            dve.wait_ge(const_in, 32)
            dve.tensor_tensor(lbd[:, :], prs("lb0"), prs("lb1"), ALU.subtract).then_inc(lb_diff, 1)
            dve_nT_rest(dve, 0, "gain1", nT_hi1)
            dve.wait_ge(lb_sig, 1)
            link(dve.tensor_scalar(omlb[:, :], lb[:, :], -1.0, 1.0, ALU.mult, ALU.add))
            dve.wait_ge(proj_act, 2)
            for hd in range(HEADS):
                last = dve.tensor_scalar(hF[:, hd, :], hF[:, hd, :], omlb[:, hd:hd + 1], lb[:, hd:hd + 1],
                                         ALU.mult, ALU.add)
            link(last)
            dve.tensor_scalar(hK[:, :, :], hF[:, :, :], -1.0, 1.0, ALU.mult, ALU.add).then_inc(f_ready, 1)
            for use, dst in ((2, hQ), (3, hQ), (4, hG), (5, hG)):
                dve.wait_ge(proj_act, use + 1)
                half = use % 2
                view = dst[:, 2 * half:2 * half + 2, :].rearrange("p a t -> p (a t)")
                dve.tensor_tensor(view, bank[IN1_BANK[use]][:, :], view, ALU.mult).then_inc(proj_dve, 1)
            dve.wait_ge(lf_ready, 1)
            for hd in range(HEADS):
                last = dve.tensor_tensor_scan(hB[:, hd, :], c("scanmask"), hF[:, hd, :], 0.0, ALU.mult, ALU.add)
            link(last)

            def chunks(tile):
                return tile[:, :, :].rearrange("p a (n s) -> p (a n) s", s=CHUNK)

            b_all = chunks(hB)
            shape = [P, HEADS * N_CHUNKS, CHUNK]
            mid = spread(b_all[:, :, CHUNK // 2 - 1:CHUNK // 2], shape)
            end = spread(b_all[:, :, CHUNK - 1:CHUNK], shape)
            dve.tensor_tensor(chunks(hD1), b_all, mid, ALU.subtract).then_inc(d_ready, 1)
            dve.tensor_tensor(chunks(hD2), end, b_all, ALU.subtract).then_inc(d_ready, 1)
            dve.wait_ge(exp_ready, 1)
            dve.wait_ge(proj_dve, 4)
            dve.tensor_tensor(hF[:, :, :], hQ[:, :, :], hF[:, :, :], ALU.mult).then_inc(qk_ready, 1)
            dve.wait_ge(exp_ready, 2)
            dve.tensor_tensor(hD1[:, :, :], hK[:, :, :], hD1[:, :, :], ALU.mult).then_inc(qk_ready, 1)
            dve.wait_ge(exp_ready, 3)
            dve.tensor_tensor(hD2[:, :, :], hK[:, :, :], hD2[:, :, :], ALU.mult).then_inc(qk_ready, 1)
            dve.wait_ge(exp_ready, 4)
            dve.wait_ge(qk_zero, 2)
            for odd, dst in enumerate((hQE, hQO)):
                def pick(tile):
                    return tile[:, :, :].rearrange("p a (n e s) -> p (a n) e s", e=2, s=CHUNK)[:, :, odd, :]
                dve.tensor_tensor(pick(dst), pick(hQ), pick(hEB), ALU.mult).then_inc(qk_ready, 1)
            dve.wait_ge(qk_zero, 3)
            mask = spread(c("causal").bitcast(U32).unsqueeze(1), [P, HEADS, P])
            for t in range(NT):
                dve.wait_ge(sc_done, t + 1)
                dve.copy_predicated(hSC[:, t, :, :], mask, quad(bank[t])).then_inc(sc_masked, 1)
            dve.wait_ge(proj_act, 10)
            link(dve.tensor_tensor(mSQ[:, :, :], mV[:, :, :], mV[:, :, :], ALU.mult))
            link(dve.tensor_reduce(vss[:, :], mSQ[:, :, :].rearrange("p t (g c) -> p (t g) c", g=HEADS), AX_X, ALU.add))
            dve.tensor_scalar(vss[:, :], vss[:, :], 1.0 / P, EPS, ALU.mult, ALU.add).then_inc(v_ms, 1)
            dve.wait_ge(v_sd, 1)
            link(dve.reciprocal(vrs[:, :], vrs[:, :]))
            v8 = mV[:, :, :].rearrange("p t (g c) -> p (t g) c", g=HEADS)
            dve.tensor_tensor(v8, v8, spread(vrs[:, :].unsqueeze(2), [P, NT * HEADS, P]), ALU.mult).then_inc(vh_ready, 1)
            dve.wait_ge(state_done, 1)
            dve.tensor_copy(hS[:, 0, :, :], quad(bank[4])).then_inc(state_ready, 1)
            eb = hEB[:, :, :].rearrange("p a (n s) -> p a n s", s=CHUNK)
            for n in (1, 2):
                dve.wait_ge(state_ready, n)
                decay = spread(eb[:, :, n, CHUNK - 1:CHUNK], [P, HEADS, P])
                link(dve.tensor_tensor(hS[:, n, :, :], hS[:, n - 1, :, :], decay, ALU.mult))
                dve.wait_ge(state_done, n + 1)
                dve.tensor_tensor(hS[:, n, :, :], quad(bank[4 + n]), hS[:, n, :, :], ALU.add).then_inc(state_ready, 1)
            dve.wait_ge(rows_in, 64)
            dve.wait_ge(proj_act, 12)
            for g in range(HEADS):
                dve.wait_ge(mixed_done, g // 2 + 1)
                src = bank[7 if g < 2 else 4][:, (g % 2) * T:(g % 2 + 1) * T].rearrange("p (t i) -> p t i", t=NT)
                bias = spread(row("b_s")[:, g * P:(g + 1) * P].unsqueeze(1), [P, NT, P])
                dst = mixT[:, g, :].rearrange("p (t i) -> p t i", t=NT)
                link(dve.scalar_tensor_tensor(dst, src, pr("vgain", g), bias, ALU.mult, ALU.add))
                dve.tensor_tensor(mixT[:, g, :], mixT[:, g, :], mU[:, g, :], ALU.mult).then_inc(mix_g, 1)
            dve.wait_ge(o_sq, NT)
            link(dve.tensor_reduce(oss[:, :], mSQ[:, :, :].rearrange("p t (g c) -> p (t g) c", g=HEADS), AX_X, ALU.add))
            dve.tensor_scalar(oss[:, :], oss[:, :], 1.0 / P, EPS, ALU.mult, ALU.add).then_inc(o_ms, 1)
            dve.wait_ge(o_sd, 1)
            link(dve.reciprocal(ors[:, :], ors[:, :]))
            for t in range(NT):
                last = dve.tensor_tensor(hON[:, t, :].rearrange("p (g c) -> p g c", g=HEADS), quad(bank[t]),
                                         spread(ors[:, t * HEADS:(t + 1) * HEADS].unsqueeze(2), [P, HEADS, P]), ALU.mult)
            last.then_inc(on_ready, 1)
            for hd in range(HEADS):
                dve.wait_ge(on_turned, hd // 2 + 1)
                dve.scalar_tensor_tensor(mixT[:, HEADS + hd, :], bank[2 + hd // 2][:, (hd % 2) * T:(hd % 2 + 1) * T],
                                         pr("ogain", hd), hG[:, hd, :], ALU.mult, ALU.mult).then_inc(mix_h, 1)
            for half in range(2):
                for t in range(NT):
                    dve.wait_ge(out1_done, 2 * half + t + 1)
                    dst = h[:, t, half * 512:(half + 1) * 512]
                    dve.tensor_tensor(dst, bank[OUT1_BANK[2 * half + t]][:, :], dst, ALU.add).then_inc(h_ready, 1)
            dve_stats(dve, link, 1)
            dve_xhat(dve)
            dve_nT(dve, 1, "gain2")
            dve.memset(g8[:, :, :], BIG)
            dve.memset(em[:, :, :], BIG)
            dve.wait_ge(router_done, 1)
            link(dve.tensor_tensor(lg[:, :, :], bank[4][:, 0:2 * 64].rearrange("p (t e) -> p t e", t=NT)[:, :, 0:NE],
                                   spread(row("b_router").unsqueeze(1), [P, NT, NE]), ALU.add))
            link(dve.tensor_copy(g8[:, :, 0:N_GROUPS], lg[:, :, 0:N_GROUPS]))
            for t in range(NT):
                last = dve.max(gm8[:, t, :], g8[:, t, :])
            link(last)
            for t in range(NT):
                last = dve.max_index(gi8[:, t, :], gm8[:, t, :], g8[:, t, :])
            link(last)
            dve.tensor_scalar(gneg[:, :].unsqueeze(2), gm8[:, :, 0:1], -1.0, None, ALU.mult).then_inc(gneg_ready, 1)
            link(dve.tensor_copy(gid[:, :].unsqueeze(2), gi8[:, :, 0:1]))
            for t in range(NT):
                last = dve.tensor_scalar(emask[:, t, :], c("group"), gid[:, t:t + 1], None, ALU.is_equal)
            link(last)
            link(dve.copy_predicated(em[:, :, :], emask[:, :, :], lg[:, :, N_GROUPS:]))
            for t in range(NT):
                last = dve.max(ev8[:, t, :], em[:, t, :])
            link(last)
            for t in range(NT):
                last = dve.max_index(ei8[:, t, :], ev8[:, t, :], em[:, t, :])
            link(last)
            dve.tensor_scalar(eneg[:, :].unsqueeze(2), ev8[:, :, 0:1], -1.0, None, ALU.mult).then_inc(eneg_ready, 1)
            link(dve.tensor_copy(eid[:, :, :], ei8[:, :, 0:2]))
            for k in range(2):
                for t in range(NT):
                    last = dve.tensor_scalar(chosen[:, k, t, :], c("iota")[:, 0:N_EXPERTS], eid[:, t, k:k + 1], None,
                                             ALU.is_equal)
            link(last)
            dve.tensor_tensor(assigned[:, :, :], chosen[:, 0, :, :], chosen[:, 1, :, :], ALU.add).then_inc(assign_ready, 1)
            dve.wait_ge(gsum_ready, NT)
            dve.wait_ge(e21_ready, NT)
            link(dve.scalar_tensor_tensor(wt[:, 0, :], e21[:, :], 1.0, gsum[:, :], ALU.add, ALU.mult))
            link(dve.reciprocal(wt[:, 0, :], wt[:, 0, :]))
            link(dve.tensor_tensor(wt[:, 1, :], wt[:, 0, :], e21[:, :], ALU.mult))
            dve.wait_ge(rank_done, 1)
            link(dve.tensor_copy(counts[:, :], bank[5][:, 64:96]))
            link(dve.tensor_tensor_scan(starts[:, :], c("ones")[:, 0:N_EXPERTS], counts[:, :], 0.0, ALU.mult, ALU.add))
            dve.tensor_reduce(most[:, :], counts[:, :], AX_X, ALU.max)
            link(dve.tensor_tensor(starts[:, :], starts[:, :], counts[:, :], ALU.subtract))
            dve.tensor_copy(most_i[:, :], most[0:1, :])
            dve.tensor_copy(starts_i[:, :], starts[0:1, :]).then_inc(starts_ready, 1)
            link(dve.tensor_tensor(place_of[:, :, :], bank[5][:, 0:64].rearrange("p (t e) -> p t e", t=NT),
                                   spread(starts[:, :].unsqueeze(1), [P, NT, N_EXPERTS]), ALU.add))
            for k in range(2):
                last = dve.tensor_tensor(chosen[:, k, :, :], chosen[:, k, :, :], place_of[:, :, :], ALU.mult)
            link(last)
            link(dve.tensor_reduce(slot[:, :, :], chosen[:, :, :, :], AX_X, ALU.add))
            for t in range(NT):
                link(dve.tensor_scalar(pick_slot[:, t, :], c("iota"), slot[:, 0, t:t + 1], None, ALU.is_equal))
                dve.scalar_tensor_tensor(pick_slot[:, t, :], c("iota"), slot[:, 1, t:t + 1], pick_slot[:, t, :].bitcast(F32),
                                         ALU.is_equal, ALU.add).then_inc(pick_ready, 1)
            for t in range(NT):
                dve.tensor_scalar(pick_wt[:, t, :], c("iota"), slot[:, 0, t:t + 1], wt[:, 0, t:t + 1],
                                  ALU.is_equal, ALU.mult)
                link(dve.tensor_scalar(pick_tmp[:, t, :], c("iota"), slot[:, 1, t:t + 1], wt[:, 1, t:t + 1],
                                       ALU.is_equal, ALU.mult))
                dve.tensor_tensor(pick_wt[:, t, :], pick_wt[:, t, :], pick_tmp[:, t, :], ALU.add).then_inc(pick_ready, 1)
            for k in range(1, KD, 2):
                dve.wait_ge(gather_done, k + 1)
                dve.tensor_scalar(xs[:, k, 0:SLOTS], bank[GATHER_BANK[k]][:, :], pr("gain2", k), None,
                                  ALU.mult).then_inc(xs_dve, 1)

            dve.wait_ge(starts_ready, 1)
            load_most = dve.value_load(most_i[0:1, 0:1], min_val=0, max_val=T)
            with dve.If(load_most > BLOCK):
                def many_vector(e, peeled):
                    for b in range(BLOCKS_MAX):
                        n = e * BLOCKS_MAX + b
                        dve.wait_ge(many_up, n + 1)
                        dve.wait_ge(sil_ready, n + 1)
                        dve.tensor_tensor(hid[0][:, :], bank[2][0:BLOCK, :], hid[0][:, :], ALU.mult).then_inc(hid_ready, 1)
                        dve.wait_ge(many_down, 2 * n + 2)
                        if b or not peeled:
                            dve.wait_ge(many_stored, 16 * n)
                        dve.tensor_copy(y_blk[0][:, 512:], bank[7][0:BLOCK, :]).then_inc(y_dve, 1)

                many_vector(0, True)
                with dve.Fori(1, N_EXPERTS) as e:
                    many_vector(e, False)
            with dve.Else():
                def split_rest(e, j, kind):
                    slot = W_SLOT[3 * j + kind]
                    for half in range(2):
                        part = slice(4 * half, 4 * half + 4)
                        dve.wait_ge(w_lead_ready, 4 * e + 2 * kind + half + 1)
                        dve.tensor_tensor(ring_rest8(slot)[:, part, :], ring8(slot)[:, part, :],
                                          w_lead[half][:, :, :].bitcast(F32), ALU.subtract).then_inc(w_rest_ready, 1)

                def total(e, j, kind):
                    dve.wait_ge((gate_low, up_low)[kind], e + 1)
                    dst = (hid, upv)[kind][j]
                    return dve.tensor_tensor(dst[:, :], bank[2 * kind + j][0:BLOCK, :], dst[:, :],
                                             ALU.add).then_inc((gate_sum, up_sum)[kind], 1)

                def copy(e, j, peeled):
                    dve.wait_ge(down_done, 2 * e + 2)
                    if not peeled:
                        dve.wait_ge(y_stored, 16 * e - 16)
                    dve.tensor_copy(y_blk[j][:, 512:], bank[7][0:BLOCK, :]).then_inc(y_dve, 1)

                def expert_vector(e, j, peeled, former_peeled):
                    split_rest(e, j, 0)
                    if not peeled:
                        copy(e - 2, j, former_peeled)
                    split_rest(e, j, 1)
                    total(e, j, 0)
                    total(e, j, 1)
                    dve.wait_ge(up_sum, e + 1)
                    dve.wait_ge(sil_ready, e + 1)
                    dve.tensor_tensor(hid[j][:, :], hid[j][:, :], upv[j][:, :], ALU.mult).then_inc(hid_ready, 1)

                for j in range(2):
                    expert_vector(j, j, True, True)
                for j in range(2):
                    expert_vector(2 + j, j, False, True)
                with dve.Fori(2, PAIRS) as pair:
                    for j in range(2):
                        expert_vector(2 * pair + j, j, False, False)
                for j in range(2):
                    copy(N_EXPERTS - 2 + j, j, False)
            for use in range(4):
                half, t = divmod(use, NT)
                dve.wait_ge(moe_done, use + 1)
                dst = h[:, t, half * 512:(half + 1) * 512]
                dve.tensor_tensor(dst, bank[use][:, :], dst, ALU.add).then_inc(h_ready, 1)
            dve_stats(dve, link, 2)
            dve.wait_ge(gain_in, 16)
            for t in range(NT):
                dve.scalar_tensor_tensor(h[:, t, :], h[:, t, :], stat_rs[:, t:t + 1], gain_row[:, :],
                                         ALU.mult, ALU.mult).then_inc(h_ready, 1)
            dve_stats(dve, link, 3)
            dve_xhat(dve)
            dve_nT_rest(dve, 2, "gain12", nT_hi)
            def halves(ap, half):
                return ap.rearrange("p (s e f) -> p s e f", s=2, e=2)[:, :, half, :]

            dve.wait_ge(h_ready, H_COUNT[3])
            for i, gain in enumerate(("qgain", "kgain")):
                for t in range(NT):
                    cs = c("cos")[:, t * DH:(t + 1) * DH]
                    sn = c("sin")[:, t * DH:(t + 1) * DH]
                    dve.tensor_tensor(cos_gain[:, i, t, :], cs, row(gain), ALU.mult)
                    for half in range(2):
                        last = dve.tensor_tensor(halves(sin_gain[:, i, t, :], half), halves(sn, half),
                                                 halves(row(gain), 1 - half), ALU.mult)
            link(last)
            dve.wait_ge(p2_act, 3)
            link(dve.tensor_reduce(qk_ss[:, :], qk_sq[:, :, :].rearrange("p t (a d) -> p (t a) d", d=DH), AX_X, ALU.add))
            dve.tensor_scalar(qk_ss[:, :], qk_ss[:, :], 1.0 / DH, EPS, ALU.mult, ALU.add).then_inc(qk_ms, 1)
            dve.wait_ge(qk_sd, 1)
            link(dve.reciprocal(qk_rs[:, :], qk_rs[:, :]))
            heads = qk[:, :, :].rearrange("p t (a d) -> p (t a) d", d=DH)
            link(dve.tensor_tensor(heads, heads, spread(qk_rs[:, :].unsqueeze(2), [P, NT * N_QK, DH]), ALU.mult))
            for t in range(NT):
                for i, (a, b) in enumerate(((0, GQA_HEADS), (GQA_HEADS, N_QK))):
                    src = qk[:, t, a * DH:b * DH].rearrange("p (a s e f) -> p (a s) e f", s=2, e=2, f=DH // 4)
                    dst = qk_rot[:, t, a * DH:b * DH].rearrange("p (a s e f) -> p (a s) e f", s=2, e=2, f=DH // 4)
                    for half in range(2):
                        table = spread(halves(sin_gain[:, i, t, :], half).unsqueeze(1), [P, b - a, 2, DH // 4])
                        last = dve.tensor_tensor(dst[:, :, half, :].rearrange("p (a s) f -> p a s f", s=2),
                                                 src[:, :, 1 - half, :].rearrange("p (a s) f -> p a s f", s=2), table, ALU.mult)
            link(last)
            for t in range(NT):
                for i, (a, b) in enumerate(((0, GQA_HEADS), (GQA_HEADS, N_QK))):
                    view = qk[:, t, a * DH:b * DH].rearrange("p (a d) -> p a d", d=DH)
                    last = dve.tensor_tensor(view, view, spread(cos_gain[:, i, t, :].unsqueeze(1), [P, b - a, DH]), ALU.mult)
            link(last)
            nq = GQA_HEADS * DH
            for copy in range(2):
                dve.tensor_tensor(kk[:, :, :, copy, :], qk[:, :, nq:].rearrange("p t (a d) -> p t a d", d=DH),
                                  qk_rot[:, :, nq:].rearrange("p t (a d) -> p t a d", d=DH), ALU.add)
            dve.tensor_tensor(qk[:, :, 0:nq], qk[:, :, 0:nq], qk_rot[:, :, 0:nq], ALU.add).then_inc(qk_roped, 1)
            dve.wait_ge(bias_in, 16 * KROWS)
            for t in range(NT):
                view = rel_bias[:, t, :, :].rearrange("p a (k c) -> p (a k) c", k=KROWS)
                last = dve.tensor_tensor(view, view, spread(c("window").unsqueeze(1), [P, NA_HEADS * KROWS, GRID_W]), ALU.add)
            link(last)
            for i, dst in enumerate((qaT[:, 0:2, :].rearrange("p a t -> p (a t)"),
                                     qaT[:, 2:4, :].rearrange("p a t -> p (a t)"), va[:, 0, :], va[:, 1, :])):
                dve.wait_ge(p2_done, (4, 5, 8, 9)[i])
                dve.tensor_copy(dst, bank[(7, 0, 3, 4)[i]][:, :]).then_inc(p2_dve, 1)
            dve.wait_ge(qk_turned, 3)
            dve.tensor_copy(kbT[:, :, :].rearrange("p a t -> p (a t)"), bank[7][:, :]).then_inc(kbT_ready, 1)
            sa = bank[0][:, :].rearrange("p (t k) -> p t k", t=NT)
            sb = bank[1][:, :].rearrange("p (t k) -> p t k", t=NT)
            for i in range(NA_HEADS):
                dve.wait_ge(sa_done, i + 1)
                if i:
                    dve.wait_ge(pa_turned, i)
                link(dve.scalar_tensor_tensor(prob_a[:, :, :], sa, SCALE, rel_bias[:, :, i, :], ALU.mult, ALU.add))
                link(dve.tensor_reduce(top_a[:, :], prob_a[:, :, :], AX_X, ALU.max))
                dve.tensor_scalar(top_a[:, :], top_a[:, :], -1.0, None, ALU.mult).then_inc(ta_ready, 1)
                dve.wait_ge(sb_done, i + 1)
                link(dve.tensor_reduce(top_b[:, :], sb, AX_X, ALU.max))
                dve.tensor_scalar(top_b[:, :], top_b[:, :], -SCALE, None, ALU.mult).then_inc(tb_ready, 1)
                dve.wait_ge(ea_ready, 2 * (i + 1))
                link(dve.reciprocal(sum_a[:, :], sum_a[:, :]))
                dve.tensor_tensor(prob_a[:, :, :], prob_a[:, :, :], spread(sum_a[:, :].unsqueeze(2), [P, NT, T]),
                                  ALU.mult).then_inc(pa_ready, 1)
                dve.wait_ge(eb_ready, 2 * (i + 1))
                link(dve.reciprocal(sum_b[:, :], sum_b[:, :]))
                dve.tensor_tensor(prob_b[:, :, :], prob_b[:, :, :], spread(sum_b[:, :].unsqueeze(2), [P, NT, T]),
                                  ALU.mult).then_inc(pb_ready, 1)
                dve.wait_ge(pb_turned, i + 1)
                if i:
                    dve.wait_ge(yb_done, i)
                dve.tensor_copy(prob_bT[:, :, :].rearrange("p k q -> p (k q)"), bank[3][:, :]).then_inc(pbT_ready, 1)
            dve.wait_ge(sg_ready, 2)
            for i in range(4):
                part = slice(2 * i, 2 * i + 2)
                for b, gate in enumerate((sga, sgb)):
                    dve.wait_ge(branch_done, 2 * i + b + 1)
                    view = gate[:, part, :].rearrange("p a t -> p (a t)")
                    last = dve.tensor_tensor(view, bank[BRANCH_BANK[b][i]][:, :], view, ALU.mult)
                link(last)
                dve.tensor_tensor(sga[:, part, :], sga[:, part, :], sgb[:, part, :], ALU.add).then_inc(merged_ready, 1)
            for half in range(2):
                for t in range(NT):
                    dve.wait_ge(out2_done, 2 * half + t + 1)
                    dst = h[:, t, half * 512:(half + 1) * 512]
                    dve.tensor_tensor(dst, bank[2 * half + t][:, :], dst, ALU.add).then_inc(h_ready, 1)
            dve_stats(dve, link, 4)
            dve_xhat(dve)
            dve_nT_rest(dve, 3, "gain22", nT_hi)
            for use in range(1, 8, 2):
                dve.wait_ge(query_done, use + 1)
                dve.tensor_copy(qT[:, 2 * use:2 * use + 2, :].rearrange("p a t -> p (a t)"),
                                bank[QUERY_BANK[use]][:, :]).then_inc(query_dve, 1)

            def best_of(views):
                for lo in (0, 8):
                    for score, value, _ in views:
                        last = dve.max(value[:, lo:lo + 8], score)
                    link(last)
                    for score, value, place in views:
                        last = dve.max_index(place[:, lo:lo + 8], value[:, lo:lo + 8], score)
                    link(last)
                    if lo == 0:
                        for score, value, _ in views:
                            last = dve.match_replace(score, value[:, 0:8], score, BIG)
                        link(last)

            for use in range(8):
                t, part = divmod(use, 4)
                dve.wait_ge(score_ready, use + 1)
                best_of([(sc[:, t, hp, :], ts[:, t, hp, :], ti[:, t, hp, :]) for hp in range(4 * part, 4 * part + 4)])
            link(dve.tensor_copy(tif[:, :, :, :], ti[:, :, :, :]))
            wide = [P, PEER_HEADS, TOPK, TOPK]

            def half_of(tile, t, half):
                return tile[:, t, :, :].rearrange("p (a e) k -> p a e k", e=2)[:, :, half, :]

            for t in range(NT):
                last = dve.tensor_tensor(cand[:, t, :, :, :], spread(half_of(ts, t, 0).unsqueeze(3), wide),
                                         spread(half_of(ts, t, 1).unsqueeze(2), wide), ALU.add)
            link(last)
            for t in range(NT):
                best_of([(cand[:, t, a, :, :].rearrange("p x y -> p (x y)"), best[:, t, a * TOPK:(a + 1) * TOPK],
                          bpos[:, t, a * TOPK:(a + 1) * TOPK]) for a in range(PEER_HEADS)])
            dve.tensor_scalar(bdig[:, 0, :, :], bpos[:, :, :], 4, None, ALU.logical_shift_right)
            link(dve.tensor_scalar(bdig[:, 1, :, :], bpos[:, :, :], TOPK - 1, None, ALU.bitwise_and))
            link(dve.tensor_copy(bdigf[:, :, :, :], bdig[:, :, :, :]))
            for half in range(2):
                for t in range(NT):
                    link(dve.tensor_tensor(match[:, :, :], spread(c("iota")[:, 0:TOPK].unsqueeze(1), [P, HK, TOPK]),
                                           spread(bdigf[:, half, t, :].unsqueeze(2), [P, HK, TOPK]), ALU.is_equal))
                    by_head = match[:, :, :].rearrange("p (a k) x -> p a k x", a=PEER_HEADS)
                    link(dve.tensor_tensor(by_head, by_head, spread(half_of(tif, t, half).unsqueeze(2), wide), ALU.mult))
                    link(dve.tensor_reduce(ij[:, half, t, :], match[:, :, :], AX_X, ALU.add))
            by_head = best[:, :, :].rearrange("p t (a k) -> p (t a) k", k=TOPK)
            flat = [P, NT * PEER_HEADS, TOPK]
            link(dve.tensor_copy(best_sum[:, :].unsqueeze(2), by_head[:, :, 0:1]))
            dve.tensor_tensor(by_head, by_head, spread(best_sum[:, :].unsqueeze(2), flat), ALU.subtract).then_inc(routed, 1)
            dve.wait_ge(best_exp, 1)
            link(dve.tensor_reduce(best_sum[:, :], by_head, AX_X, ALU.add))
            link(dve.reciprocal(best_sum[:, :], best_sum[:, :]))
            dve.tensor_tensor(by_head, by_head, spread(best_sum[:, :].unsqueeze(2), flat), ALU.mult).then_inc(gates_ready, 1)

            def lead_of(dst, src):
                return dve.tensor_copy(dst, src)

            def split_chunk(n, at_n, loaded):
                slot, b = at_n % RAW_SLOTS, at_n % 2
                dve.wait_ge(raw_full[slot], loaded)
                dve.wait_ge(chunk_used, n - 1)
                lead_of(lead[b][:, :], raw[slot][:, :]).then_inc(lead_ready, 1)
                dve.wait_ge(lead_ready, n + 1)
                dve.tensor_tensor(rest[slot][:, :], raw[slot][:, :], lead[b][:, :].bitcast(F32), ALU.subtract).then_inc(rest_ready, 1)

            dve.wait_ge(route_turned, 1)
            dve.tensor_copy(bestT[:, :], bank[6][:, 0:T])
            dve.tensor_copy(ijT[:, 0, :], bank[6][:, T:])
            dve.tensor_copy(ijT[:, 1, :], bank[7][:, 0:T]).then_inc(route_ready, 1)

            def one_hots(g, b):
                first = 0 if b < VECTOR_HOTS else 1
                whole = [P, 2 - first, GT, NKEYS]
                dve.tensor_tensor(hot[b][:, first:, :, :], spread(c("iota")[:, 0:NKEYS].unsqueeze(1).unsqueeze(1), whole),
                                  spread(ijT[:, first:, bass.ds(g * GT, GT)].unsqueeze(3), whole),
                                  ALU.is_equal).then_inc(hot_ready, 1)

            def gate_columns(g, b):
                dve.wait_ge(gates_done, g + 1)
                view = A[:, :, bass.ds(g * GT, GT)]
                dve.tensor_tensor(view, bank[4 + b][:, :].rearrange("p (t j) -> p j t", t=GT), view, ALU.mult).then_inc(gated, 1)

            dve.wait_ge(rest_ready, ROUTING)
            with dve.Fori(0, (PEER_CHUNKS - ROUTING) // UNROLL) as i:
                for s in range(UNROLL):
                    n = ROUTING + UNROLL * i + s
                    split_chunk(n, ROUTING + s, fill(i, ROUTING + s))
            dve.wait_ge(route_ready, 1)
            dve.wait_ge(chunk_used, PEER_CHUNKS)
            for b in range(HOTS):
                one_hots(b, b)
            dve.wait_ge(act_ready, PEER_CHUNKS)
            with dve.Fori(0, GROUPS // HOTS - 1) as turn:
                for b in range(HOTS):
                    gate_columns(HOTS * turn + b, b)
                    one_hots(HOTS * turn + b + HOTS, b)
            for b in range(HOTS):
                gate_columns(GROUPS - HOTS + b, b)
            def split_hidden(n, at_n):
                c, b = n - PEER_CHUNKS, at_n % 2
                src = A[:, bass.ds(c * CJ, CJ), :]
                lead_of(hid_hi[b][:, :, :], src).then_inc(hid_hi_ready, 1)
                dve.wait_ge(hid_hi_ready, c + 1)
                dve.tensor_tensor(hid_lo[b][:, :, :], src, hid_hi[b][:, :, :].bitcast(F32), ALU.subtract).then_inc(hid_lo_ready, 1)

            def split_both(n, at_n, loaded):
                split_chunk(n, at_n, loaded)
                split_hidden(n, at_n)

            dve.wait_ge(gated, GROUPS)
            dve.wait_ge(gates_done, GROUPS)
            dve.wait_ge(hot_j_ready, GROUPS)
            v_head = 2
            for n in range(PEER_CHUNKS, PEER_CHUNKS + v_head):
                split_both(n, n, fill(0, n))
            with dve.Fori(0, PEER_CHUNKS // UNROLL) as i:
                for s in range(UNROLL):
                    at_n = PEER_CHUNKS + v_head + s
                    n = at_n + UNROLL * i
                    split_both(n, at_n, fill(i, at_n))
            for n in range(2 * PEER_CHUNKS - 2, 2 * PEER_CHUNKS):
                split_both(n, n, fill(0, n))
            for use in range(4):
                half, t = divmod(use, NT)
                dve.wait_ge(chunk_used, 2 * PEER_CHUNKS)
                dst = h[:, t, half * 512:(half + 1) * 512]
                dve.tensor_tensor(dst, bank[2 * half + t][:, :], dst, ALU.add).then_inc(h_ready, 1)
            dve_stats(dve, link, 5)
            dve.wait_ge(gain_f_in, 16)
            for t in range(NT):
                dve.scalar_tensor_tensor(h[:, t, :], h[:, t, :], stat_rs[:, t:t + 1], gain_f[:, :],
                                         ALU.mult, ALU.mult).then_inc(out_ready, 1)

        return locals()


def layouts(inputs):
    g = {k: np.asarray(v) for k, v in inputs.items()}

    def across(a):
        return a.reshape(-1, P).T

    out = {
        "x": g["x"][0],
        "const": constants(),
        "param": np.concatenate([
            across(g["norm1_gain"][0]), across(g["gmlp_v_gain"][0]), across(g["hgrn_lower_bounds"][0]),
            across(g["hgrn_lower_bounds"][1]), across(g["hgrn_out_gain"][0]), across(g["norm2_gain"][0]),
            across(g["norm1_g_2"][0]), across(g["norm2_g_2"][0])], axis=1),
        "rows": np.concatenate([g["gqa_q_norm_g_2"][0], g["gqa_k_norm_g_2"][0], g["gmlp_b_s"][0].reshape(-1),
                                g["b_group_router"][0], g["b_expert_router"][0]])[None],
        "w_in": g["w_in"][0],
        "w_sT": g["gmlp_w_s"][0].transpose(2, 0, 1).reshape(P, HEADS * P),
        "w_out": g["w_out"][0],
        "w_group_router": g["w_group_router"][0],
        "w_expert_router": g["w_expert_router"][0],
        "w_gate": g["w_gate"][0],
        "w_up": g["w_up"][0],
        "w_down": g["w_down"][0],
        "final_gain": g["final_gain"][None],
        "w_in_2": g["w_in_2"][0],
        "rpb": g["na_rpb_2"][0].reshape(-1),
        "w_proj_a": g["w_proj_a_2"][0],
        "w_proj_b": g["w_proj_b_2"][0],
        "w_out_2": g["w_out_2"][0],
        "w_q": g["peer_w_q_2"][0],
        "keysT": g["peer_sub_keys_2"][0].transpose(3, 0, 1, 2).reshape(P, HP * NKEYS),
        "u": g["peer_u_2"][0].reshape(NKEYS, PEER_CHUNKS, CJ, KD, P).transpose(1, 4, 3, 2, 0).reshape(PEER_CHUNKS, P, -1),
        "v": g["peer_v_2"][0].reshape(NKEYS, PEER_CHUNKS, CJ * D).transpose(1, 0, 2),
        "norm_f_g": g["norm_f_g_2"][None],
    }
    return {k: np.ascontiguousarray(v) for k, v in out.items()}


def kernel(**inputs):
    import concourse.bacc as bacc
    from concourse.bass_utils import run_bass_kernel_spmd

    arrays = layouts(inputs)
    nc = bacc.Bacc("TRN2", target_bir_lowering=False, num_devices=1)
    dram = {k: nc.dram_tensor(f"in_{k}", v.shape, mybir.dt.from_np(v.dtype), kind="ExternalInput").ap()
            for k, v in arrays.items()}
    out = nc.dram_tensor("out", (T, D), F32, kind="ExternalOutput").ap()
    build(nc, dram, out)
    r = run_bass_kernel_spmd(nc, [{f"in_{k}": v for k, v in arrays.items()}], core_ids=[0])
    return r.results[0]["out"].reshape(1, T, D)
```
